# Optimizing a Trainium2 kernel written in Bass

```python
import math
import jax
import jax.numpy as jnp
from jax import lax
import numpy as np

D_MODEL = 1024
BATCH = 1
SEQ = 128
DEPTH = 2
DEC_BATCH = 1
DEC_SEQ = 512
PAST_LEN = 128

GRID_W = 64
HEAD_DIM = 64
N_BRANCH = 4
BRANCH_DIM = D_MODEL // N_BRANCH
NA_HEADS = BRANCH_DIM // HEAD_DIM
NA_WIN_H = 8
NA_WIN_W = 16
NA_QCOLS = 16
NA_KCOLS = 32
SWA_Q_HEADS = BRANCH_DIM // HEAD_DIM
SWA_KV_HEADS = 2
SWA_WINDOW = 128
SWA_BLOCK = 128
FNET_GROUPS = 4
FNET_GROUP_DIM = BRANCH_DIM // FNET_GROUPS
DIFF_HEADS = 4
DIFF_V_DIM = BRANCH_DIM // DIFF_HEADS
DIFF_QK_DIM = DIFF_V_DIM // 2
D_FF = ((-(-8 * D_MODEL // 3)) + 255) // 256 * 256
Q_BLOCK = 128
ROPE_BASE = 10000.0
NORM_EPS = 1e-6
NEG_INF = -1e30
NA_W = NA_HEADS * HEAD_DIM
SWA_QW = SWA_Q_HEADS * HEAD_DIM
SWA_KW = SWA_KV_HEADS * HEAD_DIM
FNET_W = FNET_GROUPS * FNET_GROUP_DIM
DIFF_QKW = DIFF_HEADS * 2 * DIFF_QK_DIM
DIFF_VW = DIFF_HEADS * DIFF_V_DIM
SPLIT_SIZES = (NA_W, NA_W, NA_W, SWA_QW, SWA_KW, SWA_KW, FNET_W, DIFF_QKW, DIFF_QKW, DIFF_VW)
D_IN = 3 * NA_W + SWA_QW + 2 * SWA_KW + FNET_W + 2 * DIFF_QKW + DIFF_VW

kernel_name = "hybrid_flow_prefix_step"

def rmsnorm(x, g):
    xf = x.astype(jnp.float32)
    y = xf * lax.rsqrt(jnp.mean(jnp.square(xf), axis=-1, keepdims=True) + NORM_EPS)
    return (y * g.astype(jnp.float32)).astype(x.dtype)

def rope_1d(x, pos):
    m = x.shape[-1]
    half = m // 2
    inv = ROPE_BASE ** (-jnp.arange(half, dtype=jnp.float32) * 2.0 / m)
    ang = pos.astype(jnp.float32)[:, None] * inv[None, :]
    cos = jnp.cos(ang)[:, None, :]
    sin = jnp.sin(ang)[:, None, :]
    xf = x.astype(jnp.float32)
    x1, x2 = xf[..., :half], xf[..., half:]
    return jnp.concatenate([x1 * cos - x2 * sin, x2 * cos + x1 * sin], axis=-1).astype(x.dtype)

def axial_rope(x, rows, cols):
    h = x.shape[-1] // 2
    return jnp.concatenate([rope_1d(x[..., :h], rows), rope_1d(x[..., h:], cols)], axis=-1)

def rope_diff(x, rows, cols):
    B, L, H, C, dq = x.shape
    return axial_rope(x.reshape(B, L, H * C, dq), rows, cols).reshape(x.shape)

def map_qblocks(fn, q):
    B, L = q.shape[:2]
    nb = L // Q_BLOCK
    qb = jnp.moveaxis(q.reshape((B, nb, Q_BLOCK) + q.shape[2:]), 1, 0)
    ob = lax.map(fn, qb)
    return jnp.moveaxis(ob, 0, 1).reshape((B, L) + ob.shape[3:])

def dense_attn(q, k, v, sink=None):
    B, L, Hq, d = q.shape
    Hkv = k.shape[2]
    G = Hq // Hkv
    scale = d ** -0.5

    def blk(qb):
        qg = qb.reshape(B, Q_BLOCK, Hkv, G, d)
        s = jnp.einsum('bqhgd,bkhd->bhgqk', qg, k).astype(jnp.float32) * scale
        if sink is not None:
            sk = jnp.broadcast_to(sink.astype(jnp.float32).reshape(1, Hkv, G, 1, 1), s.shape[:-1] + (1,))
            p = jax.nn.softmax(jnp.concatenate([sk, s], axis=-1), axis=-1)[..., 1:]
        else:
            p = jax.nn.softmax(s, axis=-1)
        o = jnp.einsum('bhgqk,bkhd->bqhgd', p.astype(v.dtype), v)
        return o.reshape(B, Q_BLOCK, Hq, d)

    return map_qblocks(blk, q)

def na_latent(q, k, v, ck, cv, rpb):
    B, L, H, d = q.shape
    R = L // GRID_W
    kh = min(NA_WIN_H, R)
    nb = GRID_W // NA_QCOLS
    kk = kh * NA_KCOLS
    scale = d ** -0.5
    r = np.arange(R)
    rs = np.clip(r - kh // 2, 0, R - kh)
    key_rows = rs[:, None] + np.arange(kh)
    kb = np.clip(np.arange(nb) * NA_QCOLS - NA_WIN_W // 2, 0, GRID_W - NA_KCOLS)
    key_cols = kb[:, None] + np.arange(NA_KCOLS)
    qcols = np.arange(GRID_W).reshape(nb, NA_QCOLS)
    cs = np.clip(qcols - NA_WIN_W // 2, 0, GRID_W - NA_WIN_W)
    idx = (key_rows[:, None, :, None] * GRID_W + key_cols[None, :, None, :]).reshape(R, nb, kk)
    kg = k[:, idx]
    vg = v[:, idx]
    qb = q.reshape(B, R, nb, NA_QCOLS, H, d)
    kc = key_cols[:, None, None, :]
    valid = (kc >= cs[:, :, None, None]) & (kc < cs[:, :, None, None] + NA_WIN_W)
    valid = np.broadcast_to(valid, (nb, NA_QCOLS, kh, NA_KCOLS)).reshape(nb, NA_QCOLS, kk)
    dr = key_rows - r[:, None] + NA_WIN_H - 1
    dc = np.clip(key_cols[:, None, :] - qcols[:, :, None] + NA_WIN_W - 1, 0, 2 * NA_WIN_W - 2)
    bias = rpb[:, dr[:, None, None, :, None], dc[None, :, :, None, :]]
    bias = jnp.transpose(bias, (1, 2, 0, 3, 4, 5)).reshape(R, nb, H, NA_QCOLS, kk).astype(jnp.float32)
    s_loc = jnp.einsum('brnqhd,brnkhd->brnhqk', qb, kg).astype(jnp.float32) * scale + bias
    s_loc = jnp.where(valid[None, None, :, None], s_loc, NEG_INF)
    s_ctx = jnp.einsum('brnqhd,bkhd->brnhqk', qb, ck).astype(jnp.float32) * scale
    p = jax.nn.softmax(jnp.concatenate([s_loc, s_ctx], axis=-1), axis=-1).astype(v.dtype)
    o = (jnp.einsum('brnhqk,brnkhd->brnqhd', p[..., :kk], vg)
         + jnp.einsum('brnhqk,bkhd->brnqhd', p[..., kk:], cv))
    return o.reshape(B, L, H, d)

def swa_latent(q, k, v, ck, cv, sink):
    B, L, Hq, d = q.shape
    Hkv = k.shape[2]
    G = Hq // Hkv
    nb = L // SWA_BLOCK
    kw = 3 * SWA_BLOCK
    scale = d ** -0.5
    pad = ((0, 0), (SWA_BLOCK, SWA_BLOCK), (0, 0), (0, 0))
    kp = jnp.pad(k, pad)
    vp = jnp.pad(v, pad)
    idx = (np.arange(nb) * SWA_BLOCK)[:, None] + np.arange(kw)
    kbl = kp[:, idx]
    vbl = vp[:, idx]
    kpos = idx - SWA_BLOCK
    qpos = (np.arange(nb) * SWA_BLOCK)[:, None] + np.arange(SWA_BLOCK)
    valid = ((np.abs(kpos[:, None, :] - qpos[:, :, None]) <= SWA_WINDOW)
             & (kpos >= 0)[:, None, :] & (kpos < L)[:, None, :])
    qb = q.reshape(B, nb, SWA_BLOCK, Hkv, G, d)
    s_loc = jnp.einsum('bnqhgd,bnkhd->bnhgqk', qb, kbl).astype(jnp.float32) * scale
    s_loc = jnp.where(valid[None, :, None, None], s_loc, NEG_INF)
    s_ctx = jnp.einsum('bnqhgd,bkhd->bnhgqk', qb, ck).astype(jnp.float32) * scale
    s_sink = jnp.broadcast_to(sink.astype(jnp.float32).reshape(1, 1, Hkv, G, 1, 1), s_loc.shape[:-1] + (1,))
    p = jax.nn.softmax(jnp.concatenate([s_sink, s_loc, s_ctx], axis=-1), axis=-1).astype(v.dtype)
    o = (jnp.einsum('bnhgqk,bnkhd->bnqhgd', p[..., 1:1 + kw], vbl)
         + jnp.einsum('bnhgqk,bkhd->bnqhgd', p[..., 1 + kw:], cv))
    return o.reshape(B, L, Hq, d)

def fourier_mix(u):
    y = jnp.fft.fft2(u.astype(jnp.float32), axes=(1, 3), norm='ortho').real
    return y.astype(u.dtype)

def lambda_value(lp, lam_init):
    lp = lp.astype(jnp.float32)
    return jnp.exp(jnp.sum(lp[0] * lp[1])) - jnp.exp(jnp.sum(lp[2] * lp[3])) + lam_init

def diff_attn(q, k, v, lam, lam_init, subln_g):
    scale = DIFF_QK_DIM ** -0.5

    def blk(qb):
        s = jnp.einsum('bqhcd,bkhcd->bhcqk', qb, k).astype(jnp.float32) * scale
        p = jax.nn.softmax(s, axis=-1)
        a = p[:, :, 0] - lam * p[:, :, 1]
        return jnp.einsum('bhqk,bkhd->bqhd', a.astype(v.dtype), v)

    o = map_qblocks(blk, q)
    return rmsnorm(o, subln_g) * (1.0 - lam_init)

def adaln(cond, ada_w, ada_b):
    m = jax.nn.silu(cond) @ ada_w + ada_b
    return tuple(t[:, None, :] for t in jnp.split(m, 6, axis=-1))

def project(h, w_in):
    B, L, _ = h.shape
    p = h @ w_in
    parts = []
    start = 0
    for w in SPLIT_SIZES:
        parts.append(p[..., start:start + w])
        start += w
    na_q, na_k, na_v = [t.reshape(B, L, NA_HEADS, HEAD_DIM) for t in parts[0:3]]
    swa_q = parts[3].reshape(B, L, SWA_Q_HEADS, HEAD_DIM)
    swa_k = parts[4].reshape(B, L, SWA_KV_HEADS, HEAD_DIM)
    swa_v = parts[5].reshape(B, L, SWA_KV_HEADS, HEAD_DIM)
    fu = parts[6].reshape(B, L, FNET_GROUPS, FNET_GROUP_DIM)
    dq = parts[7].reshape(B, L, DIFF_HEADS, 2, DIFF_QK_DIM)
    dk = parts[8].reshape(B, L, DIFF_HEADS, 2, DIFF_QK_DIM)
    dv = parts[9].reshape(B, L, DIFF_HEADS, DIFF_V_DIM)
    return na_q, na_k, na_v, swa_q, swa_k, swa_v, fu, dq, dk, dv

def finish_layer(x, h, branches, g1, sh2, sc2, g2, w_branch, w_gate, b_gate, w_o, norm2_g, w_ffn_in, w_ffn_out):
    B, L, _ = x.shape
    br = jnp.stack([b.reshape(B, L, BRANCH_DIM) for b in branches], axis=2)
    up = jnp.einsum('blkc,kcd->blkd', br, w_branch)
    gates = jax.nn.sigmoid(h @ w_gate + b_gate).reshape(B, L, N_BRANCH, D_MODEL)
    x = x + g1 * (jnp.sum(gates * up, axis=2) @ w_o)
    h2 = rmsnorm(x, norm2_g) * (1.0 + sc2) + sh2
    a, b = jnp.split(h2 @ w_ffn_in, 2, axis=-1)
    return x + g2 * ((jax.nn.silu(a) * b) @ w_ffn_out)

def setup_inputs(seed: int = 0) -> dict:
    key = jax.random.key(seed)
    ks = jax.random.split(key, 24)
    f32 = jnp.float32

    def nrm(k, shape, s):
        return jax.random.normal(k, shape, f32) * s

    return {
        "x_prompt": nrm(ks[0], (BATCH, SEQ, D_MODEL), 1.0),
        "x_sample": nrm(ks[1], (DEC_BATCH, DEC_SEQ, D_MODEL), 1.0),
        "cache_na_kv": nrm(ks[2], (DEC_BATCH, DEPTH, 2, PAST_LEN, NA_HEADS, HEAD_DIM), 1.0),
        "cache_swa_kv": nrm(ks[3], (DEC_BATCH, DEPTH, 2, PAST_LEN, SWA_KV_HEADS, HEAD_DIM), 1.0),
        "cache_diff_kv": nrm(ks[4], (DEC_BATCH, DEPTH, 2, PAST_LEN, DIFF_HEADS, DIFF_V_DIM), 1.0),
        "c": nrm(ks[5], (DEC_BATCH, D_MODEL), 1.0),
        "c_ctx": nrm(ks[6], (D_MODEL,), 1.0),
        "norm1_g": 1.0 + nrm(ks[7], (DEPTH, D_MODEL), 0.02),
        "norm2_g": 1.0 + nrm(ks[8], (DEPTH, D_MODEL), 0.02),
        "ada_w": nrm(ks[9], (DEPTH, D_MODEL, 6 * D_MODEL), 0.5 * D_MODEL ** -0.5),
        "ada_b": nrm(ks[10], (DEPTH, 6 * D_MODEL), 0.02),
        "w_in": nrm(ks[11], (DEPTH, D_MODEL, D_IN), D_MODEL ** -0.5),
        "na_rpb": nrm(ks[12], (DEPTH, NA_HEADS, 2 * NA_WIN_H - 1, 2 * NA_WIN_W - 1), 0.02),
        "swa_sink": nrm(ks[13], (DEPTH, SWA_Q_HEADS), 1.0),
        "diff_lambda": nrm(ks[14], (DEPTH, 4, DIFF_QK_DIM), 0.1),
        "diff_subln_g": 1.0 + nrm(ks[15], (DEPTH, DIFF_V_DIM), 0.02),
        "w_branch": nrm(ks[16], (DEPTH, N_BRANCH, BRANCH_DIM, D_MODEL), BRANCH_DIM ** -0.5),
        "w_gate": nrm(ks[17], (DEPTH, D_MODEL, N_BRANCH * D_MODEL), D_MODEL ** -0.5),
        "b_gate": nrm(ks[18], (DEPTH, N_BRANCH * D_MODEL), 0.02),
        "w_o": nrm(ks[19], (DEPTH, D_MODEL, D_MODEL), D_MODEL ** -0.5),
        "w_ffn_in": nrm(ks[20], (DEPTH, D_MODEL, 2 * D_FF), D_MODEL ** -0.5),
        "w_ffn_out": nrm(ks[21], (DEPTH, D_FF, D_MODEL), D_FF ** -0.5),
        "final_norm_g": 1.0 + nrm(ks[22], (D_MODEL,), 0.02),
    }

def reference(x_prompt, x_sample, cache_na_kv, cache_swa_kv, cache_diff_kv, c, c_ctx,
              norm1_g, norm2_g, ada_w, ada_b, w_in, na_rpb, swa_sink, diff_lambda, diff_subln_g,
              w_branch, w_gate, b_gate, w_o, w_ffn_in, w_ffn_out, final_norm_g):
    xp = x_prompt
    B, Lc, _ = xp.shape
    na_states, swa_states, diff_states = [], [], []
    for l in range(DEPTH):
        lam_init = 0.8 - 0.6 * math.exp(-0.3 * l)
        lam = lambda_value(diff_lambda[l], lam_init)
        sh1, sc1, g1, sh2, sc2, g2 = adaln(c_ctx[None, :], ada_w[l], ada_b[l])
        h = rmsnorm(xp, norm1_g[l]) * (1.0 + sc1) + sh1
        na_q, na_k, na_v, swa_q, swa_k, swa_v, fu, dq, dk, dv = project(h, w_in[l])
        o_na = dense_attn(na_q, na_k, na_v)
        o_swa = dense_attn(swa_q, swa_k, swa_v, swa_sink[l])
        o_f = fourier_mix(fu)
        o_d = diff_attn(dq, dk, dv, lam, lam_init, diff_subln_g[l])
        xp = finish_layer(xp, h, [o_na, o_swa, o_f, o_d], g1, sh2, sc2, g2, w_branch[l], w_gate[l],
                          b_gate[l], w_o[l], norm2_g[l], w_ffn_in[l], w_ffn_out[l])
        na_states.append(jnp.stack([na_k, na_v], axis=1))
        swa_states.append(jnp.stack([swa_k, swa_v], axis=1))
        diff_states.append(jnp.stack([dk.reshape(B, Lc, DIFF_HEADS, 2 * DIFF_QK_DIM), dv], axis=1))
    y_prompt = rmsnorm(xp, final_norm_g)
    new_na_kv = jnp.stack(na_states, axis=1)
    new_swa_kv = jnp.stack(swa_states, axis=1)
    new_diff_kv = jnp.stack(diff_states, axis=1)

    xs = x_sample
    Bd, L, _ = xs.shape
    Lp = cache_diff_kv.shape[3]
    pos = jnp.arange(L)
    rows = pos // GRID_W
    cols = pos % GRID_W
    for l in range(DEPTH):
        lam_init = 0.8 - 0.6 * math.exp(-0.3 * l)
        lam = lambda_value(diff_lambda[l], lam_init)
        sh1, sc1, g1, sh2, sc2, g2 = adaln(c, ada_w[l], ada_b[l])
        h = rmsnorm(xs, norm1_g[l]) * (1.0 + sc1) + sh1
        na_q, na_k, na_v, swa_q, swa_k, swa_v, fu, dq, dk, dv = project(h, w_in[l])
        o_na = na_latent(na_q, na_k, na_v, cache_na_kv[:, l, 0], cache_na_kv[:, l, 1], na_rpb[l])
        o_swa = swa_latent(axial_rope(swa_q, rows, cols), axial_rope(swa_k, rows, cols), swa_v,
                           cache_swa_kv[:, l, 0], cache_swa_kv[:, l, 1], swa_sink[l])
        o_f = fourier_mix(fu)
        ck = cache_diff_kv[:, l, 0].reshape(Bd, Lp, DIFF_HEADS, 2, DIFF_QK_DIM)
        k_all = jnp.concatenate([rope_diff(dk, rows, cols), ck], axis=1)
        v_all = jnp.concatenate([dv, cache_diff_kv[:, l, 1]], axis=1)
        o_d = diff_attn(rope_diff(dq, rows, cols), k_all, v_all, lam, lam_init, diff_subln_g[l])
        xs = finish_layer(xs, h, [o_na, o_swa, o_f, o_d], g1, sh2, sc2, g2, w_branch[l], w_gate[l],
                          b_gate[l], w_o[l], norm2_g[l], w_ffn_in[l], w_ffn_out[l])
    y_sample = rmsnorm(xs, final_norm_g)
    return (y_prompt, y_sample, new_na_kv, new_swa_kv, new_diff_kv)


_drawn_inputs = setup_inputs


def setup_inputs(seed=0):
    import zlib

    import numpy as np

    out = dict(_drawn_inputs(seed))
    spreads = {}
    factors = {'cache_na_kv': 2.948,
     'cache_swa_kv': 3.79,
     'norm1_g': 2.927,
     'norm2_g': 6.545,
     'na_rpb': 8.0,
     'swa_sink': 64.0,
     'diff_subln_g': 8.0,
     'b_gate': 8.0,
     'final_norm_g': 7.752,
     'cache_diff_kv': 8.0}
    for name, (base, spread) in spreads.items():
        noise = np.random.default_rng([zlib.crc32(name.encode()), seed]).standard_normal(out[name].shape)
        drawn = base * np.exp(spread * noise) if base else spread * noise
        out[name] = jnp.asarray(drawn.astype(out[name].dtype))
    for name, factor in factors.items():
        out[name] = (out[name] * factor).astype(out[name].dtype)
    return out
```

```python
from contextlib import ExitStack
import math

import numpy as np

import concourse.bass as bass
from concourse import mybir

F32 = mybir.dt.float32
F32R = mybir.dt.float32r
ALU = mybir.AluOpType
ACT = mybir.ActivationFunctionType
AX = mybir.AxisListType

P = 128
DM = 1024
KD = DM // P
NCTX, NLAT = 128, 512
T = NCTX + NLAT
TH = T // 2
TILES = T // P
L = 2
DFF = 2816
HD = 64
GRID_W = 64
PAST = 128
KEYS = NLAT + PAST
EPS = 1e-6
SC_HEAD = HD ** -0.5
SC_DIFF = 32 ** -0.5

NA_Q, SWA_Q, DIFF_Q, NA_K, DIFF_K, SWA_K = 0, 2, 4, 6, 8, 11
IN_A, IN_B = 10, 8
QK = IN_A + 2
V_NA, V_SWA, V_DIFF, FU = 0, 256, 384, 640
NBR = 4
FA, FB = 12, 10
N_GATE = KD * NBR
SLOTS = (IN_A + IN_B, N_GATE, KD, 2 * FA, KD, 2 * FB, KD)
SLOT0 = [sum(SLOTS[:i]) for i in range(8)]
CHUNKS = (IN_A + IN_B, 2 * N_GATE, KD, 2 * FA, KD, 2 * FB, KD)
D0 = [sum(CHUNKS[:i]) // 2 for i in range(8)]
UNITS = (KD, KD + 2, KD, KD, FA, KD, FB)
PER_SLOT = SLOT0[7] // 2
PER_DR = D0[7]
W_IN, GATE, W_O, FF_A, OUT_A, FF_B, OUT_B = range(7)
ADA_A, DFT, ADA_B = 16, 4, 32
PER_SM = (ADA_A + DFT + ADA_B) // 2
LOCAL = {"PER_V": 190, "PER_ATT": 64}
UNITS_T = [("na", h, 0) for h in range(4)] + [("swa", h, 0) for h in range(4)] + \
          [("df", h, c) for h in range(4) for c in range(2)]
NU, NF, NC = 16, 12, 4
WARM = {0: 7, 2: 3, 4: 4}
V_N1, V_N2, V_ADAB, V_BG, V_SINK, V_SUBG, V_LAM, V_LI, NV = 0, 8, 16, 64, 96, 100, 164, 292, 294
C_ID, C_ONE, C_RS, C_RD, C_CB, C_SB, C_C1, C_S1, NCC = [i * P for i in range(9)]


def build(nc, xT, ada, win, wgu, wo, wff, wfa, wfb, vec, cond, fgv, cst, rope, dft, bias, ckT, cvt,
          yT, okT, ovt):
    with ExitStack() as ctx:
        def sb(name, shape, dt=F32, stack=ctx):
            return stack.enter_context(nc.sbuf_tensor(name, shape, dt))

        def sem(name):
            return ctx.enter_context(nc.semaphore(name))

        x = sb("x", [P, KD, T])
        rstd = sb("rstd", [P, T])
        sqacc = sb("sqacc", [P, T])
        tmp = sb("tmp", [P, 4, T])
        wst = sb("wst", [P, 2, FA * P])
        wr = sb("wr", [P, 2, 2, FA * P], F32R)
        small = sb("small", [P, 2, KD * P])
        con = sb("con", [P, NCC])
        rp = sb("rp", [P, 4, NLAT])
        vc = sb("vc", [P, NV])
        cd = sb("cd", [P, KD, 2])
        fg = sb("fg", [P, KD])
        mod = sb("mod", [P, 48, 2])
        am = sb("am", [P, 2, KD, 2])
        st = sb("st", [P, 72])
        nm, rs, rv = st[:, 0:4], st[:, 4:8], st[:, 64:72]
        lam2, neglam, c1 = st[:, 12:14], st[:, 14:15], st[:, 16:18]
        epst = st[:, 18:19]
        ssq, srt = st[:, 20:40], st[:, 40:60]
        qs = sb("qs", [P, 2, 6, P])
        with ExitStack() as s1:
            H = sb("H", [P, 2, KD, T], F32R, s1)
        with ExitStack() as s1:
            prob = sb("prob", [P, 4, KEYS + 1], F32, s1)
            bt = sb("bt", [P, 3, KEYS], F32, s1)
            ck = sb("ck", [P, 5, PAST], F32, s1)
            cv = sb("cv", [P, 640], F32, s1)
            otm = sb("otm", [P, TILES, 768], F32, s1)
            yf = sb("yf", [P, 2, T], F32, s1)
        ft = prob[:, :, :].rearrange("p a b -> p (a b)")[:, 0:2048].rearrange("p (c s t) -> p c s t", c=2, s=2)
        ftp = prob[:, :, :].rearrange("p a b -> p (a b)")[:, 2048:2560].rearrange("p (c s t) -> p c s t", c=2, s=2)
        sb("region1", [P, 11008])
        with ExitStack() as s1:
            qk = sb("qk", [P, QK, T], F32, s1)
            sp = sb("sp", [P, 2, KEYS + 1], F32, s1)
            pts = sb("pts", [P, 2, KEYS], F32, s1)
            tm = sb("tm", [P, TILES, IN_B * P], F32, s1)
        with ExitStack() as s1:
            BR = sb("BR", [P, 2, KD, T], F32R, s1)
            sb("pad", [P, 16], F32, s1)
            mg = sb("mg", [P, KD, T], F32, s1)
        with ExitStack() as s1:
            G = sb("G", [P, 2, FA, T], F32R, s1)

        lp = [ctx.enter_context(nc.psum_tensor(f"lp{i}", [P, 2, 512], F32)) for i in range(2)]
        ss = [ctx.enter_context(nc.psum_tensor(f"ss{i}", [P, 2, 512], F32)) for i in range(2)]
        pt = lp[0][:, :, :].rearrange("p a b -> p (a b)")
        sflat = [t[:, :, :].rearrange("p a b -> p (a b)") for t in ss]

        def halves(ap):
            return ap.rearrange("p (h t) -> p h t", h=2)

        ld_x, ld_c, ld_v = sem("ld_x"), sem("ld_c"), sem("ld_v")
        ld_w = [sem(f"ld_w{i}") for i in range(2)]
        ld_s = [sem(f"ld_s{i}") for i in range(2)]
        ld_b = [sem(f"ld_b{i}") for i in range(3)]
        ld_k = sem("ld_k")
        st_k, st_y = sem("st_k"), sem("st_y")
        w_hi = [sem(f"w_hi{i}") for i in range(2)]
        w_lo = [sem(f"w_lo{i}") for i in range(2)]
        small_used = [sem(f"small_used{i}") for i in range(2)]
        lin = [sem(f"lin{i}") for i in range(2)]
        drained = [sem(f"drained{i}") for i in range(2)]
        split = sem("split")
        a_hi = sem("a_hi")
        a_f = sem("a_f")
        v_f = sem("v_f")
        a_own, v_own = sem("a_own"), sem("v_own")
        sq = sem("sq")
        sqs = sem("sqs")
        nsum, nrt, nrs = sem("nsum"), sem("nrt"), sem("nrs")
        cond_ready = sem("cond_ready")
        mods = sem("mods")
        turned, tmw = sem("turned"), sem("tmw")
        f1, f2, f3, f4 = sem("f1"), sem("f2"), sem("f3"), sem("f4")
        rot, roped = sem("rot"), sem("roped")
        staged = sem("staged")
        s_ready, s_pre, s_exp, s_comb = sem("s_ready"), sem("s_pre"), sem("s_exp"), sem("s_comb")
        t_done, pt_out, pv_done, o_out = sem("t_done"), sem("pt_out"), sem("pv_done"), sem("o_out")
        sub_a, sub_s, sub_d = sem("sub_a"), sem("sub_s"), sem("sub_d")
        bt_done = sem("bt_done")
        fin = sem("fin")

        SPLITS = (KD, KD, KD, KD, KD, FA, FB)
        SP0 = [sum(SPLITS[:i]) for i in range(8)]
        PER_SPL = SP0[7]
        PER_VF = 1 + 4 * KD
        S_H1, S_BR, S_H1B, S_MG, S_H2, S_GA, S_GB = range(7)

        ident, ones = con[:, C_ID:C_ID + P], con[:, C_ONE:C_ONE + P]

        class Own:

            def __init__(self, eng, s):
                self.eng, self.s, self.base, self.n, self.kept = eng, s, 0, 0, []

            def mark(self, ins):
                self.n += 1
                ins.then_inc(self.s, 1)

            def wait(self):
                self.eng.wait_ge(self.s, self.base + self.n)

            def step(self, ins):
                self.mark(ins)
                self.wait()

            def enter(self, i, per):
                self.kept.append((self.base, self.n))
                self.base, self.n = self.base + self.n + i * per, 0

            def leave(self, times, per):
                assert self.n == per, (self.n, per)
                self.base, n = self.kept.pop()
                self.n = n + times * per

        def plan(seq):
            turn, combs, f = {}, [], 0
            for u, (_, (kind, _, c)) in enumerate(seq):
                if kind != "df" or c == 1:
                    turn.setdefault(u + 3, []).append((u, f))
                    f += 1
                combs.append(sum(1 for _, (k, _, c2) in seq[:u + 1] if k == "df" and c2 == 1))
            return turn, combs

        block = ctx.enter_context(nc.Block())

        @block.sync
        def _(sy):
            for started in (*w_lo, *small_used, *lin, *drained, tmw, o_out, pt_out, turned, pv_done):
                sy.sem_inc(started, 1)
            sy.dma_start(cd[:], cond).then_inc(ld_c, 16)
            sy.dma_start(con[:], cst).then_inc(ld_c, 16)
            sy.dma_start(vc[:], vec[0]).then_inc(ld_v, 16)
            sy.dma_start(x[:], xT).then_inc(ld_x, 16)
            sy.dma_start(rp[:], rope).then_inc(ld_c, 16)
            sy.dma_start(fg[:], fgv).then_inc(ld_c, 16)

            def weight(l, stage, src, j, s, skip=0):
                n = l * PER_SLOT + SLOT0[stage] // 2 + j
                sy.wait_ge(w_lo[s], 1 + n)
                sy.dma_start(wst[:, s, 0:UNITS[stage] * P], src[l, 2 * j + s + skip]).then_inc(ld_w[s], 16)

            def little(l, first, src, j, s):
                sy.wait_ge(small_used[s], 1 + l * PER_SM + first // 2 + j)
                sy.dma_start(small[:, s, :], src).then_inc(ld_s[s], 16)

            with sy.Fori(0, L) as l:
                with sy.Fori(0, ADA_A // 2) as j:
                    for s in range(2):
                        little(l, 0, ada[l, 2 * j + s], j, s)
                with sy.Fori(0, (IN_A + IN_B) // 2) as j:
                    for s in range(2):
                        weight(l, W_IN, win, j, s)
                for j in range(2):
                    for s in range(2):
                        little(l, ADA_A, dft[2 * j + s], j, s)
                sy.wait_ge(lin[1], 1 + l * PER_DR + D0[GATE])
                sy.dma_start(ck[:], ckT[l]).then_inc(ld_k, 16)
                sy.dma_start(cv[:], cvt[l]).then_inc(ld_k, 16)
                for s in range(2):
                    weight(l, GATE, wgu, 0, s)
                sy.wait_ge(tmw, 1 + (l + 1) * IN_B)
                for n, c in enumerate((NA_K, NA_K + 1, DIFF_K, DIFF_K + 1, SWA_K)):
                    sy.dma_start(okT[l, :, n], qk[:, c, 0:NCTX]).then_inc(st_k, 16)
                sy.dma_start(ovt[l], tm[:, 0, 0:640]).then_inc(st_k, 16)
                with sy.Fori(0, 4) as i:
                    for h in range(4):
                        if h < 2:
                            sy.wait_ge(s_pre, l * 5 * NU + NU + i * NU - NU + h + 3)
                        else:
                            sy.wait_ge(s_pre, l * 5 * NU + NU + i * NU + h - 1)
                        sy.dma_start(bt[:, h % 2, :], bias[l, i, h]).then_inc(ld_b[h % 2], 16)
                    sy.dma_start(bt[:, 2, :], bias[l, i, 4]).then_inc(ld_b[2], 16)

                def smalls(j):
                    for s in range(2):
                        little(l, ADA_A + DFT, ada[l, 2 * j + s + ADA_A], j, s)

                smalls(0)
                with sy.Fori(1, N_GATE // 2) as j:
                    for s in range(2):
                        weight(l, GATE, wgu, j, s)
                    smalls(j)
                for stage, src in ((W_O, wo), (FF_A, wff), (OUT_A, wfa), (FF_B, wff), (OUT_B, wfb)):
                    with sy.Fori(0, SLOTS[stage] // 2) as j:
                        for s in range(2):
                            weight(l, stage, src, j, s, 2 * FA if stage == FF_B else 0)
                sy.wait_ge(drained[1], 1 + (l + 1) * PER_DR)
                sy.wait_ge(drained[0], 1 + (l + 1) * PER_DR)
                sy.dma_start(vc[:], vec[(l + 1) % L]).then_inc(ld_v, 16)
            for k in range(KD):
                sy.wait_ge(fin, k + 1)
                sy.dma_start(yT[:, k, :], x[:, k, :]).then_inc(st_y, 16)
            sy.wait_ge(st_y, 16 * KD)
            sy.wait_ge(st_k, 16 * 6 * L)
            sy.wait_ge(ld_v, 16 * (L + 1))

        @block.gpsimd
        def _(pool):
            pool.wait_ge(ld_c, 64)

            def split_weights(l, stage, j, s):
                n = l * PER_SLOT + SLOT0[stage] // 2 + j
                w = UNITS[stage] * P
                pool.wait_ge(ld_w[s], 16 * (n + 1))
                if stage == GATE and not isinstance(j, int):
                    pool.wait_ge(lin[1], 1 + l * PER_DR + D0[GATE] + 2 * j + s - 1)
                else:
                    pool.wait_ge(lin[s], 1 + l * PER_DR + D0[stage] + j)
                pool.tensor_tensor(wr[:, s, 0, 0:w], wst[:, s, 0:w], con[:, C_ONE:C_ONE + 1].to_broadcast([P, w]), ALU.mult).then_inc(w_hi[s], 1)
                pool.wait_ge(w_hi[s], n + 1)
                pool.tensor_tensor(wr[:, s, 1, 0:w], wst[:, s, 0:w], wr[:, s, 0, 0:w].bitcast(F32),
                                   ALU.subtract).then_inc(w_lo[s], 1)

            with pool.Fori(0, L) as l:
                with pool.Fori(0, SLOTS[W_IN] // 2) as j:
                    for s in range(2):
                        split_weights(l, W_IN, j, s)
                for s in range(2):
                    split_weights(l, GATE, 0, s)
                with pool.Fori(0, 2) as i:
                    pool.wait_ge(roped, (l + 1) * 7)
                    for s in range(2):
                        pool.wait_ge(s_ready, l * 5 * NU + (2 * i + s) * NU + (1 - s))
                        pool.tensor_copy(qs[:, s, :, :], qk[:, 0:6, bass.ds(NCTX + (2 * i + s) * P, P)])\
                            .then_inc(staged, 1)
                with pool.Fori(1, SLOTS[GATE] // 2) as j:
                    for s in range(2):
                        split_weights(l, GATE, j, s)
                for stage in (W_O, FF_A, OUT_A, FF_B, OUT_B):
                    with pool.Fori(0, SLOTS[stage] // 2) as j:
                        for s in range(2):
                            split_weights(l, stage, j, s)

        @block.tensor
        def _(pe):
            def product(out, w, act, k, first, last):
                for i, (wi, ai) in enumerate(((0, 0), (0, 1), (1, 0))):
                    for h in range(2):
                        mm = pe.matmul(out[:, h, 0:TH], w[wi], act[:, ai, k, h * TH:(h + 1) * TH],
                                       start=first and i == 0, stop=last and i == 2)
                return mm

            def chunk(l, stage, j, s, act, kk, unit0=0, c=None, pair=None):
                pair = s if pair is None else pair
                pe.wait_ge(drained[pair], 1 + l * PER_DR + D0[stage] + (j if c is None else c))
                for n, k in enumerate(kk):
                    w = [wr[:, s, i, (unit0 + n) * P:(unit0 + n + 1) * P] for i in range(2)]
                    mm = product(lp[pair], w, act, k, n == 0, n == len(kk) - 1)
                mm.then_inc(lin[pair], 1)

            def weights(l, stage, j, s):
                pe.wait_ge(w_lo[s], 1 + l * PER_SLOT + SLOT0[stage] // 2 + j + 1)

            def ada_chunk(l, first, j, s, col):
                pe.wait_ge(ld_s[s], 16 * (l * PER_SM + first // 2 + j + 1))
                for k in range(KD):
                    mm = pe.matmul(ss[1][:, 0, col], small[:, s, k * P:(k + 1) * P], cd[:, k, :],
                                   start=(k == 0), stop=(k == KD - 1))
                mm.then_inc(small_used[s], 1)

            def norm_sum(n):
                pe.wait_ge(sqs, n)
                for h in range(2):
                    mm = pe.matmul(ss[0][:, h, 0:TH], ones, sqacc[:, h * TH:(h + 1) * TH], start=True, stop=True)
                mm.then_inc(nsum, 1)

            def warm(times):
                for _ in range(times):
                    pe.matmul(lp[1][:, 0, HD:512], ident, con[:, 0:512 - HD], start=True, stop=True)

            def attend(seq, u0, f0, comb0):
                turn, combs = plan(seq)
                if seq[0][0] is not None:
                    pe.wait_ge(o_out, 1 + f0)
                    warm(WARM[0])
                for u in range(len(seq) + 5):
                    if u < len(seq):
                        t, (kind, h, c) = seq[u]
                        if u >= 2:
                            pt_, (k_, _, _) = seq[u - 2]
                            if (k_ == "na" and pt_ is not None) or k_ == "swa":
                                pe.wait_ge(s_pre, u0 + u - 1)
                            else:
                                pe.wait_ge(s_exp, u0 + u - 1)
                        if kind == "na":
                            qc, kc, p0, n = NA_Q + h // 2, NA_K + h // 2, (h % 2) * 64, 64
                            cc = h // 2
                        elif kind == "swa":
                            qc, kc, p0, n = SWA_Q + h % 2, SWA_K, (h // 2) * 64, 64
                            cc = 2
                        else:
                            qc, kc, p0, n = DIFF_Q + h // 2, DIFF_K + h // 2, (h % 2) * 64 + c * 32, 32
                            cc = 3 + h // 2
                        out = sflat[u % 2]
                        if t is None:
                            mm = pe.matmul(out[:, NLAT:KEYS], qk[p0:p0 + n, qc, 0:NCTX], qk[p0:p0 + n, kc, 0:NCTX],
                                           start=True, stop=True)
                        else:
                            q = qs[p0:p0 + n, t, qc, :]
                            pe.matmul(out[:, 0:NLAT], q, qk[p0:p0 + n, kc, NCTX:T], start=True, stop=True)
                            mm = pe.matmul(out[:, NLAT:KEYS], q, ck[p0:p0 + n, cc, :], start=True, stop=True)
                        mm.then_inc(s_ready, 1)
                        if t is not None:
                            warm(WARM.get(u + 1, 0))
                    for v, f in turn.get(u - 1, ()):
                        t, (kind, h, c) = seq[v]
                        pe.wait_ge(pt_out, 1 + f0 + f + 1)
                        pe.wait_ge(o_out, 1 + f0 + f - 1) if f >= 2 else pe.wait_ge(o_out, 1 + f0)
                        v0 = {"na": V_NA + h * 64, "swa": V_SWA + (h // 2) * 64, "df": V_DIFF + h * 64}[kind]
                        js = (4,) if t is None else range(5)
                        for j in js:
                            val = tm[:, 0, v0:v0 + 64] if t is None else \
                                cv[:, v0:v0 + 64] if j == 4 else tm[:, 1 + j, v0:v0 + 64]
                            mm = pe.matmul(lp[1][:, f % 2, 0:64], pts[:, f % 2, j * P:(j + 1) * P], val,
                                           start=(j == js[0]), stop=(j == 4))
                        mm.then_inc(pv_done, 1)
                    for v, f in turn.get(u, ()):
                        t, (kind, h, c) = seq[v]
                        if kind == "df":
                            pe.wait_ge(s_comb, comb0 + combs[v])
                        else:
                            pe.wait_ge(s_exp, u0 + v + 1)
                        pe.wait_ge(pt_out, 1 + f0 + f)
                        src = prob[:, v % 4, :]
                        for j in (4,) if t is None else range(5):
                            mm = pe.transpose(pt[:, j * P:(j + 1) * P], src[:, j * P:(j + 1) * P], ident)
                        mm.then_inc(t_done, 1)

            pe.wait_ge(ld_c, 64)
            pe.wait_ge(cond_ready, 1)
            with pe.Fori(0, L) as l:
                with pe.Fori(0, ADA_A // 2) as j:
                    for s in range(2):
                        ada_chunk(l, 0, j, s, bass.ds(2 * (2 * j + s), 2))
                norm_sum(l * 2 * KD + KD)
                with pe.Fori(0, IN_A // 2) as j:
                    pe.wait_ge(split, l * PER_SPL + KD)
                    for s in range(2):
                        weights(l, W_IN, j, s)
                        chunk(l, W_IN, j, s, H, range(KD))

                with pe.Fori(0, IN_B // 2) as j:
                    for s in range(2):
                        weights(l, W_IN, j + IN_A // 2, s)
                        chunk(l, W_IN, j + IN_A // 2, s, H, range(KD))
                    for s in range(2):
                        pe.wait_ge(drained[s], 1 + l * PER_DR + IN_A // 2 + j + 1)
                        pe.wait_ge(tmw, 1 + l * IN_B + 2 * j)
                        for t in range(TILES):
                            mm = pe.transpose(sflat[s][:, t * P:(t + 1) * P], qk[:, IN_A + s, t * P:(t + 1) * P], ident)
                        mm.then_inc(turned, 1)
                pe.wait_ge(tmw, 1 + (l + 1) * IN_B)
                for kc in range(4):
                    s = kc % 2
                    pe.wait_ge(ld_s[s], 16 * (l * PER_SM + ADA_A // 2 + kc // 2 + 1))
                    for c in range(2):
                        for i in range(2):
                            mm = pe.matmul(lp[c][:, i, :], tm[:, 1 + kc, FU + c * P:FU + (c + 1) * P],
                                           small[:, s, i * NLAT:(i + 1) * NLAT], start=(kc == 0), stop=(kc == 3))
                    mm.then_inc(small_used[s], 1)
                for c in range(2):
                    for i in range(2):
                        mm = pe.matmul(ss[1][:, 0, (2 * c + i) * P:(2 * c + i + 1) * P], tm[:, 0, FU + c * P:FU + (c + 1) * P],
                                       con[:, C_C1 + i * P:C_C1 + (i + 1) * P], start=True, stop=True)
                mm.then_inc(f1, 1)
                for n, c in enumerate((SWA_Q, SWA_Q + 1, SWA_K, DIFF_Q, DIFF_Q + 1, DIFF_K, DIFF_K + 1)):
                    r = C_RS if n < 3 else C_RD
                    if n >= 2:
                        pe.wait_ge(roped, l * 7 + n - 1)
                    pe.matmul(ss[n % 2][:, 1 if n % 2 else 0, :], con[:, r:r + P], qk[:, c, NCTX:T], start=True, stop=True)\
                        .then_inc(rot, 1)
                pe.wait_ge(f2, l * 3 + 3)
                for c in range(2):
                    for i in range(2):
                        mm = pe.matmul(lp[0][:, c, :], con[:, C_CB + i * P:C_CB + (i + 1) * P], ft[:, c, i, :],
                                       start=(i == 0), stop=(i == 1))
                for c in range(2):
                    for i in range(2):
                        mm = pe.matmul(lp[1][:, 0, c * P:(c + 1) * P], con[:, C_CB + i * P:C_CB + (i + 1) * P], ftp[:, c, i, :],
                                       start=(i == 0), stop=(i == 1))
                mm.then_inc(f3, 1)
                pe.wait_ge(f4, l + 1)
                pe.wait_ge(roped, (l + 1) * 7)
                attend([(None, u) for u in UNITS_T], l * 5 * NU, l * 5 * NF, l * 5 * NC)
                with pe.Fori(0, 2) as i:
                    pe.wait_ge(ld_k, 32 * (l + 1))
                    pe.wait_ge(staged, l * 4 + 2 * i + 2)
                    attend([(s, u) for s in range(2) for u in UNITS_T], l * 5 * NU + NU + i * 2 * NU,
                           l * 5 * NF + NF + i * 2 * NF, l * 5 * NC + NC + i * 2 * NC)
                for n in range(6):
                    if n == 0:
                        pe.wait_ge(o_out, 1 + (l + 1) * 5 * NF)
                    if n == 4:
                        pe.wait_ge(sub_d, l + 1)
                    if n >= 2:
                        pe.wait_ge(split, l * PER_SPL + SP0[S_BR] + n - 1)
                    for t in range(TILES):
                        mm = pe.transpose(sflat[n % 2][:, t * P:(t + 1) * P], otm[:, t, n * P:(n + 1) * P], ident)
                    mm.then_inc(bt_done, 1)
                def gate_pair(m, b, j, s):
                    weights(l, GATE, j, s)
                    chunk(l, GATE, j, s, H, range(KD), c=2 * j + s, pair=0)
                    chunk(l, GATE, j, s, BR, (2 * b, 2 * b + 1), unit0=KD, c=2 * j + s, pair=1)
                    ada_chunk(l, ADA_A + DFT, j, s, bass.ds(2 * (2 * j + s), 2))

                with pe.Fori(0, KD) as m:
                    pe.wait_ge(split, l * PER_SPL + SP0[S_MG])
                    for b in range(NBR):
                        gate_pair(m, b, 2 * m + b // 2, b % 2)
                with pe.Fori(0, KD // 2) as j:
                    pe.wait_ge(split, l * PER_SPL + SP0[S_H2])
                    for s in range(2):
                        weights(l, W_O, j, s)
                        chunk(l, W_O, j, s, H, range(KD))
                norm_sum(l * 2 * KD + 2 * KD)
                for ff, out, sp_end in ((FF_A, OUT_A, S_GB), (FF_B, OUT_B, 7)):
                    with pe.Fori(0, SLOTS[ff] // 2) as j:
                        pe.wait_ge(split, l * PER_SPL + SP0[S_GA])
                        for s in range(2):
                            weights(l, ff, j, s)
                            chunk(l, ff, j, s, H, range(KD))
                    with pe.Fori(0, KD // 2) as j:
                        pe.wait_ge(split, l * PER_SPL + SP0[sp_end])
                        for s in range(2):
                            weights(l, out, j, s)
                            chunk(l, out, j, s, G, range(UNITS[out]))
            norm_sum(L * 2 * KD + KD)

        @block.scalar
        def _(act):
            own = Own(act, a_own)

            def root(l, n, base):
                act.wait_ge(nsum, base)
                act.activation(halves(tmp[:, 2, :]), ss[0][:, :, 0:TH], ACT.Sqrt, bias=epst, scale=1.0 / DM)\
                    .then_inc(nrt, 1)

            def make_h(l, which, a_base, v_base, af_base, shift):
                for k in range(KD):
                    act.wait_ge(v_f, v_base + k + 1)
                    if k >= 2:
                        act.wait_ge(split, a_base + k - 1)
                    h = tmp[:, 2 + k % 2, :]
                    src = tmp[:, k % 2, :]
                    act.activation(h[:, 0:NCTX], src[:, 0:NCTX], ACT.Identity, bias=mod[:, shift + k, 0:1],
                                   scale=am[:, which, k, 0:1])
                    own.step(act.activation(h[:, NCTX:T], src[:, NCTX:T], ACT.Identity, bias=mod[:, shift + k, 1:2],
                                            scale=am[:, which, k, 1:2]))
                    act.activation(H[:, 0, k, :], h, ACT.Copy).then_inc(a_hi, 1)

            def exps(l, seq, u0, f0, comb0):
                turn, combs = plan(seq)
                done = {v: f for vf in turn.values() for v, f in vf}
                for u in range(len(seq) + 5):
                    for v, f in turn.get(u, ()):
                        lo = NLAT if seq[v][0] is None else 0
                        act.wait_ge(t_done, f0 + f + 1)
                        act.wait_ge(pv_done, 1 + f0 + max(f - 1, 0))
                        act.activation(pts[:, f % 2, lo:KEYS], pt[:, lo:KEYS], ACT.Copy).then_inc(pt_out, 1)
                    if u < len(seq):
                        t, (kind, h, c) = seq[u]
                        lo = NLAT if t is None else 0
                        act.wait_ge(s_pre, u0 + u + 1)
                        if u >= 4:
                            if u - 4 in done:
                                act.wait_ge(t_done, f0 + done[u - 4] + 1)
                            else:
                                act.wait_ge(s_comb, comb0 + combs[u - 3])
                        if kind == "swa":
                            act.activation(prob[:, u % 4, lo:KEYS + 1], sp[:, u % 2, lo:KEYS + 1], ACT.Exp,
                                           bias=nm[:, u % 4:u % 4 + 1], accum_out=rs[:, u % 4:u % 4 + 1]).then_inc(s_exp, 1)
                        elif kind == "na" and t is not None:
                            act.activation(prob[:, u % 4, 0:KEYS], sp[:, u % 2, 0:KEYS], ACT.Exp,
                                           bias=nm[:, u % 4:u % 4 + 1], accum_out=rs[:, u % 4:u % 4 + 1]).then_inc(s_exp, 1)
                        else:
                            act.activation(prob[:, u % 4, lo:KEYS], sflat[u % 2][:, lo:KEYS], ACT.Exp,
                                           bias=nm[:, u % 4:u % 4 + 1], scale=SC_HEAD if kind == "na" else SC_DIFF,
                                           accum_out=rs[:, u % 4:u % 4 + 1]).then_inc(s_exp, 1)

            act.wait_ge(ld_c, 64)
            act.activation(tmp[:, 2, 0:2 * KD], cd[:, :, :].rearrange("p k c -> p (k c)"), ACT.Silu).then_inc(a_own, 1)
            own.n += 1
            own.wait()
            act.activation(cd[:, :, :].rearrange("p k c -> p (k c)"), tmp[:, 2, 0:2 * KD], ACT.Copy).then_inc(cond_ready, 1)
            act.wait_ge(cond_ready, 1)
            act.wait_ge(ld_x, 16)
            for k in range(KD):
                if k >= 2:
                    act.wait_ge(sqs, k - 1)
                act.activation(tmp[:, 2 + k % 2, :], x[:, k, :], ACT.Square).then_inc(sq, 1)
            PER_A = 3 * KD
            with act.Fori(0, L) as l:
                own.enter(l, PER_A)
                act.wait_ge(ld_v, 16 * (l + 1))
                act.wait_ge(v_f, l * PER_VF + 1)
                act.activation(lam2, lam2, ACT.Exp).then_inc(a_f, 1)
                act.wait_ge(sqs, l * 2 * KD + KD)
                root(l, 0, l * 2 + 1)
                act.wait_ge(nrs, l * 2 + 1)
                act.wait_ge(mods, l * 2 + 1)
                vf = l * PER_VF + 1
                make_h(l, 0, l * PER_SPL, vf, None, 0)
                with act.Fori(0, IN_A // 2) as j:
                    for s in range(2):
                        act.wait_ge(lin[s], 1 + l * PER_DR + j + 1)
                        act.activation(halves(qk[:, 2 * j + s, :]), lp[s][:, :, 0:TH], ACT.Copy).then_inc(drained[s], 1)
                with act.Fori(0, IN_B // 2) as j:
                    for s in range(2):
                        act.wait_ge(lin[s], 1 + l * PER_DR + IN_A // 2 + j + 1)
                        act.wait_ge(turned, 1 + l * IN_B + 2 * j)
                        act.activation(halves(qk[:, IN_A + s, :]), lp[s][:, :, 0:TH], ACT.Copy).then_inc(drained[s], 1)
                act.wait_ge(f1, l + 1)
                for c in range(2):
                    act.activation(ft[:, c, :, :], lp[c][:, :, :], ACT.Copy).then_inc(f2, 1)
                act.activation(ftp.rearrange("p c s t -> p (c s t)"), ss[1][:, 0, :], ACT.Copy).then_inc(f2, 1)
                act.wait_ge(f3, l + 1)
                act.activation(yf[:, :, NCTX:T], lp[0][:, :, :], ACT.Copy, scale=(NLAT * HD) ** -0.5)
                act.activation(yf[:, :, 0:NCTX], lp[1][:, 0, 0:2 * P].rearrange("p (c t) -> p c t", c=2), ACT.Copy,
                               scale=(NCTX * HD) ** -0.5).then_inc(f4, 1)
                act.wait_ge(f4, l + 1)
                exps(l, [(None, u) for u in UNITS_T], l * 5 * NU, l * 5 * NF, l * 5 * NC)
                with act.Fori(0, 2) as i:
                    exps(l, [(s, u) for s in range(2) for u in UNITS_T], l * 5 * NU + NU + i * 2 * NU,
                         l * 5 * NF + NF + i * 2 * NF, l * 5 * NC + NC + i * 2 * NC)
                act.wait_ge(sub_a, l + 1)
                act.activation(srt, ssq, ACT.Sqrt, bias=epst, scale=1.0 / HD).then_inc(sub_s, 1)
                act.wait_ge(st_k, 16 * 6 * (l + 1))
                for n in range(6):
                    act.wait_ge(bt_done, l * 6 + n + 1)
                    c = n if n < 4 else n + 2
                    if n == 0:
                        act.wait_ge(pv_done, 1 + (l + 1) * 5 * NF)
                    act.activation(BR[:, 0, c, :], sflat[n % 2][:, 0:T], ACT.Copy).then_inc(a_hi, 1)
                for c in range(2):
                    act.activation(BR[:, 0, 4 + c, :], yf[:, c, :], ACT.Copy).then_inc(a_hi, 1)
                act.wait_ge(split, l * PER_SPL + SP0[S_H1B])
                make_h(l, 0, l * PER_SPL + SP0[S_H1B], vf + KD, None, 0)
                with act.Fori(0, KD) as m:
                    for b in range(NBR):
                        act.wait_ge(lin[0], 1 + l * PER_DR + D0[GATE] + 4 * m + b + 1)
                        act.wait_ge(drained[1], 1 + l * PER_DR + D0[GATE] + 4 * m + b - 1)
                        act.activation(halves(tmp[:, 2 + b % 2, :]), lp[0][:, :, 0:TH], ACT.Sigmoid,
                                       bias=vc[:, bass.ds(V_BG + 4 * m + b, 1)]).then_inc(drained[0], 1)
                act.wait_ge(lin[1], 1 + l * PER_DR + D0[W_O])
                for k in range(KD):
                    if k == 0:
                        act.wait_ge(v_f, vf + 2 * KD + KD)
                    act.activation(H[:, 0, k, :], mg[:, k, :], ACT.Copy).then_inc(a_hi, 1)
                with act.Fori(0, KD // 2) as j:
                    for s in range(2):
                        act.wait_ge(drained[s], 1 + l * PER_DR + D0[W_O] + j + 1)
                        act.wait_ge(sqs, l * 2 * KD + KD + 2 * j + s - 1)
                        act.activation(tmp[:, 2 + s, :], x[:, 2 * j + s, :], ACT.Square).then_inc(sq, 1)
                act.wait_ge(sqs, l * 2 * KD + 2 * KD)
                root(l, 1, l * 2 + 2)
                act.wait_ge(nrs, l * 2 + 2)
                act.wait_ge(mods, l * 2 + 2)
                make_h(l, 1, l * PER_SPL + SP0[S_H2], vf + 3 * KD, None, 24)
                for ff, out, n, f0, sg in ((FF_A, OUT_A, FA, 0, S_GA), (FF_B, OUT_B, FB, FA, S_GB)):
                    with act.Fori(0, n // 2) as j:
                        for s in range(2):
                            act.wait_ge(lin[0], 1 + l * PER_DR + D0[ff] + 2 * j + s + 1)
                            act.activation(halves(tmp[:, 2 + s, :]), lp[0][:, :, 0:TH], ACT.Silu).then_inc(drained[0], 1)
                            act.wait_ge(drained[1], 1 + l * PER_DR + D0[ff] + 2 * j + s + 1)
                            act.activation(G[:, 0, 2 * j + s, :], tmp[:, s, :], ACT.Copy).then_inc(a_hi, 1)
                    if out == OUT_B:
                        with act.Fori(0, KD // 2) as j:
                            for s in range(2):
                                act.wait_ge(drained[s], 1 + l * PER_DR + D0[OUT_B] + j + 1)
                                act.wait_ge(sqs, l * 2 * KD + 2 * KD + 2 * j + s - 1)
                                act.activation(tmp[:, 2 + s, :], x[:, 2 * j + s, :], ACT.Square).then_inc(sq, 1)
                own.leave(L, PER_A)
            root(L, 0, 2 * L + 1)

        @block.vector
        def _(ve):
            own = Own(ve, v_own)

            def rstd_of(n):
                ve.wait_ge(nrt, n)
                ve.reciprocal(rstd[:], tmp[:, 2, :])
                ve.memset(sqacc[:], 0.0).then_inc(nrs, 1)
                ve.wait_ge(nrs, n)

            def sum_square(n, k2):
                ve.wait_ge(sq, n)
                ve.tensor_tensor(sqacc[:], sqacc[:], tmp[:, 2 + k2, :], ALU.add).then_inc(sqs, 1)
                ve.wait_ge(sqs, n)

            def make_h(ah, vf, sp_):
                for k in range(KD + 1):
                    if k < KD:
                        if k >= 2:
                            ve.wait_ge(a_hi, ah + k - 1)
                        ve.tensor_tensor(tmp[:, k % 2, :], x[:, k, :], rstd[:], ALU.mult).then_inc(v_f, 1)
                    if k >= 1:
                        ve.wait_ge(a_hi, ah + k)
                        ve.tensor_tensor(H[:, 1, k - 1, :], tmp[:, 2 + (k - 1) % 2, :], H[:, 0, k - 1, :].bitcast(F32),
                                         ALU.subtract).then_inc(split, 1)

            def gains(which, scale, gain, n):
                for c in range(2):
                    m = ve.scalar_tensor_tensor(out=am[:, which, :, c], in0=mod[:, scale:scale + KD, c], scalar=1.0,
                                                in1=vc[:, gain:gain + KD], op0=ALU.add, op1=ALU.mult)
                m.then_inc(mods, 1)
                ve.wait_ge(mods, n)

            def residual(l, stage, j, s, gate):
                ve.wait_ge(lin[s], 1 + l * PER_DR + D0[stage] + j + 1)
                k = 2 * j + s
                for a, b, c in ((0, NCTX, 0), (NCTX, TH, 1), (TH, T, 1)):
                    h = a // TH
                    m = ve.scalar_tensor_tensor(out=x[:, k, a:b], in0=lp[s][:, h, a - h * TH:b - h * TH],
                                                scalar=mod[:, gate + 2 * j + s, c:c + 1], in1=x[:, k, a:b],
                                                op0=ALU.mult, op1=ALU.add)
                m.then_inc(drained[s], 1)

            def soft(l, seq, u0, f0, tile, comb0, i):
                turn, combs = plan(seq)
                for u in range(len(seq) + 5):
                    if u < len(seq):
                        t, (kind, h, c) = seq[u]
                        lo = NLAT if t is None else 0
                        ve.wait_ge(s_ready, u0 + u + 1)
                        mx = nm[:, u % 4:u % 4 + 1]
                        S = sflat[u % 2]
                        if kind == "swa" or (kind == "na" and t is not None):
                            if u >= 2:
                                ve.wait_ge(s_exp, u0 + u - 1)
                            hi = KEYS + (kind == "swa")
                            if kind == "swa":
                                ve.tensor_copy(sp[:, u % 2, KEYS:KEYS + 1], vc[:, V_SINK + h:V_SINK + h + 1])
                            if t is None:
                                own.step(ve.tensor_scalar(sp[:, u % 2, lo:KEYS], S[:, lo:KEYS], SC_HEAD, None, ALU.mult))
                            else:
                                if kind == "na":
                                    ve.wait_ge(ld_b[h % 2], 16 * (l * 8 + 4 * i + 2 * t + h // 2 + 1))
                                elif h == 0:
                                    ve.wait_ge(ld_b[2], 16 * (l * 4 + 2 * i + t + 1))
                                b = bt[:, h % 2 if kind == "na" else 2, :]
                                own.step(ve.scalar_tensor_tensor(out=sp[:, u % 2, 0:KEYS], in0=S[:, 0:KEYS], scalar=SC_HEAD,
                                                                 in1=b, op0=ALU.mult, op1=ALU.add))
                            ve.tensor_reduce(mx, sp[:, u % 2, lo:hi], AX.X, ALU.max, negate=True).then_inc(s_pre, 1)
                        else:
                            own.step(ve.tensor_reduce(mx, S[:, lo:KEYS], AX.X, ALU.max))
                            ve.tensor_scalar(mx, mx, -(SC_HEAD if kind == "na" else SC_DIFF), None, ALU.mult)\
                                .then_inc(s_pre, 1)
                    if 0 <= u - 1 < len(seq):
                        t, (kind, h, c) = seq[u - 1]
                        q, q8 = (u - 1) % 4, (u - 1) % 8
                        lo = NLAT if t is None else 0
                        if kind != "df":
                            ve.wait_ge(s_exp, u0 + u)
                            own.mark(ve.reciprocal(rv[:, q8:q8 + 1], rs[:, q:q + 1]))
                        elif c == 1:
                            ve.wait_ge(s_exp, u0 + u)
                            own.step(ve.reciprocal(rv[:, q8 - 1:q8 + 1], rs[:, q - 1:q + 1]))
                            own.step(ve.scalar_tensor_tensor(out=c1[:, 0:1], in0=rs[:, q - 1:q], scalar=neglam,
                                                             in1=rv[:, q8:q8 + 1], op0=ALU.mult, op1=ALU.mult))
                            ve.scalar_tensor_tensor(out=prob[:, q, lo:KEYS], in0=prob[:, q, lo:KEYS], scalar=c1[:, 0:1],
                                                    in1=prob[:, q - 1, lo:KEYS], op0=ALU.mult, op1=ALU.add)\
                                .then_inc(s_comb, 1)
                    for v, f in turn.get(u - 1, ()):
                        t, (kind, h, c) = seq[v]
                        q = v % 8 - (1 if kind == "df" else 0)
                        col = {"na": 0, "swa": 256, "df": 512}[kind] + h * 64
                        ve.wait_ge(pv_done, 1 + f0 + f + 1)
                        own.wait()
                        where = 0 if t is None else tile + t
                        ve.tensor_scalar(otm[:, where, col:col + 64], lp[1][:, f % 2, 0:64], rv[:, q:q + 1], None, ALU.mult)\
                            .then_inc(o_out, 1)

            ve.memset(epst, EPS)
            own.step(ve.memset(sqacc[:], 0.0))
            for k in range(KD):
                sum_square(k + 1, k % 2)
            PER_V = LOCAL["PER_V"]
            with ve.Fori(0, L) as l:
                own.enter(l, PER_V)
                ve.wait_ge(ld_v, 16 * (l + 1))
                ah = l * PER_SPL
                vf = l * PER_VF + 1
                for i in range(2):
                    lv = vc[:, V_LAM + 64 * i:V_LAM + 64 * i + 64]
                    m = ve.tensor_tensor_reduce(out=tmp[:, i, 0:32], in0=lv[:, 0:32], in1=lv[:, 32:64], scale=1.0, scalar=0.0,
                                                op0=ALU.mult, op1=ALU.add, accum_out=lam2[:, i:i + 1])
                m.then_inc(v_f, 1)
                ve.wait_ge(a_f, l + 1)
                own.step(ve.tensor_tensor(neglam, lam2[:, 1:2], lam2[:, 0:1], ALU.subtract))
                own.step(ve.tensor_tensor(neglam, neglam, vc[:, V_LI:V_LI + 1], ALU.subtract))
                ve.wait_ge(small_used[1], 1 + l * PER_SM + ADA_A // 2)
                for c in range(2):
                    m = ve.tensor_tensor(mod[:, 0:ADA_A, c], ss[1][:, 0, c:2 * ADA_A:2], vc[:, V_ADAB:V_ADAB + ADA_A], ALU.add)
                own.step(m)
                gains(0, 8, V_N1, 2 * l + 1)
                rstd_of(2 * l + 1)
                make_h(ah, vf, None)
                with ve.Fori(0, IN_B // 2) as j:
                    for s in range(2):
                        ve.wait_ge(turned, 1 + l * IN_B + 2 * j + s + 1)
                        ve.tensor_copy(tm[:, :, bass.ds((2 * j + s) * P, P)],
                                       sflat[s][:, 0:T].rearrange("p (t c) -> p t c", t=TILES)).then_inc(tmw, 1)
                for n, c in enumerate((SWA_Q, SWA_Q + 1, SWA_K, DIFF_Q, DIFF_Q + 1, DIFF_K, DIFF_K + 1)):
                    r = 0 if n < 3 else 2
                    ve.wait_ge(rot, l * 7 + n + 1)
                    ve.wait_ge(tmw, 1 + (l + 1) * IN_B)
                    ve.tensor_tensor(tmp[:, 0, 0:NLAT], ss[n % 2][:, 1 if n % 2 else 0, :], rp[:, r + 1, :], ALU.mult)
                    own.step(ve.tensor_tensor(tmp[:, 1, 0:NLAT], qk[:, c, NCTX:T], rp[:, r, :], ALU.mult))
                    ve.tensor_tensor(qk[:, c, NCTX:T], tmp[:, 0, 0:NLAT], tmp[:, 1, 0:NLAT], ALU.add).then_inc(roped, 1)
                    ve.wait_ge(roped, l * 7 + n + 1)
                soft(l, [(None, u) for u in UNITS_T], l * 5 * NU, l * 5 * NF, 0, 0, None)
                with ve.Fori(0, 2) as i:
                    own.enter(i, LOCAL["PER_ATT"])
                    soft(l, [(s, u) for s in range(2) for u in UNITS_T], l * 5 * NU + NU + i * 2 * NU,
                         l * 5 * NF + NF + i * 2 * NF, 1 + 2 * i, 0, i)
                    own.leave(2, LOCAL["PER_ATT"])
                ve.wait_ge(o_out, 1 + (l + 1) * 5 * NF)
                for t in range(TILES):
                    d = otm[:, t, 512:768]
                    m = ve.tensor_tensor(tmp[:, t // 2, (t % 2) * 256:(t % 2) * 256 + 256], d, d, ALU.mult)
                own.step(m)
                for t in range(TILES):
                    m = ve.tensor_reduce(ssq[:, 4 * t:4 * t + 4],
                                         tmp[:, t // 2, (t % 2) * 256:(t % 2) * 256 + 256].rearrange("p (h d) -> p h d", h=4),
                                         AX.X, ALU.add)
                m.then_inc(sub_a, 1)
                ve.wait_ge(sub_s, l + 1)
                own.step(ve.reciprocal(ssq, srt))
                own.step(ve.tensor_scalar(srt, ssq, vc[:, V_LI + 1:V_LI + 2], None, ALU.mult))
                for t in range(TILES):
                    for h in range(4):
                        d = otm[:, t, 512 + h * 64:576 + h * 64]
                        m = ve.scalar_tensor_tensor(out=d, in0=d, scalar=srt[:, 4 * t + h:4 * t + h + 1],
                                                    in1=vc[:, V_SUBG:V_SUBG + 64], op0=ALU.mult, op1=ALU.mult)
                m.then_inc(sub_d, 1)
                for n in range(6):
                    ve.wait_ge(a_hi, ah + SP0[S_BR] + n + 1)
                    c = n if n < 4 else n + 2
                    ve.tensor_tensor(BR[:, 1, c, :], sflat[n % 2][:, 0:T], BR[:, 0, c, :].bitcast(F32), ALU.subtract)\
                        .then_inc(split, 1)
                for c in range(2):
                    ve.wait_ge(a_hi, ah + SP0[S_BR] + 7 + c)
                    ve.tensor_tensor(BR[:, 1, 4 + c, :], yf[:, c, :], BR[:, 0, 4 + c, :].bitcast(F32), ALU.subtract)\
                        .then_inc(split, 1)
                make_h(ah + SP0[S_H1B], vf + KD, None)
                with ve.Fori(0, KD) as m_:
                    own.enter(m_, 2)
                    for b in range(NBR):
                        ve.wait_ge(lin[1], 1 + l * PER_DR + D0[GATE] + 4 * m_ + b + 1)
                        ve.wait_ge(drained[0], 1 + l * PER_DR + D0[GATE] + 4 * m_ + b + 1)
                        g = halves(tmp[:, 2 + b % 2, :])
                        if b == 0:
                            ve.wait_ge(v_f, vf + 2 * KD + m_)
                            m = ve.tensor_tensor(halves(tmp[:, 0, :]), lp[1][:, :, 0:TH], g, ALU.mult)
                            m.then_inc(drained[1], 1)
                        else:
                            ve.tensor_tensor(halves(tmp[:, 1, :]), lp[1][:, :, 0:TH], g, ALU.mult).then_inc(drained[1], 1)
                            ve.wait_ge(drained[1], 1 + l * PER_DR + D0[GATE] + 4 * m_ + b + 1)
                            if b < NBR - 1:
                                own.step(ve.tensor_tensor(tmp[:, 0, :], tmp[:, 0, :], tmp[:, 1, :], ALU.add))
                            else:
                                ve.tensor_tensor(mg[:, m_, :], tmp[:, 0, :], tmp[:, 1, :], ALU.add).then_inc(v_f, 1)
                    own.leave(KD, 2)
                ve.wait_ge(v_f, vf + 3 * KD)
                ve.wait_ge(small_used[1], 1 + (l + 1) * PER_SM)
                for c in range(2):
                    m = ve.tensor_tensor(mod[:, ADA_A:48, c], ss[1][:, 0, c:2 * ADA_B:2], vc[:, V_ADAB + ADA_A:V_ADAB + 48], ALU.add)
                own.step(m)
                gains(1, 32, V_N2, 2 * l + 2)
                for k in range(KD):
                    ve.wait_ge(a_hi, ah + SP0[S_MG] + k + 1)
                    ve.tensor_tensor(H[:, 1, k, :], mg[:, k, :], H[:, 0, k, :].bitcast(F32), ALU.subtract).then_inc(split, 1)
                with ve.Fori(0, KD // 2) as j:
                    for s in range(2):
                        residual(l, W_O, j, s, 16)
                        sum_square(l * 2 * KD + KD + 2 * j + s + 1, s)
                rstd_of(2 * l + 2)
                make_h(ah + SP0[S_H2], vf + 3 * KD, None)
                for ff, out, n, f0, sg in ((FF_A, OUT_A, FA, 0, S_GA), (FF_B, OUT_B, FB, FA, S_GB)):
                    with ve.Fori(0, n // 2) as j:
                        for s in range(2):
                            ve.wait_ge(lin[1], 1 + l * PER_DR + D0[ff] + 2 * j + s + 1)
                            ve.wait_ge(drained[0], 1 + l * PER_DR + D0[ff] + 2 * j + s + 1)
                            ve.tensor_tensor(halves(tmp[:, s, :]), lp[1][:, :, 0:TH], halves(tmp[:, 2 + s, :]), ALU.mult)\
                                .then_inc(drained[1], 1)
                            ve.wait_ge(drained[1], 1 + l * PER_DR + D0[ff] + 2 * j + s + 1)
                            ve.wait_ge(a_hi, ah + SP0[sg] + 2 * j + s + 1)
                            ve.tensor_tensor(G[:, 1, 2 * j + s, :], tmp[:, s, :], G[:, 0, 2 * j + s, :].bitcast(F32),
                                             ALU.subtract).then_inc(split, 1)
                    with ve.Fori(0, KD // 2) as j:
                        for s in range(2):
                            residual(l, out, j, s, 40)
                            if out == OUT_B:
                                sum_square(l * 2 * KD + 2 * KD + 2 * j + s + 1, s)
                own.leave(L, PER_V)
            rstd_of(2 * L + 1)
            for k in range(KD):
                own.step(ve.tensor_tensor(x[:, k, :], x[:, k, :], rstd[:], ALU.mult))
                ve.tensor_scalar(x[:, k, :], x[:, k, :], fg[:, k:k + 1], None, ALU.mult).then_inc(fin, 1)



def constants():
    f8 = np.float64
    con = np.zeros((P, NCC), f8)
    con[:, C_ID:C_ID + P] = np.eye(P)
    con[:, C_ONE:C_ONE + P] = 1
    rope = np.zeros((P, 4, NLAT), np.float32)
    rows, cols = np.arange(NLAT) // GRID_W, np.arange(NLAT) % GRID_W
    for n, (w, c0) in enumerate(((64, C_RS), (32, C_RD))):
        half, quarter = w // 2, w // 4
        inv = np.float32(10000.0) ** (-np.arange(quarter, dtype=np.float32) * np.float32(2.0) / np.float32(half))
        for p in range(P):
            d = p % w
            e = d % half
            ang = (rows if d < half else cols).astype(np.float32) * inv[e % quarter]
            rope[p, 2 * n], rope[p, 2 * n + 1] = np.cos(ang), np.sin(ang)
            if e < quarter:
                con[p + quarter, c0 + p] = -1
            else:
                con[p - quarter, c0 + p] = 1
    a64 = 2 * np.pi * (np.outer(np.arange(64), np.arange(64)) % 64) / 64
    for g in range(2):
        con[64 * g:64 * g + 64, C_CB + 64 * g:C_CB + 64 * g + 64] = np.cos(a64)
        con[64 * g:64 * g + 64, C_SB + 64 * g:C_SB + 64 * g + 64] = -np.sin(a64)
    a = 2 * np.pi * (np.outer(np.arange(P), np.arange(P)) % P) / P
    con[:, C_C1:C_C1 + P], con[:, C_S1:C_S1 + P] = np.cos(a), np.sin(a)
    a = 2 * np.pi * (np.outer(np.arange(NLAT), np.arange(NLAT)) % NLAT) / NLAT
    dft = np.stack([np.cos(a), np.sin(a)], 1).reshape(4, P, 2 * NLAT)
    return con.astype(np.float32), rope, dft.astype(np.float32)


def biases(rpb):
    tok = np.arange(NLAT)
    r, c = tok // GRID_W, tok % GRID_W
    cs = np.clip(c - 8, 0, GRID_W - 16)
    dr = r[None, :] - r[:, None] + 7
    dc = c[None, :] - c[:, None] + 15
    valid = (c[None, :] >= cs[:, None]) & (c[None, :] < cs[:, None] + 16)
    out = np.zeros((L, 5, NLAT, KEYS), np.float32)
    out[:, :4, :, :NLAT] = np.where(valid, rpb[:, :, dr, np.clip(dc, 0, 30)], np.float32(-1e30))
    out[:, 4, :, :NLAT] = np.where(np.abs(tok[None, :] - tok[:, None]) <= 128, 0, -1e30).astype(np.float32)
    return np.ascontiguousarray(out.reshape(L, 5, 4, P, KEYS).transpose(0, 2, 1, 3, 4))


def tiles(w):
    *lead, k, m = w.shape
    w = w.reshape(*lead, k // P, P, m // P, P)
    n = len(lead)
    w = w.transpose(*range(n), n + 2, n + 1, n, n + 3)
    return np.ascontiguousarray(w.reshape(*lead, m // P, P, k))


def kernel(**inputs):
    import concourse.bacc as _bacc
    from concourse.bass_utils import run_bass_kernel_spmd as _run

    I = {k: np.asarray(v) for k, v in inputs.items()}
    f4 = np.float32

    def col(v):
        return np.swapaxes(v.reshape(*v.shape[:-1], -1, P), -1, -2)

    x = np.concatenate([I["x_prompt"][0], I["x_sample"][0]], 0)
    A = {"xT": np.ascontiguousarray(x.T.reshape(KD, P, T).transpose(1, 0, 2))}
    A["ada"] = tiles(I["ada_w"])
    w = I["w_in"]
    swq = w[:, :, 768:1024].reshape(L, DM, 4, HD)[:, :, [0, 2, 1, 3]].reshape(L, DM, 256)
    order = [w[:, :, 0:256], swq, w[:, :, 1536:1792], w[:, :, 256:512], w[:, :, 1792:2048],
             w[:, :, 512:768], w[:, :, 1152:1280], w[:, :, 2048:2304], w[:, :, 1280:1536], w[:, :, 1024:1152]]
    A["win"] = tiles(np.concatenate(order, 2))
    gate = tiles(I["w_gate"]).reshape(L, NBR, KD, P, DM).transpose(0, 2, 1, 3, 4)
    up = tiles(I["w_branch"]).transpose(0, 2, 1, 3, 4)
    A["wgu"] = np.ascontiguousarray(np.concatenate([gate, up], 4)).reshape(L, N_GATE, P, (KD + 2) * P)
    A["wo"] = tiles(I["w_o"])
    ff = tiles(I["w_ffn_in"])
    nf = DFF // P
    A["wff"] = np.ascontiguousarray(np.stack([ff[:, :nf], ff[:, nf:]], 2)).reshape(L, 2 * nf, P, DM)
    A["wfa"] = tiles(I["w_ffn_out"][:, :FA * P])
    A["wfb"] = tiles(I["w_ffn_out"][:, FA * P:])
    rep = lambda v: np.broadcast_to(v.reshape(L, 1, -1), (L, P, v.reshape(L, -1).shape[1]))
    init = np.array([0.8 - 0.6 * math.exp(-0.3 * l) for l in range(L)])
    li = rep(np.stack([init, 1.0 - init], 1).astype(f4))
    bg = I["b_gate"].reshape(L, NBR, KD, P).transpose(0, 3, 2, 1).reshape(L, P, N_GATE)
    A["vec"] = np.ascontiguousarray(np.concatenate(
        [col(I["norm1_g"]), col(I["norm2_g"]), col(I["ada_b"]), bg, rep(I["swa_sink"]), rep(I["diff_subln_g"]),
         rep(I["diff_lambda"]), li], 2))
    A["cond"] = np.ascontiguousarray(np.stack([col(I["c_ctx"]), col(I["c"][0])], 2))
    A["fgv"] = np.ascontiguousarray(col(I["final_norm_g"]))
    A["cst"], A["rope"], A["dft"] = constants()
    A["bias"] = biases(I["na_rpb"])
    kT = lambda v: v[0, :, 0].transpose(0, 2, 3, 1).reshape(L, -1, P, PAST)
    A["ckT"] = np.ascontiguousarray(np.concatenate(
        [kT(I["cache_na_kv"]), kT(I["cache_swa_kv"]), kT(I["cache_diff_kv"])], 1).transpose(0, 2, 1, 3))
    vt = lambda v: v[0, :, 1].reshape(L, PAST, -1)
    A["cvt"] = np.ascontiguousarray(np.concatenate(
        [vt(I["cache_na_kv"]), vt(I["cache_swa_kv"]), vt(I["cache_diff_kv"])], 2))

    nc = _bacc.Bacc("TRN2", target_bir_lowering=False, num_devices=1)
    args = [nc.dram_tensor(n, a.shape, mybir.dt.from_np(a.dtype), kind="ExternalInput").ap() for n, a in A.items()]
    for n, shape in (("yT", (P, KD, T)), ("okT", (L, P, 5, NCTX)), ("ovt", (L, NCTX, 640))):
        args.append(nc.dram_tensor(n, shape, F32, kind="ExternalOutput").ap())
    build(nc, *args)
    out = _run(nc, [A], core_ids=[0]).results[0]
    y = out["yT"].transpose(1, 0, 2).reshape(DM, T).T
    ok, ov = out["okT"].transpose(0, 2, 1, 3), out["ovt"]
    back = lambda k, h: k.reshape(L, h, HD, NCTX).transpose(0, 3, 1, 2)
    pair = lambda k, v, h: np.ascontiguousarray(np.stack([back(k, h), v.reshape(L, NCTX, h, HD)], 1)[None])
    return (np.ascontiguousarray(y[:NCTX])[None], np.ascontiguousarray(y[NCTX:])[None],
            pair(ok[:, 0:2], ov[:, :, 0:256], 4), pair(ok[:, 4:5], ov[:, :, 256:384], 2),
            pair(ok[:, 2:4], ov[:, :, 384:640], 4))
```

```python
from contextlib import ExitStack
import math

import numpy as np

import concourse.bass as bass
from concourse import mybir

F32 = mybir.dt.float32
F32R = mybir.dt.float32r
ALU = mybir.AluOpType
ACT = mybir.ActivationFunctionType
AX = mybir.AxisListType

P = 128
DM = 1024
KD = DM // P
NCTX, NLAT = 128, 512
T = NCTX + NLAT
TH = T // 2
TILES = T // P
L = 2
DFF = 2816
HD = 64
GRID_W = 64
PAST = 128
KEYS = NLAT + PAST
EPS = 1e-6
SC_HEAD = HD ** -0.5
LOWEST = -3.0e38
SC_DIFF = 32 ** -0.5

NA_Q, SWA_Q, DIFF_Q, NA_K, DIFF_K, SWA_K = 0, 2, 4, 6, 8, 11
IN_A, IN_B = 10, 8
QK = IN_A + 2
V_NA, V_SWA, V_DIFF, FU = 0, 256, 384, 640
NBR = 4
FA, FB = 12, 10
N_GATE = KD * NBR
SLOTS = (IN_A + IN_B, N_GATE, KD, 2 * FA, KD, 2 * FB, KD)
SLOT0 = [sum(SLOTS[:i]) for i in range(8)]
CHUNKS = (IN_A + IN_B, 2 * N_GATE, KD, 2 * FA, KD, 2 * FB, KD)
D0 = [sum(CHUNKS[:i]) // 2 for i in range(8)]
UNITS = (KD, KD + 2, KD, KD, FA, KD, FB)
PER_SLOT = SLOT0[7] // 2
PER_DR = D0[7]
W_IN, GATE, W_O, FF_A, OUT_A, FF_B, OUT_B = range(7)
ADA_A, ADA_E = 16, 8
ADA_S, DFT, ADA_B = ADA_A - ADA_E, 4, 32
PER_SM = (ADA_S + DFT + ADA_B) // 2
LOCAL = {"PER_V": 194, "PER_ATT": 64}
UNITS_T = [("na", h, 0) for h in range(4)] + [("swa", h, 0) for h in range(4)] + \
          [("df", h, c) for h in range(4) for c in range(2)]
NU, NF, NC = 16, 12, 4
WARM = {0: 2, 2: 3, 4: 4}
V_N1, V_N2, V_ADAB, V_BG, V_SINK, V_SUBG, V_LAM, V_LI, NV = 0, 8, 16, 64, 96, 100, 164, 292, 294
C_ID, C_ONE, C_RS, C_RD, C_CB, C_SB, C_C1, C_S1, NCC = [i * P for i in range(9)]


def build(nc, xT, ada, win, wgu, wo, wff, wfa, wfb, vec, cond, fgv, cst, rope, dft, bias, ckT, cvt,
          yT, okT, ovt):
    with ExitStack() as ctx:
        def sb(name, shape, dt=F32, stack=ctx):
            return stack.enter_context(nc.sbuf_tensor(name, shape, dt))

        def sem(name):
            return ctx.enter_context(nc.semaphore(name))

        x = sb("x", [P, KD, T])
        rstd = sb("rstd", [P, T])
        sqacc = sb("sqacc", [P, T])
        tmp = sb("tmp", [P, 4, T])
        wst = sb("wst", [P, 2, FA * P])
        wr = sb("wr", [P, 2, 2, FA * P], F32R)
        small = sb("small", [P, 2, KD * P])
        con = sb("con", [P, NCC])
        rp = sb("rp", [P, 4, NLAT])
        vc = sb("vc", [P, NV])
        cd = sb("cd", [P, KD, 2])
        fg = sb("fg", [P, KD])
        mod = sb("mod", [P, 48, 2])
        am = sb("am", [P, 2, KD, 2])
        st = sb("st", [P, 80])
        nm, rs, rv = st[:, 0:4], st[:, 4:8], st[:, 64:72]
        lam2, neglam, c1 = st[:, 12:14], st[:, 14:15], st[:, 16:18]
        epst = st[:, 18:19]
        rt = st[:, 72:72 + TILES]
        ssq, srt = st[:, 20:40], st[:, 40:60]
        qs = sb("qs", [P, 2, 6, P])
        with ExitStack() as s1:
            H = sb("H", [P, 2, KD, T], F32R, s1)
        with ExitStack() as s1:
            prob = sb("prob", [P, 4, KEYS + 1], F32, s1)
            bt = sb("bt", [P, 3, KEYS], F32, s1)
            ck = sb("ck", [P, 5, PAST], F32, s1)
            cv = sb("cv", [P, 640], F32, s1)
            otm = sb("otm", [P, TILES, 768], F32, s1)
            yf = sb("yf", [P, 2, T], F32, s1)
        with ExitStack() as s1:
            adae = sb("adae", [P, ADA_E, KD * P], F32, s1)
            mrow = sb("mrow", [P, ADA_A * P], F32, s1)
        ft = prob[:, :, :].rearrange("p a b -> p (a b)")[:, 0:2048].rearrange("p (c s t) -> p c s t", c=2, s=2)
        ftp = prob[:, :, :].rearrange("p a b -> p (a b)")[:, 2048:2560].rearrange("p (c s t) -> p c s t", c=2, s=2)
        sb("region1", [P, 11008])
        with ExitStack() as s1:
            qk = sb("qk", [P, QK, T], F32, s1)
            sp = sb("sp", [P, 2, KEYS + 1], F32, s1)
            pts = sb("pts", [P, 2, KEYS], F32, s1)
            tm = sb("tm", [P, TILES, IN_B * P], F32, s1)
        with ExitStack() as s1:
            BR = sb("BR", [P, 2, KD, T], F32R, s1)
            sb("pad", [P, 16], F32, s1)
            mg = sb("mg", [P, KD, T], F32, s1)
        xn = mg
        with ExitStack() as s1:
            G = sb("G", [P, 2, FA, T], F32R, s1)

        lp = [ctx.enter_context(nc.psum_tensor(f"lp{i}", [P, 2, 512], F32)) for i in range(2)]
        ss = [ctx.enter_context(nc.psum_tensor(f"ss{i}", [P, 2, 512], F32)) for i in range(2)]
        pt = lp[0][:, :, :].rearrange("p a b -> p (a b)")
        sflat = [t[:, :, :].rearrange("p a b -> p (a b)") for t in ss]

        def halves(ap):
            return ap.rearrange("p (h t) -> p h t", h=2)

        ld_x, ld_c, ld_v, ld_cd, ld_r = sem("ld_x"), sem("ld_c"), sem("ld_v"), sem("ld_cd"), sem("ld_r")
        ld_a = [sem(f"ld_a{i}") for i in range(ADA_E // 2)]
        ada_rows, mrow_out, ada_turned = sem("ada_rows"), sem("mrow_out"), sem("ada_turned")
        ld_w = [sem(f"ld_w{i}") for i in range(2)]
        ld_s = [sem(f"ld_s{i}") for i in range(2)]
        ld_b = [sem(f"ld_b{i}") for i in range(3)]
        ld_k = sem("ld_k")
        st_k, st_y = sem("st_k"), sem("st_y")
        w_hi = [sem(f"w_hi{i}") for i in range(2)]
        w_lo = [sem(f"w_lo{i}") for i in range(2)]
        small_used = [sem(f"small_used{i}") for i in range(2)]
        lin = [sem(f"lin{i}") for i in range(2)]
        drained = [sem(f"drained{i}") for i in range(2)]
        split = sem("split")
        a_hi = sem("a_hi")
        norm_x = sem("norm_x")
        h_hi = sem("h_hi")
        a_f = sem("a_f")
        v_f = sem("v_f")
        a_own, v_own = sem("a_own"), sem("v_own")
        sq = sem("sq")
        sqs = sem("sqs")
        nsum = sem("nsum")
        nrt = sem("nrt")
        diag = sem("diag")
        nbc = sem("nbc")
        nrs = sem("nrs")
        cond_ready = sem("cond_ready")
        mods = sem("mods")
        turned, tmw = sem("turned"), sem("tmw")
        f1, f2, f3, f4 = sem("f1"), sem("f2"), sem("f3"), sem("f4")
        rot, roped = sem("rot"), sem("roped")
        staged = sem("staged")
        s_ready, s_pre, s_exp, s_comb = sem("s_ready"), sem("s_pre"), sem("s_exp"), sem("s_comb")
        t_done, pt_out, pv_done, o_out = sem("t_done"), sem("pt_out"), sem("pv_done"), sem("o_out")
        sub_a, sub_s, sub_d = sem("sub_a"), sem("sub_s"), sem("sub_d")
        bt_done = sem("bt_done")
        fin = sem("fin")

        SPLITS = (KD, KD, KD, KD, KD, FA, FB)
        SP0 = [sum(SPLITS[:i]) for i in range(8)]
        PER_SPL = SP0[7]
        PER_VF = 1 + 3 * KD // 2 + KD
        S_H1, S_BR, S_H1B, S_MG, S_H2, S_GA, S_GB = range(7)
        HI0, PER_HI = {S_BR: 0, S_MG: KD, S_GA: 2 * KD, S_GB: 2 * KD + FA}, 2 * KD + FA + FB

        def odd_h(l, use, k):
            return l * PER_VF + 1 + use * KD // 2 + (KD if use == 2 else 0) + (k + 1) // 2

        ident, ones = con[:, C_ID:C_ID + P], con[:, C_ONE:C_ONE + P]

        class Own:

            def __init__(self, eng, s):
                self.eng, self.s, self.base, self.n, self.kept = eng, s, 0, 0, []

            def mark(self, ins):
                self.n += 1
                ins.then_inc(self.s, 1)

            def wait(self):
                self.eng.wait_ge(self.s, self.base + self.n)

            def step(self, ins):
                self.mark(ins)
                self.wait()

            def enter(self, i, per):
                self.kept.append((self.base, self.n))
                self.base, self.n = self.base + self.n + i * per, 0

            def leave(self, times, per):
                assert self.n == per, (self.n, per)
                self.base, n = self.kept.pop()
                self.n = n + times * per

        def plan(seq):
            turn, combs, f = {}, [], 0
            for u, (_, (kind, _, c)) in enumerate(seq):
                if kind != "df" or c == 1:
                    turn.setdefault(u + 3, []).append((u, f))
                    f += 1
                combs.append(sum(1 for _, (k, _, c2) in seq[:u + 1] if k == "df" and c2 == 1))
            return turn, combs

        block = ctx.enter_context(nc.Block())

        @block.sync
        def _(sy):
            for started in (*w_lo, *small_used, *lin, *drained, tmw, o_out, pt_out, turned, pv_done):
                sy.sem_inc(started, 1)
            sy.dma_start(cd[:], cond).then_inc(ld_cd, 16)

            def early(l, i):
                sy.dma_start(adae[:, 2 * i:2 * i + 2, :], ada[l, 2 * i:2 * i + 2].rearrange("c p k -> p c k"))\
                    .then_inc(ld_a[i], 16)

            early(0, 0)
            early(0, 1)
            sy.dma_start(x[:], xT).then_inc(ld_x, 16)
            sy.dma_start(con[:], cst).then_inc(ld_c, 16)
            sy.dma_start(vc[:], vec[0]).then_inc(ld_v, 16)
            early(0, 2)
            early(0, 3)
            sy.dma_start(rp[:], rope).then_inc(ld_r, 16)
            sy.dma_start(fg[:], fgv).then_inc(ld_r, 16)

            def weight(l, stage, src, j, s, skip=0):
                n = l * PER_SLOT + SLOT0[stage] // 2 + j
                sy.wait_ge(w_lo[s], 1 + n)
                sy.dma_start(wst[:, s, 0:UNITS[stage] * P], src[l, 2 * j + s + skip]).then_inc(ld_w[s], 16)

            def little(l, first, src, j, s):
                sy.wait_ge(small_used[s], 1 + l * PER_SM + first // 2 + j)
                sy.dma_start(small[:, s, :], src).then_inc(ld_s[s], 16)

            with sy.Fori(0, L) as l:
                with sy.Fori(0, ADA_S // 2) as j:
                    for s in range(2):
                        little(l, 0, ada[l, 2 * j + s + ADA_E], j, s)
                with sy.Fori(0, (IN_A + IN_B) // 2) as j:
                    for s in range(2):
                        weight(l, W_IN, win, j, s)
                for j in range(2):
                    for s in range(2):
                        little(l, ADA_S, dft[2 * j + s], j, s)
                sy.wait_ge(lin[1], 1 + l * PER_DR + D0[GATE])
                sy.dma_start(ck[:], ckT[l]).then_inc(ld_k, 16)
                sy.dma_start(cv[:], cvt[l]).then_inc(ld_k, 16)
                for s in range(2):
                    weight(l, GATE, wgu, 0, s)
                sy.wait_ge(tmw, 1 + (l + 1) * IN_B)
                for n, c in enumerate((NA_K, NA_K + 1, DIFF_K, DIFF_K + 1, SWA_K)):
                    sy.dma_start(okT[l, :, n], qk[:, c, 0:NCTX]).then_inc(st_k, 16)
                sy.dma_start(ovt[l], tm[:, 0, 0:640]).then_inc(st_k, 16)
                with sy.Fori(0, 4) as i:
                    for h in range(4):
                        if h < 2:
                            sy.wait_ge(s_pre, l * 5 * NU + NU + i * NU - NU + h + 3)
                        else:
                            sy.wait_ge(s_pre, l * 5 * NU + NU + i * NU + h - 1)
                        sy.dma_start(bt[:, h % 2, :], bias[l, i, h]).then_inc(ld_b[h % 2], 16)
                    sy.dma_start(bt[:, 2, :], bias[l, i, 4]).then_inc(ld_b[2], 16)

                def smalls(j):
                    for s in range(2):
                        little(l, ADA_S + DFT, ada[l, 2 * j + s + ADA_A], j, s)

                smalls(0)
                with sy.Fori(1, N_GATE // 2) as j:
                    for s in range(2):
                        weight(l, GATE, wgu, j, s)
                    smalls(j)
                for stage, src in ((W_O, wo), (FF_A, wff), (OUT_A, wfa), (FF_B, wff)):
                    with sy.Fori(0, SLOTS[stage] // 2) as j:
                        for s in range(2):
                            weight(l, stage, src, j, s, 2 * FA if stage == FF_B else 0)
                for j in range(KD // 2):
                    for s in range(2):
                        weight(l, OUT_B, wfb, j, s)
                    if j == 0:
                        for s in range(2):
                            sy.wait_ge(lin[s], 1 + l * PER_DR + D0[OUT_B])
                    early((l + 1) % L, j)
                sy.wait_ge(drained[1], 1 + (l + 1) * PER_DR)
                sy.wait_ge(drained[0], 1 + (l + 1) * PER_DR)
                sy.dma_start(vc[:], vec[(l + 1) % L]).then_inc(ld_v, 16)
            for k in range(KD):
                sy.wait_ge(fin, k + 1)
                sy.dma_start(yT[:, k, :], x[:, k, :]).then_inc(st_y, 16)
            sy.wait_ge(st_y, 16 * KD)
            sy.wait_ge(st_k, 16 * 6 * L)
            sy.wait_ge(ld_v, 16 * (L + 1))
            for i in range(ADA_E // 2):
                sy.wait_ge(ld_a[i], 16 * (L + 1))

        @block.gpsimd
        def _(pool):
            pool.wait_ge(ld_c, 16)

            def split_weights(l, stage, j, s):
                n = l * PER_SLOT + SLOT0[stage] // 2 + j
                w = UNITS[stage] * P
                pool.wait_ge(ld_w[s], 16 * (n + 1))
                if stage == GATE and not isinstance(j, int):
                    pool.wait_ge(lin[1], 1 + l * PER_DR + D0[GATE] + 2 * j + s - 1)
                else:
                    pool.wait_ge(lin[s], 1 + l * PER_DR + D0[stage] + j)
                pool.tensor_tensor(wr[:, s, 0, 0:w], wst[:, s, 0:w], con[:, C_ONE:C_ONE + 1].to_broadcast([P, w]), ALU.mult).then_inc(w_hi[s], 1)
                pool.wait_ge(w_hi[s], n + 1)
                pool.tensor_tensor(wr[:, s, 1, 0:w], wst[:, s, 0:w], wr[:, s, 0, 0:w].bitcast(F32),
                                   ALU.subtract).then_inc(w_lo[s], 1)

            with pool.Fori(0, L) as l:
                with pool.Fori(0, SLOTS[W_IN] // 2) as j:
                    for s in range(2):
                        split_weights(l, W_IN, j, s)
                for s in range(2):
                    split_weights(l, GATE, 0, s)
                with pool.Fori(0, 2) as i:
                    pool.wait_ge(roped, (l + 1) * 7)
                    for s in range(2):
                        pool.wait_ge(s_ready, l * 5 * NU + (2 * i + s) * NU + (1 - s))
                        pool.tensor_copy(qs[:, s, :, :], qk[:, 0:6, bass.ds(NCTX + (2 * i + s) * P, P)])\
                            .then_inc(staged, 1)
                pool.wait_ge(pv_done, 1 + (l + 1) * 5 * NF)
                pool.wait_ge(st_k, 16 * 6 * (l + 1))
                pool.wait_ge(nrs, l + 1)
                for k in range(KD):
                    pool.tensor_tensor(xn[:, k, :], x[:, k, :], rstd[:], ALU.mult).then_inc(norm_x, 1)
                with pool.Fori(1, SLOTS[GATE] // 2) as j:
                    for s in range(2):
                        split_weights(l, GATE, j, s)
                for stage in (W_O, FF_A, OUT_A, FF_B, OUT_B):
                    with pool.Fori(0, SLOTS[stage] // 2) as j:
                        for s in range(2):
                            split_weights(l, stage, j, s)

        @block.tensor
        def _(pe):
            def product(out, w, act, k, first, last):
                for i, (wi, ai) in enumerate(((0, 0), (0, 1), (1, 0))):
                    for h in range(2):
                        mm = pe.matmul(out[:, h, 0:TH], w[wi], act[:, ai, k, h * TH:(h + 1) * TH],
                                       start=first and i == 0, stop=last and i == 2)
                return mm

            def chunk(l, stage, j, s, act, kk, unit0=0, c=None, pair=None, ready=None):
                pair = s if pair is None else pair
                pe.wait_ge(drained[pair], 1 + l * PER_DR + D0[stage] + (j if c is None else c))
                for n, k in enumerate(kk):
                    if ready is not None:
                        pe.wait_ge(split, l * PER_SPL + SP0[ready] + n + 1)
                    w = [wr[:, s, i, (unit0 + n) * P:(unit0 + n + 1) * P] for i in range(2)]
                    mm = product(lp[pair], w, act, k, n == 0, n == len(kk) - 1)
                mm.then_inc(lin[pair], 1)

            def weights(l, stage, j, s):
                pe.wait_ge(w_lo[s], 1 + l * PER_SLOT + SLOT0[stage] // 2 + j + 1)

            def ada_chunk(l, first, j, s, col):
                pe.wait_ge(ld_s[s], 16 * (l * PER_SM + first // 2 + j + 1))
                for k in range(KD):
                    mm = pe.matmul(ss[1][:, 0, col], small[:, s, k * P:(k + 1) * P], cd[:, k, :],
                                   start=(k == 0), stop=(k == KD - 1))
                mm.then_inc(small_used[s], 1)

            def norm_sum(n):
                pe.wait_ge(ld_c, 16)
                pe.wait_ge(sqs, n)
                for t in range(TILES):
                    mm = pe.matmul(ss[0][:, 0, t:t + 1], sqacc[:, t * P:(t + 1) * P], ones[:, 0:1], start=True, stop=True)
                mm.then_inc(nsum, 1)

            def norm_spread(n):
                for t in range(TILES):
                    pe.wait_ge(diag, n * TILES + t + 1)
                    mm = pe.matmul(sflat[0][:, t * P:(t + 1) * P], ones, rstd[:, t * P:(t + 1) * P], start=True, stop=True)
                mm.then_inc(nbc, 1)

            def warm(times):
                for _ in range(times):
                    pe.matmul(lp[1][:, 0, P:512], ident, con[:, 0:512 - P], start=True, stop=True)

            def attend(seq, u0, f0, comb0):
                turn, combs = plan(seq)
                if seq[0][0] is not None:
                    pe.wait_ge(o_out, 1 + f0)
                    warm(WARM[0])
                for u in range(len(seq) + 5):
                    if u < len(seq):
                        t, (kind, h, c) = seq[u]
                        if u >= 2:
                            pt_, (k_, _, _) = seq[u - 2]
                            if (k_ == "na" and pt_ is not None) or k_ == "swa":
                                pe.wait_ge(s_pre, u0 + u - 1)
                            else:
                                pe.wait_ge(s_exp, u0 + u - 1)
                        if kind == "na":
                            qc, kc, p0, n = NA_Q + h // 2, NA_K + h // 2, (h % 2) * 64, 64
                            cc = h // 2
                        elif kind == "swa":
                            qc, kc, p0, n = SWA_Q + h % 2, SWA_K, (h // 2) * 64, 64
                            cc = 2
                        else:
                            qc, kc, p0, n = DIFF_Q + h // 2, DIFF_K + h // 2, (h % 2) * 64 + c * 32, 32
                            cc = 3 + h // 2
                        out = sflat[u % 2]
                        if t is None:
                            mm = pe.matmul(out[:, NLAT:KEYS], qk[p0:p0 + n, qc, 0:NCTX], qk[p0:p0 + n, kc, 0:NCTX],
                                           start=True, stop=True)
                        else:
                            q = qs[p0:p0 + n, t, qc, :]
                            pe.matmul(out[:, 0:NLAT], q, qk[p0:p0 + n, kc, NCTX:T], start=True, stop=True)
                            mm = pe.matmul(out[:, NLAT:KEYS], q, ck[p0:p0 + n, cc, :], start=True, stop=True)
                        mm.then_inc(s_ready, 1)
                        if t is not None:
                            warm(WARM.get(u + 1, 0))
                    for v, f in turn.get(u - 1, ()):
                        t, (kind, h, c) = seq[v]
                        pe.wait_ge(pt_out, 1 + f0 + f + 1)
                        pe.wait_ge(o_out, 1 + f0 + f - 1) if f >= 2 else pe.wait_ge(o_out, 1 + f0)
                        v0 = {"na": V_NA + h * 64, "swa": V_SWA + (h // 2) * 64, "df": V_DIFF + h * 64}[kind]
                        v0 -= v0 % P
                        js = (4,) if t is None else range(5)
                        for j in js:
                            val = tm[:, 0, v0:v0 + P] if t is None else \
                                cv[:, v0:v0 + P] if j == 4 else tm[:, 1 + j, v0:v0 + P]
                            mm = pe.matmul(lp[1][:, f % 2, 0:P], pts[:, f % 2, j * P:(j + 1) * P], val,
                                           start=(j == js[0]), stop=(j == 4))
                        mm.then_inc(pv_done, 1)
                    for v, f in turn.get(u, ()):
                        t, (kind, h, c) = seq[v]
                        if kind == "df":
                            pe.wait_ge(s_comb, comb0 + combs[v])
                        else:
                            pe.wait_ge(s_exp, u0 + v + 1)
                        pe.wait_ge(pt_out, 1 + f0 + f)
                        src = prob[:, v % 4, :]
                        for j in (4,) if t is None else range(5):
                            mm = pe.transpose(pt[:, j * P:(j + 1) * P], src[:, j * P:(j + 1) * P], ident)
                        mm.then_inc(t_done, 1)

            pe.wait_ge(cond_ready, 1)
            with pe.Fori(0, L) as l:
                for s in range(2):
                    pe.wait_ge(drained[s], 1 + l * PER_DR)
                for m in range(ADA_A):
                    if m < ADA_E:
                        if m % 2 == 0:
                            pe.wait_ge(ld_a[m // 2], 16 * (l + 1))
                        w = adae[:, m, :]
                    else:
                        pe.wait_ge(ld_s[m % 2], 16 * (l * PER_SM + (m - ADA_E) // 2 + 1))
                        w = small[:, m % 2, :]
                    for k in range(KD):
                        mm = pe.matmul(lp[m // 8][0:2, m // 4 % 2, m % 4 * P:(m % 4 + 1) * P], cd[:, k, :],
                                       w[:, k * P:(k + 1) * P], start=(k == 0), stop=(k == KD - 1))
                    if m == ADA_E - 1:
                        mm.then_inc(ada_rows, 1)
                        norm_sum(l * 2 * KD + KD)
                    elif m >= ADA_E:
                        mm.then_inc(small_used[m % 2], 1)
                    if m == ADA_E + 1:
                        norm_spread(2 * l)
                pe.wait_ge(mrow_out, 2 * (l + 1))
                for m in range(ADA_A):
                    mm = pe.matmul(ss[1][:, 0, 2 * m:2 * m + 2], mrow[0:2, m * P:(m + 1) * P], con[0:2, C_ID:C_ID + 2],
                                   start=True, stop=True)
                mm.then_inc(ada_turned, 1)
                with pe.Fori(0, IN_A // 2) as j:
                    for s in range(2):
                        weights(l, W_IN, j, s)
                        chunk(l, W_IN, j, s, H, range(KD), ready=None if s else S_H1)

                with pe.Fori(0, IN_B // 2) as j:
                    for s in range(2):
                        weights(l, W_IN, j + IN_A // 2, s)
                        chunk(l, W_IN, j + IN_A // 2, s, H, range(KD))
                    for s in range(2):
                        pe.wait_ge(drained[s], 1 + l * PER_DR + IN_A // 2 + j + 1)
                        pe.wait_ge(tmw, 1 + l * IN_B + 2 * j)
                        for t in range(TILES):
                            mm = pe.transpose(sflat[s][:, t * P:(t + 1) * P], qk[:, IN_A + s, t * P:(t + 1) * P], ident)
                        mm.then_inc(turned, 1)
                pe.wait_ge(tmw, 1 + (l + 1) * IN_B)
                turns = (SWA_Q, SWA_Q + 1, SWA_K, DIFF_Q, DIFF_Q + 1, DIFF_K, DIFF_K + 1)
                for kc in range(4):
                    for n in range(2 * kc, min(2 * kc + 2, len(turns))):
                        r = C_RS if n < 3 else C_RD
                        if n >= 2:
                            pe.wait_ge(roped, l * 7 + n - 1)
                        pe.matmul(ss[n % 2][:, n % 2, :], con[:, r:r + P], qk[:, turns[n], NCTX:T], start=True, stop=True)\
                            .then_inc(rot, 1)
                    s = kc % 2
                    pe.wait_ge(ld_s[s], 16 * (l * PER_SM + ADA_S // 2 + kc // 2 + 1))
                    for c in range(2):
                        for i in range(2):
                            mm = pe.matmul(lp[c][:, i, :], tm[:, 1 + kc, FU + c * P:FU + (c + 1) * P],
                                           small[:, s, i * NLAT:(i + 1) * NLAT], start=(kc == 0), stop=(kc == 3))
                    mm.then_inc(small_used[s], 1)
                for c in range(2):
                    for i in range(2):
                        mm = pe.matmul(ss[1][:, 0, (2 * c + i) * P:(2 * c + i + 1) * P], tm[:, 0, FU + c * P:FU + (c + 1) * P],
                                       con[:, C_C1 + i * P:C_C1 + (i + 1) * P], start=True, stop=True)
                mm.then_inc(f1, 1)
                pe.wait_ge(f2, l * 3 + 3)
                for c in range(2):
                    for i in range(2):
                        mm = pe.matmul(lp[0][:, c, :], con[:, C_CB + i * P:C_CB + (i + 1) * P], ft[:, c, i, :],
                                       start=(i == 0), stop=(i == 1))
                for c in range(2):
                    for i in range(2):
                        mm = pe.matmul(lp[1][:, 0, c * P:(c + 1) * P], con[:, C_CB + i * P:C_CB + (i + 1) * P], ftp[:, c, i, :],
                                       start=(i == 0), stop=(i == 1))
                mm.then_inc(f3, 1)
                pe.wait_ge(f4, l + 1)
                pe.wait_ge(roped, (l + 1) * 7)
                attend([(None, u) for u in UNITS_T], l * 5 * NU, l * 5 * NF, l * 5 * NC)
                pe.wait_ge(o_out, 1 + l * 5 * NF + NF)
                warm(6)
                with pe.Fori(0, 2) as i:
                    pe.wait_ge(ld_k, 32 * (l + 1))
                    pe.wait_ge(staged, l * 4 + 2 * i + 2)
                    attend([(s, u) for s in range(2) for u in UNITS_T], l * 5 * NU + NU + i * 2 * NU,
                           l * 5 * NF + NF + i * 2 * NF, l * 5 * NC + NC + i * 2 * NC)
                for n in range(6):
                    if n == 0:
                        pe.wait_ge(o_out, 1 + (l + 1) * 5 * NF)
                    if n == 4:
                        pe.wait_ge(sub_d, l + 1)
                    if n >= 2:
                        pe.wait_ge(split, l * PER_SPL + SP0[S_BR] + n - 1)
                    for t in range(TILES):
                        mm = pe.transpose(sflat[n % 2][:, t * P:(t + 1) * P], otm[:, t, n * P:(n + 1) * P], ident)
                    mm.then_inc(bt_done, 1)
                def gate_pair(m, b, j, s):
                    weights(l, GATE, j, s)
                    chunk(l, GATE, j, s, H, range(KD), c=2 * j + s, pair=0, ready=None if b else S_H1B)
                    chunk(l, GATE, j, s, BR, (2 * b, 2 * b + 1), unit0=KD, c=2 * j + s, pair=1)
                    ada_chunk(l, ADA_S + DFT, j, s, bass.ds(2 * (2 * j + s), 2))

                with pe.Fori(0, KD) as m:
                    for b in range(NBR):
                        gate_pair(m, b, 2 * m + b // 2, b % 2)
                with pe.Fori(0, KD // 2) as j:
                    for s in range(2):
                        weights(l, W_O, j, s)
                        chunk(l, W_O, j, s, H, range(KD), ready=None if s else S_MG)
                norm_sum(l * 2 * KD + 2 * KD)
                norm_spread(2 * l + 1)
                for ff, out, inner in ((FF_A, OUT_A, S_GA), (FF_B, OUT_B, S_GB)):
                    with pe.Fori(0, SLOTS[ff] // 2) as j:
                        for s in range(2):
                            weights(l, ff, j, s)
                            chunk(l, ff, j, s, H, range(KD), ready=None if s else S_H2)
                    with pe.Fori(0, KD // 2) as j:
                        for s in range(2):
                            weights(l, out, j, s)
                            chunk(l, out, j, s, G, range(UNITS[out]), ready=None if s else inner)
            norm_sum(L * 2 * KD + KD)
            norm_spread(2 * L)

        @block.scalar
        def _(act):
            own = Own(act, a_own)

            def root(l, n, base):
                act.wait_ge(nsum, base)
                act.activation(rt, ss[0][:, 0, 0:TILES], ACT.Sqrt, bias=epst, scale=1.0 / DM).then_inc(nrt, 1)

            def h_hi_part(l, use, k):
                which, shift = (1, 24) if use == 2 else (0, 0)
                if k % 2 == 0:
                    act.wait_ge(norm_x, (l * 3 + use) * KD + k + 1)
                    act.activation(xn[:, k, 0:NCTX], xn[:, k, 0:NCTX], ACT.Identity, bias=mod[:, shift + k, 0:1],
                                   scale=am[:, which, k, 0:1])
                    own.step(act.activation(xn[:, k, NCTX:T], xn[:, k, NCTX:T], ACT.Identity,
                                            bias=mod[:, shift + k, 1:2], scale=am[:, which, k, 1:2]))
                else:
                    act.wait_ge(v_f, odd_h(l, use, k))
                act.activation(H[:, 0, k, :], xn[:, k, :], ACT.Copy).then_inc(h_hi, 1)

            def exps(l, seq, u0, f0, comb0):
                turn, combs = plan(seq)
                done = {v: f for vf in turn.values() for v, f in vf}
                for u in range(len(seq) + 5):
                    for v, f in turn.get(u, ()):
                        lo = NLAT if seq[v][0] is None else 0
                        act.wait_ge(t_done, f0 + f + 1)
                        act.wait_ge(pv_done, 1 + f0 + max(f - 1, 0))
                        act.activation(pts[:, f % 2, lo:KEYS], pt[:, lo:KEYS], ACT.Copy).then_inc(pt_out, 1)
                    if u < len(seq):
                        t, (kind, h, c) = seq[u]
                        lo = NLAT if t is None else 0
                        act.wait_ge(s_pre, u0 + u + 1)
                        if u >= 4:
                            if u - 4 in done:
                                act.wait_ge(t_done, f0 + done[u - 4] + 1)
                            else:
                                act.wait_ge(s_comb, comb0 + combs[u - 3])
                        if kind == "swa":
                            act.activation(prob[:, u % 4, lo:KEYS + 1], sp[:, u % 2, lo:KEYS + 1], ACT.Exp,
                                           bias=nm[:, u % 4:u % 4 + 1], accum_out=rs[:, u % 4:u % 4 + 1]).then_inc(s_exp, 1)
                        elif kind == "na" and t is not None:
                            act.activation(prob[:, u % 4, 0:KEYS], sp[:, u % 2, 0:KEYS], ACT.Exp,
                                           bias=nm[:, u % 4:u % 4 + 1], accum_out=rs[:, u % 4:u % 4 + 1]).then_inc(s_exp, 1)
                        else:
                            act.activation(prob[:, u % 4, lo:KEYS], sflat[u % 2][:, lo:KEYS], ACT.Exp,
                                           bias=nm[:, u % 4:u % 4 + 1], scale=1.0 if kind == "na" else SC_DIFF,
                                           accum_out=rs[:, u % 4:u % 4 + 1]).then_inc(s_exp, 1)

            act.wait_ge(ld_cd, 16)
            act.activation(tmp[:, 2, 0:2 * KD], cd[:, :, :].rearrange("p k c -> p (k c)"), ACT.Silu).then_inc(a_own, 1)
            own.n += 1
            own.wait()
            act.activation(cd[:, :, :].rearrange("p k c -> p (k c)"), tmp[:, 2, 0:2 * KD], ACT.Copy).then_inc(cond_ready, 1)
            act.wait_ge(cond_ready, 1)
            act.wait_ge(ld_x, 16)
            for k in range(KD):
                if k >= 2:
                    act.wait_ge(sqs, k - 1)
                act.activation(tmp[:, 2 + k % 2, :], x[:, k, :], ACT.Square).then_inc(sq, 1)
            PER_A = 3 * KD // 2
            with act.Fori(0, L) as l:
                own.enter(l, PER_A)
                act.wait_ge(ld_v, 16 * (l + 1))
                act.wait_ge(v_f, l * PER_VF + 1)
                act.activation(lam2, lam2, ACT.Exp).then_inc(a_f, 1)
                act.wait_ge(ada_rows, l + 1)
                act.activation(mrow[0:2, 0:ADA_A * P // 2], lp[0][0:2, :, :].rearrange("p a b -> p (a b)"), ACT.Copy)\
                    .then_inc(mrow_out, 1)
                act.wait_ge(sqs, l * 2 * KD + KD)
                root(l, 0, l * 2 + 1)
                act.wait_ge(small_used[1], 1 + l * PER_SM + ADA_S // 2)
                act.activation(mrow[0:2, ADA_A * P // 2:ADA_A * P], lp[1][0:2, :, :].rearrange("p a b -> p (a b)"), ACT.Copy)\
                    .then_inc(mrow_out, 1)
                act.wait_ge(nbc, l * 2 + 1)
                act.activation(rstd[:], sflat[0][:, 0:T], ACT.Copy).then_inc(nrs, 1)
                act.wait_ge(mods, l * 2 + 1)
                for k in range(KD):
                    h_hi_part(l, 0, k)
                for j0, j1, scale in ((0, DIFF_Q // 2, SC_HEAD), (DIFF_Q // 2, IN_A // 2, 1.0)):
                    with act.Fori(j0, j1) as j:
                        for s in range(2):
                            act.wait_ge(lin[s], 1 + l * PER_DR + j + 1)
                            act.activation(halves(qk[:, 2 * j + s, :]), lp[s][:, :, 0:TH], ACT.Copy, scale=scale)\
                                .then_inc(drained[s], 1)
                with act.Fori(0, IN_B // 2) as j:
                    for s in range(2):
                        act.wait_ge(lin[s], 1 + l * PER_DR + IN_A // 2 + j + 1)
                        act.wait_ge(turned, 1 + l * IN_B + 2 * j)
                        act.activation(halves(qk[:, IN_A + s, :]), lp[s][:, :, 0:TH], ACT.Copy).then_inc(drained[s], 1)
                act.wait_ge(f1, l + 1)
                for c in range(2):
                    act.activation(ft[:, c, :, :], lp[c][:, :, :], ACT.Copy).then_inc(f2, 1)
                act.activation(ftp.rearrange("p c s t -> p (c s t)"), ss[1][:, 0, :], ACT.Copy).then_inc(f2, 1)
                act.wait_ge(f3, l + 1)
                act.activation(yf[:, :, NCTX:T], lp[0][:, :, :], ACT.Copy, scale=(NLAT * HD) ** -0.5)
                act.activation(yf[:, :, 0:NCTX], lp[1][:, 0, 0:2 * P].rearrange("p (c t) -> p c t", c=2), ACT.Copy,
                               scale=(NCTX * HD) ** -0.5).then_inc(f4, 1)
                act.wait_ge(f4, l + 1)
                exps(l, [(None, u) for u in UNITS_T], l * 5 * NU, l * 5 * NF, l * 5 * NC)
                with act.Fori(0, 2) as i:
                    exps(l, [(s, u) for s in range(2) for u in UNITS_T], l * 5 * NU + NU + i * 2 * NU,
                         l * 5 * NF + NF + i * 2 * NF, l * 5 * NC + NC + i * 2 * NC)
                act.wait_ge(st_k, 16 * 6 * (l + 1))
                for n in range(6):
                    act.wait_ge(bt_done, l * 6 + n + 1)
                    c = n if n < 4 else n + 2
                    if n == 0:
                        act.wait_ge(pv_done, 1 + (l + 1) * 5 * NF)
                    act.activation(BR[:, 0, c, :], sflat[n % 2][:, 0:T], ACT.Copy).then_inc(a_hi, 1)
                    if n == 1:
                        act.wait_ge(sub_a, l + 1)
                        act.activation(srt, ssq, ACT.Sqrt, bias=epst, scale=1.0 / HD).then_inc(sub_s, 1)
                    if n >= 3:
                        h_hi_part(l, 1, n - 3)
                for c in range(2):
                    act.activation(BR[:, 0, 4 + c, :], yf[:, c, :], ACT.Copy).then_inc(a_hi, 1)
                for k in range(3, KD):
                    h_hi_part(l, 1, k)
                with act.Fori(0, KD) as m:
                    for b in range(NBR):
                        act.wait_ge(lin[0], 1 + l * PER_DR + D0[GATE] + 4 * m + b + 1)
                        act.wait_ge(drained[1], 1 + l * PER_DR + D0[GATE] + 4 * m + b - 1)
                        act.activation(halves(tmp[:, 2 + b % 2, :]), lp[0][:, :, 0:TH], ACT.Sigmoid,
                                       bias=vc[:, bass.ds(V_BG + 4 * m + b, 1)]).then_inc(drained[0], 1)
                act.wait_ge(lin[1], 1 + l * PER_DR + D0[W_O])
                for k in range(KD):
                    if k == 0:
                        act.wait_ge(v_f, l * PER_VF + 1 + 2 * KD)
                    act.activation(H[:, 0, k, :], mg[:, k, :], ACT.Copy).then_inc(a_hi, 1)
                with act.Fori(0, KD // 2) as j:
                    for s in range(2):
                        act.wait_ge(drained[s], 1 + l * PER_DR + D0[W_O] + j + 1)
                        act.wait_ge(sqs, l * 2 * KD + KD + 2 * j + s - 1)
                        act.activation(tmp[:, 2 + s, :], x[:, 2 * j + s, :], ACT.Square).then_inc(sq, 1)
                act.wait_ge(sqs, l * 2 * KD + 2 * KD)
                root(l, 1, l * 2 + 2)
                act.wait_ge(mods, l * 2 + 2)
                for k in range(KD):
                    h_hi_part(l, 2, k)
                for ff, out, n, f0, sg in ((FF_A, OUT_A, FA, 0, S_GA), (FF_B, OUT_B, FB, FA, S_GB)):
                    with act.Fori(0, n // 2) as j:
                        for s in range(2):
                            act.wait_ge(lin[0], 1 + l * PER_DR + D0[ff] + 2 * j + s + 1)
                            act.activation(halves(tmp[:, 2 + s, :]), lp[0][:, :, 0:TH], ACT.Silu).then_inc(drained[0], 1)
                            act.wait_ge(drained[1], 1 + l * PER_DR + D0[ff] + 2 * j + s + 1)
                            act.activation(G[:, 0, 2 * j + s, :], tmp[:, s, :], ACT.Copy).then_inc(a_hi, 1)
                    if out == OUT_B:
                        with act.Fori(0, KD // 2) as j:
                            for s in range(2):
                                act.wait_ge(drained[s], 1 + l * PER_DR + D0[OUT_B] + j + 1)
                                act.wait_ge(sqs, l * 2 * KD + 2 * KD + 2 * j + s - 1)
                                act.activation(tmp[:, 2 + s, :], x[:, 2 * j + s, :], ACT.Square).then_inc(sq, 1)
                own.leave(L, PER_A)
            root(L, 0, 2 * L + 1)

        @block.vector
        def _(ve):
            own = Own(ve, v_own)

            def rstd_of(n):
                ve.wait_ge(nrt, n)
                own.step(ve.reciprocal(rt, rt))
                for t in range(TILES):
                    ve.tensor_scalar(rstd[:, t * P:(t + 1) * P], ident, rt[:, t:t + 1], None, ALU.mult).then_inc(diag, 1)
                ve.wait_ge(nbc, n)

            def sum_square(n, k2):
                ve.wait_ge(sq, n)
                ve.tensor_tensor(sqacc[:], sqacc[:], tmp[:, 2 + k2, :], ALU.add).then_inc(sqs, 1)
                ve.wait_ge(sqs, n)

            def normalised(k, over_rms):
                ve.tensor_tensor(xn[:, k, :], x[:, k, :], over_rms, ALU.mult).then_inc(norm_x, 1)

            def odd(l, use, k):
                which, shift = (1, 24) if use == 2 else (0, 0)
                ve.wait_ge(norm_x, (l * 3 + use) * KD + k + 1)
                for a, b, c in ((0, NCTX, 0), (NCTX, T, 1)):
                    m = ve.tensor_scalar(xn[:, k, a:b], xn[:, k, a:b], am[:, which, k, c:c + 1],
                                         mod[:, shift + k, c:c + 1], ALU.mult, ALU.add)
                m.then_inc(v_f, 1)

            def h_lo_part(l, use, k):
                ve.wait_ge(h_hi, (l * 3 + use) * KD + k + 1)
                ve.tensor_tensor(H[:, 1, k, :], xn[:, k, :], H[:, 0, k, :].bitcast(F32), ALU.subtract).then_inc(split, 1)

            def gains(which, scale, gain, n):
                for c in range(2):
                    m = ve.scalar_tensor_tensor(out=am[:, which, :, c], in0=mod[:, scale:scale + KD, c], scalar=1.0,
                                                in1=vc[:, gain:gain + KD], op0=ALU.add, op1=ALU.mult)
                m.then_inc(mods, 1)
                ve.wait_ge(mods, n)

            def residual(l, stage, j, s, gate):
                ve.wait_ge(lin[s], 1 + l * PER_DR + D0[stage] + j + 1)
                k = 2 * j + s
                for a, b, c in ((0, NCTX, 0), (NCTX, TH, 1), (TH, T, 1)):
                    h = a // TH
                    m = ve.scalar_tensor_tensor(out=x[:, k, a:b], in0=lp[s][:, h, a - h * TH:b - h * TH],
                                                scalar=mod[:, gate + 2 * j + s, c:c + 1], in1=x[:, k, a:b],
                                                op0=ALU.mult, op1=ALU.add)
                m.then_inc(drained[s], 1)

            def soft(l, seq, u0, f0, tile, comb0, i):
                turn, combs = plan(seq)
                for u in range(len(seq) + 5):
                    if u < len(seq):
                        t, (kind, h, c) = seq[u]
                        lo = NLAT if t is None else 0
                        ve.wait_ge(s_ready, u0 + u + 1)
                        mx = nm[:, u % 4:u % 4 + 1]
                        S = sflat[u % 2]
                        if kind == "swa" or (kind == "na" and t is not None):
                            if u >= 2:
                                ve.wait_ge(s_exp, u0 + u - 1)
                            hi = KEYS + (kind == "swa")
                            if kind == "na":
                                ve.wait_ge(ld_b[h % 2], 16 * (l * 8 + 4 * i + 2 * t + h // 2 + 1))
                            elif t is not None and h == 0:
                                ve.wait_ge(ld_b[2], 16 * (l * 4 + 2 * i + t + 1))
                            if kind == "swa":
                                ve.tensor_copy(sp[:, u % 2, KEYS:KEYS + 1], vc[:, V_SINK + h:V_SINK + h + 1])
                            else:
                                ve.memset(sp[:, u % 2, KEYS:KEYS + 1], LOWEST)
                            if t is None:
                                own.step(ve.tensor_copy(sp[:, u % 2, lo:KEYS], S[:, lo:KEYS]))
                                ve.tensor_reduce(mx, sp[:, u % 2, lo:hi], AX.X, ALU.max, negate=True).then_inc(s_pre, 1)
                            else:
                                b = bt[:, h % 2 if kind == "na" else 2, :]
                                own.step(ve.tensor_tensor_reduce(
                                    out=sp[:, u % 2, 0:KEYS], in0=S[:, 0:KEYS], in1=b, scale=1.0,
                                    scalar=vc[:, V_SINK + h:V_SINK + h + 1] if kind == "swa" else LOWEST,
                                    op0=ALU.add, op1=ALU.max, accum_out=mx))
                                ve.tensor_scalar(mx, mx, -1.0, None, ALU.mult).then_inc(s_pre, 1)
                        else:
                            own.step(ve.tensor_reduce(mx, S[:, lo:KEYS], AX.X, ALU.max))
                            ve.tensor_scalar(mx, mx, -(1.0 if kind == "na" else SC_DIFF), None, ALU.mult)\
                                .then_inc(s_pre, 1)
                    if 0 <= u - 1 < len(seq):
                        t, (kind, h, c) = seq[u - 1]
                        q, q8 = (u - 1) % 4, (u - 1) % 8
                        lo = NLAT if t is None else 0
                        if kind != "df":
                            ve.wait_ge(s_exp, u0 + u)
                            own.mark(ve.reciprocal(rv[:, q8:q8 + 1], rs[:, q:q + 1]))
                        elif c == 1:
                            ve.wait_ge(s_exp, u0 + u)
                            own.step(ve.reciprocal(rv[:, q8 - 1:q8 + 1], rs[:, q - 1:q + 1]))
                            own.step(ve.scalar_tensor_tensor(out=c1[:, 0:1], in0=rs[:, q - 1:q], scalar=neglam,
                                                             in1=rv[:, q8:q8 + 1], op0=ALU.mult, op1=ALU.mult))
                            ve.scalar_tensor_tensor(out=prob[:, q, lo:KEYS], in0=prob[:, q, lo:KEYS], scalar=c1[:, 0:1],
                                                    in1=prob[:, q - 1, lo:KEYS], op0=ALU.mult, op1=ALU.add)\
                                .then_inc(s_comb, 1)
                    for v, f in turn.get(u - 1, ()):
                        t, (kind, h, c) = seq[v]
                        q = v % 8 - (1 if kind == "df" else 0)
                        col = {"na": 0, "swa": 256, "df": 512}[kind] + h * 64
                        o = (h // 2 if kind == "swa" else h) % 2 * HD
                        ve.wait_ge(pv_done, 1 + f0 + f + 1)
                        own.wait()
                        where = 0 if t is None else tile + t
                        ve.tensor_scalar(otm[:, where, col:col + 64], lp[1][:, f % 2, o:o + HD], rv[:, q:q + 1], None, ALU.mult)\
                            .then_inc(o_out, 1)

            ve.memset(epst, EPS)
            own.step(ve.memset(sqacc[:], 0.0))
            for k in range(KD):
                sum_square(k + 1, k % 2)
            PER_V = LOCAL["PER_V"]
            with ve.Fori(0, L) as l:
                own.enter(l, PER_V)
                ve.wait_ge(ld_v, 16 * (l + 1))
                ah = l * PER_HI
                merged0 = l * PER_VF + 1 + KD
                for i in range(2):
                    lv = vc[:, V_LAM + 64 * i:V_LAM + 64 * i + 64]
                    m = ve.tensor_tensor_reduce(out=tmp[:, i, 0:32], in0=lv[:, 0:32], in1=lv[:, 32:64], scale=1.0, scalar=0.0,
                                                op0=ALU.mult, op1=ALU.add, accum_out=lam2[:, i:i + 1])
                m.then_inc(v_f, 1)
                ve.wait_ge(a_f, l + 1)
                own.step(ve.tensor_tensor(neglam, lam2[:, 1:2], lam2[:, 0:1], ALU.subtract))
                own.step(ve.tensor_tensor(neglam, neglam, vc[:, V_LI:V_LI + 1], ALU.subtract))
                rstd_of(2 * l + 1)
                ve.wait_ge(nrs, l + 1)
                for k in range(KD):
                    normalised(k, rstd[:])
                ve.wait_ge(ada_turned, l + 1)
                for c in range(2):
                    m = ve.tensor_tensor(mod[:, 0:ADA_A, c], ss[1][:, 0, c:2 * ADA_A:2], vc[:, V_ADAB:V_ADAB + ADA_A], ALU.add)
                own.step(m)
                gains(0, 8, V_N1, 2 * l + 1)
                for k in range(KD + 2):
                    if k < KD and k % 2:
                        odd(l, 0, k)
                    if k == KD:
                        own.mark(ve.memset(sqacc[:], 0.0))
                    if k == KD + 1:
                        own.wait()
                    if k >= 2:
                        h_lo_part(l, 0, k - 2)
                with ve.Fori(0, IN_B // 2) as j:
                    for s in range(2):
                        ve.wait_ge(turned, 1 + l * IN_B + 2 * j + s + 1)
                        ve.tensor_copy(tm[:, :, bass.ds((2 * j + s) * P, P)],
                                       sflat[s][:, 0:T].rearrange("p (t c) -> p t c", t=TILES)).then_inc(tmw, 1)
                ve.wait_ge(ld_r, 32)
                for n, c in enumerate((SWA_Q, SWA_Q + 1, SWA_K, DIFF_Q, DIFF_Q + 1, DIFF_K, DIFF_K + 1)):
                    r = 0 if n < 3 else 2
                    ve.wait_ge(rot, l * 7 + n + 1)
                    ve.wait_ge(tmw, 1 + (l + 1) * IN_B)
                    ve.tensor_tensor(tmp[:, 0, 0:NLAT], ss[n % 2][:, n % 2, :], rp[:, r + 1, :], ALU.mult)
                    own.step(ve.tensor_tensor(tmp[:, 1, 0:NLAT], qk[:, c, NCTX:T], rp[:, r, :], ALU.mult))
                    ve.tensor_tensor(qk[:, c, NCTX:T], tmp[:, 0, 0:NLAT], tmp[:, 1, 0:NLAT], ALU.add).then_inc(roped, 1)
                    ve.wait_ge(roped, l * 7 + n + 1)
                soft(l, [(None, u) for u in UNITS_T], l * 5 * NU, l * 5 * NF, 0, 0, None)
                with ve.Fori(0, 2) as i:
                    own.enter(i, LOCAL["PER_ATT"])
                    soft(l, [(s, u) for s in range(2) for u in UNITS_T], l * 5 * NU + NU + i * 2 * NU,
                         l * 5 * NF + NF + i * 2 * NF, 1 + 2 * i, 0, i)
                    own.leave(2, LOCAL["PER_ATT"])
                def branch_lo(n):
                    ve.wait_ge(a_hi, ah + HI0[S_BR] + n + 1)
                    c = n if n < 4 else n + 2
                    ve.tensor_tensor(BR[:, 1, c, :], sflat[n % 2][:, 0:T], BR[:, 0, c, :].bitcast(F32), ALU.subtract)\
                        .then_inc(split, 1)

                ve.wait_ge(o_out, 1 + (l + 1) * 5 * NF)
                for t in range(TILES):
                    d = otm[:, t, 512:768]
                    m = ve.tensor_tensor(tmp[:, t // 2, (t % 2) * 256:(t % 2) * 256 + 256], d, d, ALU.mult)
                own.step(m)
                for t in range(TILES):
                    m = ve.tensor_reduce(ssq[:, 4 * t:4 * t + 4],
                                         tmp[:, t // 2, (t % 2) * 256:(t % 2) * 256 + 256].rearrange("p (h d) -> p h d", h=4),
                                         AX.X, ALU.add)
                m.then_inc(sub_a, 1)
                for n in range(4):
                    branch_lo(n)
                ve.wait_ge(sub_s, l + 1)
                own.step(ve.reciprocal(ssq, srt))
                own.step(ve.tensor_scalar(srt, ssq, vc[:, V_LI + 1:V_LI + 2], None, ALU.mult))
                for t in range(TILES):
                    for h in range(4):
                        d = otm[:, t, 512 + h * 64:576 + h * 64]
                        m = ve.scalar_tensor_tensor(out=d, in0=d, scalar=srt[:, 4 * t + h:4 * t + h + 1],
                                                    in1=vc[:, V_SUBG:V_SUBG + 64], op0=ALU.mult, op1=ALU.mult)
                m.then_inc(sub_d, 1)
                for n in range(4, 6):
                    odd(l, 1, 4 * n - 15)
                    odd(l, 1, 4 * n - 13)
                    branch_lo(n)
                for c in range(2):
                    ve.wait_ge(a_hi, ah + HI0[S_BR] + 7 + c)
                    ve.tensor_tensor(BR[:, 1, 4 + c, :], yf[:, c, :], BR[:, 0, 4 + c, :].bitcast(F32), ALU.subtract)\
                        .then_inc(split, 1)
                ve.wait_ge(split, l * PER_SPL + SP0[S_H1B])
                for k in range(KD):
                    h_lo_part(l, 1, k)
                with ve.Fori(0, KD) as m_:
                    own.enter(m_, 2)
                    for b in range(NBR):
                        ve.wait_ge(lin[1], 1 + l * PER_DR + D0[GATE] + 4 * m_ + b + 1)
                        ve.wait_ge(drained[0], 1 + l * PER_DR + D0[GATE] + 4 * m_ + b + 1)
                        g = halves(tmp[:, 2 + b % 2, :])
                        if b == 0:
                            ve.wait_ge(v_f, merged0 + m_)
                            m = ve.tensor_tensor(halves(tmp[:, 0, :]), lp[1][:, :, 0:TH], g, ALU.mult)
                            m.then_inc(drained[1], 1)
                        else:
                            ve.tensor_tensor(halves(tmp[:, 1, :]), lp[1][:, :, 0:TH], g, ALU.mult).then_inc(drained[1], 1)
                            ve.wait_ge(drained[1], 1 + l * PER_DR + D0[GATE] + 4 * m_ + b + 1)
                            if b < NBR - 1:
                                own.step(ve.tensor_tensor(tmp[:, 0, :], tmp[:, 0, :], tmp[:, 1, :], ALU.add))
                            else:
                                ve.tensor_tensor(mg[:, m_, :], tmp[:, 0, :], tmp[:, 1, :], ALU.add).then_inc(v_f, 1)
                    own.leave(KD, 2)
                ve.wait_ge(v_f, merged0 + KD)
                ve.wait_ge(small_used[1], 1 + (l + 1) * PER_SM)
                for c in range(2):
                    m = ve.tensor_tensor(mod[:, ADA_A:48, c], ss[1][:, 0, c:2 * ADA_B:2], vc[:, V_ADAB + ADA_A:V_ADAB + 48], ALU.add)
                own.step(m)
                gains(1, 32, V_N2, 2 * l + 2)
                for k in range(KD):
                    ve.wait_ge(a_hi, ah + HI0[S_MG] + k + 1)
                    ve.tensor_tensor(H[:, 1, k, :], mg[:, k, :], H[:, 0, k, :].bitcast(F32), ALU.subtract).then_inc(split, 1)
                with ve.Fori(0, KD // 2) as j:
                    for s in range(2):
                        residual(l, W_O, j, s, 16)
                        sum_square(l * 2 * KD + KD + 2 * j + s + 1, s)
                rstd_of(2 * l + 2)
                for k in range(KD + 2):
                    if k < KD:
                        normalised(k, sflat[0][:, 0:T])
                        if k % 2:
                            odd(l, 2, k)
                    if k == KD:
                        own.mark(ve.memset(sqacc[:], 0.0))
                    if k == KD + 1:
                        own.wait()
                    if k >= 2:
                        h_lo_part(l, 2, k - 2)
                for ff, out, n, f0, sg in ((FF_A, OUT_A, FA, 0, S_GA), (FF_B, OUT_B, FB, FA, S_GB)):
                    with ve.Fori(0, n // 2) as j:
                        for s in range(2):
                            ve.wait_ge(lin[1], 1 + l * PER_DR + D0[ff] + 2 * j + s + 1)
                            ve.wait_ge(drained[0], 1 + l * PER_DR + D0[ff] + 2 * j + s + 1)
                            ve.tensor_tensor(halves(tmp[:, s, :]), lp[1][:, :, 0:TH], halves(tmp[:, 2 + s, :]), ALU.mult)\
                                .then_inc(drained[1], 1)
                            ve.wait_ge(drained[1], 1 + l * PER_DR + D0[ff] + 2 * j + s + 1)
                            ve.wait_ge(a_hi, ah + HI0[sg] + 2 * j + s + 1)
                            ve.tensor_tensor(G[:, 1, 2 * j + s, :], tmp[:, s, :], G[:, 0, 2 * j + s, :].bitcast(F32),
                                             ALU.subtract).then_inc(split, 1)
                    with ve.Fori(0, KD // 2) as j:
                        for s in range(2):
                            residual(l, out, j, s, 40)
                            if out == OUT_B:
                                sum_square(l * 2 * KD + 2 * KD + 2 * j + s + 1, s)
                own.leave(L, PER_V)
            rstd_of(2 * L + 1)
            for k in range(KD):
                own.step(ve.tensor_tensor(x[:, k, :], x[:, k, :], sflat[0][:, 0:T], ALU.mult))
                ve.tensor_scalar(x[:, k, :], x[:, k, :], fg[:, k:k + 1], None, ALU.mult).then_inc(fin, 1)



def constants():
    f8 = np.float64
    con = np.zeros((P, NCC), f8)
    con[:, C_ID:C_ID + P] = np.eye(P)
    con[:, C_ONE:C_ONE + P] = 1
    rope = np.zeros((P, 4, NLAT), np.float32)
    rows, cols = np.arange(NLAT) // GRID_W, np.arange(NLAT) % GRID_W
    for n, (w, c0) in enumerate(((64, C_RS), (32, C_RD))):
        half, quarter = w // 2, w // 4
        inv = np.float32(10000.0) ** (-np.arange(quarter, dtype=np.float32) * np.float32(2.0) / np.float32(half))
        for p in range(P):
            d = p % w
            e = d % half
            ang = (rows if d < half else cols).astype(np.float32) * inv[e % quarter]
            rope[p, 2 * n], rope[p, 2 * n + 1] = np.cos(ang), np.sin(ang)
            if e < quarter:
                con[p + quarter, c0 + p] = -1
            else:
                con[p - quarter, c0 + p] = 1
    a64 = 2 * np.pi * (np.outer(np.arange(64), np.arange(64)) % 64) / 64
    for g in range(2):
        con[64 * g:64 * g + 64, C_CB + 64 * g:C_CB + 64 * g + 64] = np.cos(a64)
        con[64 * g:64 * g + 64, C_SB + 64 * g:C_SB + 64 * g + 64] = -np.sin(a64)
    a = 2 * np.pi * (np.outer(np.arange(P), np.arange(P)) % P) / P
    con[:, C_C1:C_C1 + P], con[:, C_S1:C_S1 + P] = np.cos(a), np.sin(a)
    a = 2 * np.pi * (np.outer(np.arange(NLAT), np.arange(NLAT)) % NLAT) / NLAT
    dft = np.stack([np.cos(a), np.sin(a)], 1).reshape(4, P, 2 * NLAT)
    return con.astype(np.float32), rope, dft.astype(np.float32)


def biases(rpb):
    tok = np.arange(NLAT)
    r, c = tok // GRID_W, tok % GRID_W
    cs = np.clip(c - 8, 0, GRID_W - 16)
    dr = r[None, :] - r[:, None] + 7
    dc = c[None, :] - c[:, None] + 15
    valid = (c[None, :] >= cs[:, None]) & (c[None, :] < cs[:, None] + 16)
    out = np.zeros((L, 5, NLAT, KEYS), np.float32)
    out[:, :4, :, :NLAT] = np.where(valid, rpb[:, :, dr, np.clip(dc, 0, 30)], np.float32(-1e30))
    out[:, 4, :, :NLAT] = np.where(np.abs(tok[None, :] - tok[:, None]) <= 128, 0, -1e30).astype(np.float32)
    return np.ascontiguousarray(out.reshape(L, 5, 4, P, KEYS).transpose(0, 2, 1, 3, 4))


def tiles(w):
    *lead, k, m = w.shape
    w = w.reshape(*lead, k // P, P, m // P, P)
    n = len(lead)
    w = w.transpose(*range(n), n + 2, n + 1, n, n + 3)
    return np.ascontiguousarray(w.reshape(*lead, m // P, P, k))


def kernel(**inputs):
    import concourse.bacc as _bacc
    from concourse.bass_utils import run_bass_kernel_spmd as _run

    I = {k: np.asarray(v) for k, v in inputs.items()}
    f4 = np.float32

    def col(v):
        return np.swapaxes(v.reshape(*v.shape[:-1], -1, P), -1, -2)

    x = np.concatenate([I["x_prompt"][0], I["x_sample"][0]], 0)
    A = {"xT": np.ascontiguousarray(x.T.reshape(KD, P, T).transpose(1, 0, 2))}
    A["ada"] = tiles(I["ada_w"])
    w = I["w_in"]
    swq = w[:, :, 768:1024].reshape(L, DM, 4, HD)[:, :, [0, 2, 1, 3]].reshape(L, DM, 256)
    order = [w[:, :, 0:256], swq, w[:, :, 1536:1792], w[:, :, 256:512], w[:, :, 1792:2048],
             w[:, :, 512:768], w[:, :, 1152:1280], w[:, :, 2048:2304], w[:, :, 1280:1536], w[:, :, 1024:1152]]
    A["win"] = tiles(np.concatenate(order, 2))
    gate = tiles(I["w_gate"]).reshape(L, NBR, KD, P, DM).transpose(0, 2, 1, 3, 4)
    up = tiles(I["w_branch"]).transpose(0, 2, 1, 3, 4)
    A["wgu"] = np.ascontiguousarray(np.concatenate([gate, up], 4)).reshape(L, N_GATE, P, (KD + 2) * P)
    A["wo"] = tiles(I["w_o"])
    ff = tiles(I["w_ffn_in"])
    nf = DFF // P
    A["wff"] = np.ascontiguousarray(np.stack([ff[:, :nf], ff[:, nf:]], 2)).reshape(L, 2 * nf, P, DM)
    A["wfa"] = tiles(I["w_ffn_out"][:, :FA * P])
    A["wfb"] = tiles(I["w_ffn_out"][:, FA * P:])
    rep = lambda v: np.broadcast_to(v.reshape(L, 1, -1), (L, P, v.reshape(L, -1).shape[1]))
    init = np.array([0.8 - 0.6 * math.exp(-0.3 * l) for l in range(L)])
    li = rep(np.stack([init, 1.0 - init], 1).astype(f4))
    bg = I["b_gate"].reshape(L, NBR, KD, P).transpose(0, 3, 2, 1).reshape(L, P, N_GATE)
    A["vec"] = np.ascontiguousarray(np.concatenate(
        [col(I["norm1_g"]), col(I["norm2_g"]), col(I["ada_b"]), bg, rep(I["swa_sink"]), rep(I["diff_subln_g"]),
         rep(I["diff_lambda"]), li], 2))
    A["cond"] = np.ascontiguousarray(np.stack([col(I["c_ctx"]), col(I["c"][0])], 2))
    A["fgv"] = np.ascontiguousarray(col(I["final_norm_g"]))
    A["cst"], A["rope"], A["dft"] = constants()
    A["bias"] = biases(I["na_rpb"])
    kT = lambda v: v[0, :, 0].transpose(0, 2, 3, 1).reshape(L, -1, P, PAST)
    A["ckT"] = np.ascontiguousarray(np.concatenate(
        [kT(I["cache_na_kv"]), kT(I["cache_swa_kv"]), kT(I["cache_diff_kv"])], 1).transpose(0, 2, 1, 3))
    vt = lambda v: v[0, :, 1].reshape(L, PAST, -1)
    A["cvt"] = np.ascontiguousarray(np.concatenate(
        [vt(I["cache_na_kv"]), vt(I["cache_swa_kv"]), vt(I["cache_diff_kv"])], 2))

    nc = _bacc.Bacc("TRN2", target_bir_lowering=False, num_devices=1)
    args = [nc.dram_tensor(n, a.shape, mybir.dt.from_np(a.dtype), kind="ExternalInput").ap() for n, a in A.items()]
    for n, shape in (("yT", (P, KD, T)), ("okT", (L, P, 5, NCTX)), ("ovt", (L, NCTX, 640))):
        args.append(nc.dram_tensor(n, shape, F32, kind="ExternalOutput").ap())
    build(nc, *args)
    out = _run(nc, [A], core_ids=[0]).results[0]
    y = out["yT"].transpose(1, 0, 2).reshape(DM, T).T
    ok, ov = out["okT"].transpose(0, 2, 1, 3), out["ovt"]
    back = lambda k, h: k.reshape(L, h, HD, NCTX).transpose(0, 3, 1, 2)
    pair = lambda k, v, h: np.ascontiguousarray(np.stack([back(k, h), v.reshape(L, NCTX, h, HD)], 1)[None])
    return (np.ascontiguousarray(y[:NCTX])[None], np.ascontiguousarray(y[NCTX:])[None],
            pair(ok[:, 0:2], ov[:, :, 0:256], 4), pair(ok[:, 4:5], ov[:, :, 256:384], 2),
            pair(ok[:, 2:4], ov[:, :, 384:640], 4))
```

```python
from contextlib import ExitStack
import math

import numpy as np

import concourse.bass as bass
from concourse import mybir

F32 = mybir.dt.float32
F32R = mybir.dt.float32r
ALU = mybir.AluOpType
ACT = mybir.ActivationFunctionType
AX = mybir.AxisListType

P = 128
DM = 1024
KD = DM // P
NCTX, NLAT = 128, 512
T = NCTX + NLAT
TH = T // 2
TILES = T // P
L = 2
DFF = 2816
HD = 64
GRID_W = 64
PAST = 128
KEYS = NLAT + PAST
EPS = 1e-6
SC_HEAD = HD ** -0.5
LOWEST = -3.0e38
SC_DIFF = 32 ** -0.5

NA_Q, SWA_Q, DIFF_Q, NA_K, DIFF_K, SWA_K = 0, 2, 4, 6, 8, 11
IN_A, IN_B = 10, 8
QK = IN_A + 2
V_NA, V_SWA, V_DIFF, FU = 0, 256, 384, 640
NBR = 4
FA, FB = 12, 10
N_GATE = KD * NBR
SLOTS = (IN_A + IN_B, N_GATE, KD, 2 * FA, KD, 2 * FB, KD)
SLOT0 = [sum(SLOTS[:i]) for i in range(8)]
CHUNKS = (IN_A + IN_B, 2 * N_GATE, KD, 2 * FA, KD, 2 * FB, KD)
D0 = [sum(CHUNKS[:i]) // 2 for i in range(8)]
UNITS = (KD, KD + 2, KD, KD, FA, KD, FB)
PER_SLOT = SLOT0[7] // 2
PER_DR = D0[7]
W_IN, GATE, W_O, FF_A, OUT_A, FF_B, OUT_B = range(7)
ADA_A, ADA_E = 16, 8
ADA_S, DFT, ADA_B = ADA_A - ADA_E, 4, 32
PER_SM = (ADA_S + DFT + ADA_B) // 2
LOCAL = {"PER_V": 195, "PER_ATT": 64}
UNITS_T = [("na", h, 0) for h in range(4)] + [("swa", h, 0) for h in range(4)] + \
          [("df", h, c) for h in range(4) for c in range(2)]
NU, NF, NC = 16, 12, 4
V_N1, V_N2, V_ADAB, V_BG, V_SINK, V_SUBG, V_LAM, V_LI, NV = 0, 8, 16, 64, 96, 100, 101, 229, 231
C_ID, C_ONE, C_RS, C_RD, C_CB, C_SB, C_C1, C_S1, NCC = [i * P for i in range(9)]


def build(nc, xT, ada, adb, win, wgu, wo, wff, wfa, wfb, vec, cond, fgv, cst, rope, dft, bias, ckT, cvt,
          yT, okT, ovt):
    with ExitStack() as ctx:
        def sb(name, shape, dt=F32, stack=ctx):
            return stack.enter_context(nc.sbuf_tensor(name, shape, dt))

        def sem(name):
            return ctx.enter_context(nc.semaphore(name))

        x = sb("x", [P, KD, T])
        rstd = sb("rstd", [P, T])
        sqacc = sb("sqacc", [P, T])
        tmp = sb("tmp", [P, 4, T])
        wst = sb("wst", [P, 2, FA * P])
        wr = sb("wr", [P, 2, 2, FA * P], F32R)
        with ExitStack() as s1:
            small = sb("small", [P, 2, KD * P], F32, s1)
        small_lo = sb("small_lo", [P, 2, KD * P], F32R)
        con = sb("con", [P, NCC])
        with ExitStack() as s1:
            rp = sb("rp", [P, 4, NLAT], F32, s1)
        small_hi = sb("small_hi", [P, 2, KD * P], F32R)
        cds = sb("cds", [P, KD, 4], F32R)
        vc = sb("vc", [P, NV])
        cd = sb("cd", [P, KD, 2])
        fg = sb("fg", [P, KD])
        mod = sb("mod", [P, 48, 2])
        am = sb("am", [P, 2, KD, 2])
        st = sb("st", [P, 80])
        nm, rs, rv = st[:, 0:4], st[:, 4:8], st[:, 64:72]
        lam2, neglam, c1 = st[:, 12:14], st[:, 14:15], st[:, 16:18]
        epst = st[:, 18:19]
        rt = st[:, 72:72 + TILES]
        ssq, srt = st[:, 20:40], st[:, 40:60]
        qs = sb("qs", [P, 2, 6, P])
        grow = qs[:, :, :, :].rearrange("p a b c -> p (a b c)")[:, 0:KD * P]
        with ExitStack() as s1:
            H = sb("H", [P, 2, KD, T], F32R, s1)
        with ExitStack() as s1:
            prob = sb("prob", [P, 4, KEYS + 1], F32, s1)
            bt = sb("bt", [P, 3, KEYS], F32, s1)
            ck = sb("ck", [P, 5, PAST], F32, s1)
            cv = sb("cv", [P, 640], F32, s1)
            otm = sb("otm", [P, TILES, 768], F32, s1)
            yf = sb("yf", [P, 2, T], F32, s1)
        with ExitStack() as s1:
            adae = sb("adae", [P, ADA_E, KD * P], F32, s1)
            mrow = sb("mrow", [P, ADA_A * P], F32, s1)
        ft = prob[:, :, :].rearrange("p a b -> p (a b)")[:, 0:2048].rearrange("p (c s t) -> p c s t", c=2, s=2)
        ftp = prob[:, :, :].rearrange("p a b -> p (a b)")[:, 2048:2560].rearrange("p (c s t) -> p c s t", c=2, s=2)
        sb("region1", [P, 11008])
        with ExitStack() as s1:
            qk = sb("qk", [P, QK, T], F32, s1)
            sp = sb("sp", [P, 2, KEYS + 1], F32, s1)
            pts = sb("pts", [P, 2, KEYS], F32, s1)
            tm = sb("tm", [P, TILES, IN_B * P], F32, s1)
        with ExitStack() as s1:
            BR = sb("BR", [P, 2, KD, T], F32R, s1)
            sb("pad", [P, 16], F32, s1)
            mg = sb("mg", [P, KD, T], F32, s1)
        xn = mg
        with ExitStack() as s1:
            G = sb("G", [P, 2, FA, T], F32R, s1)

        lp = [ctx.enter_context(nc.psum_tensor(f"lp{i}", [P, 2, 512], F32)) for i in range(2)]
        ss = [ctx.enter_context(nc.psum_tensor(f"ss{i}", [P, 2, 512], F32)) for i in range(2)]
        pt = lp[0][:, :, :].rearrange("p a b -> p (a b)")
        sflat = [t[:, :, :].rearrange("p a b -> p (a b)") for t in ss]

        def halves(ap):
            return ap.rearrange("p (h t) -> p h t", h=2)

        ld_x, ld_c, ld_v, ld_cd, ld_r, ld_f = [sem(n) for n in ("ld_x", "ld_c", "ld_v", "ld_cd", "ld_r", "ld_f")]
        cond_hi, cond_split = sem("cond_hi"), sem("cond_split")
        s_hi = [sem(f"s_hi{i}") for i in range(2)]
        s_lo = [sem(f"s_lo{i}") for i in range(2)]
        grow_out = sem("grow_out")
        group_turned = sem("group_turned")
        ld_a = [sem(f"ld_a{i}") for i in range(ADA_E // 2)]
        ada_rows, mrow_out, ada_turned = sem("ada_rows"), sem("mrow_out"), sem("ada_turned")
        ld_w = [sem(f"ld_w{i}") for i in range(2)]
        ld_s = [sem(f"ld_s{i}") for i in range(2)]
        ld_b = [sem(f"ld_b{i}") for i in range(3)]
        ld_k = sem("ld_k")
        st_k, st_y = sem("st_k"), sem("st_y")
        w_hi = [sem(f"w_hi{i}") for i in range(2)]
        w_lo = [sem(f"w_lo{i}") for i in range(2)]
        small_used = [sem(f"small_used{i}") for i in range(2)]
        lin = [sem(f"lin{i}") for i in range(2)]
        drained = [sem(f"drained{i}") for i in range(2)]
        split = sem("split")
        a_hi = sem("a_hi")
        norm_x = sem("norm_x")
        h_hi = sem("h_hi")
        a_f = sem("a_f")
        v_f = sem("v_f")
        a_own, v_own = sem("a_own"), sem("v_own")
        sq = sem("sq")
        sqs = sem("sqs")
        nsum = sem("nsum")
        nrt = sem("nrt")
        diag = sem("diag")
        nbc = sem("nbc")
        nrs = sem("nrs")
        cond_ready = sem("cond_ready")
        mods = sem("mods")
        turned, tmw = sem("turned"), sem("tmw")
        f1, f2, f3, f4 = sem("f1"), sem("f2"), sem("f3"), sem("f4")
        rot, roped = sem("rot"), sem("roped")
        staged = sem("staged")
        s_ready, s_pre, s_exp, s_comb = sem("s_ready"), sem("s_pre"), sem("s_exp"), sem("s_comb")
        t_done, pt_out, pv_done, o_out = sem("t_done"), sem("pt_out"), sem("pv_done"), sem("o_out")
        sub_a, sub_s, sub_d = sem("sub_a"), sem("sub_s"), sem("sub_d")
        bt_done = sem("bt_done")
        fin = sem("fin")

        SPLITS = (KD, KD, KD, KD, KD, FA, FB)
        SP0 = [sum(SPLITS[:i]) for i in range(8)]
        PER_SPL = SP0[7]
        PER_VF = 1 + KD + KD
        S_H1, S_BR, S_H1B, S_MG, S_H2, S_GA, S_GB = range(7)
        HI0, PER_HI = {S_BR: 0, S_MG: KD, S_GA: 2 * KD, S_GB: 2 * KD + FA}, 2 * KD + FA + FB

        def odd_h(l, use, k):
            return l * PER_VF + 1 + use * KD // 2 + (k + 1) // 2

        ident, ones = con[:, C_ID:C_ID + P], con[:, C_ONE:C_ONE + P]

        class Own:

            def __init__(self, eng, s):
                self.eng, self.s, self.base, self.n, self.kept = eng, s, 0, 0, []

            def mark(self, ins):
                self.n += 1
                ins.then_inc(self.s, 1)

            def wait(self):
                self.eng.wait_ge(self.s, self.base + self.n)

            def step(self, ins):
                self.mark(ins)
                self.wait()

            def enter(self, i, per):
                self.kept.append((self.base, self.n))
                self.base, self.n = self.base + self.n + i * per, 0

            def leave(self, times, per):
                assert self.n == per, (self.n, per)
                self.base, n = self.kept.pop()
                self.n = n + times * per

        def plan(seq):
            turn, combs, f = {}, [], 0
            for u, (_, (kind, _, c)) in enumerate(seq):
                if kind != "df" or c == 1:
                    turn.setdefault(u + 3, []).append((u, f))
                    f += 1
                combs.append(sum(1 for _, (k, _, c2) in seq[:u + 1] if k == "df" and c2 == 1))
            return turn, combs

        block = ctx.enter_context(nc.Block())

        @block.sync
        def _(sy):
            for started in (*w_lo, *small_used, *lin, *drained, tmw, o_out, pt_out, turned, pv_done, grow_out):
                sy.sem_inc(started, 1)
            sy.dma_start(cd[:], cond).then_inc(ld_cd, 16)

            def early(l, i):
                sy.dma_start(adae[:, 2 * i:2 * i + 2, :], ada[l, 2 * i:2 * i + 2].rearrange("c p k -> p c k"))\
                    .then_inc(ld_a[i], 16)

            for i in range(ADA_E // 2):
                early(0, i)
            sy.dma_start(x[:], xT).then_inc(ld_x, 16)
            sy.dma_start(con[:], cst).then_inc(ld_c, 16)
            sy.dma_start(vc[:], vec[0]).then_inc(ld_v, 16)

            def weight(l, stage, src, j, s, skip=0):
                n = l * PER_SLOT + SLOT0[stage] // 2 + j
                sy.wait_ge(w_lo[s], 1 + n)
                sy.dma_start(wst[:, s, 0:UNITS[stage] * P], src[l, 2 * j + s + skip]).then_inc(ld_w[s], 16)

            def little(l, first, src, j, s):
                sy.wait_ge(small_used[s], 1 + l * PER_SM + first // 2 + j)
                sy.dma_start(small[:, s, :], src).then_inc(ld_s[s], 16)

            with sy.Fori(0, L) as l:
                with sy.Fori(0, ADA_S // 2) as j:
                    for s in range(2):
                        little(l, 0, ada[l, 2 * j + s + ADA_E], j, s)
                for s in range(2):
                    sy.wait_ge(small_used[s], 1 + l * PER_SM)
                sy.dma_start(rp[:], rope).then_inc(ld_r, 16)
                with sy.Fori(0, (IN_A + IN_B) // 2) as j:
                    for s in range(2):
                        weight(l, W_IN, win, j, s)
                for j in range(2):
                    for s in range(2):
                        little(l, ADA_S, dft[2 * j + s], j, s)
                sy.wait_ge(lin[1], 1 + l * PER_DR + D0[GATE])
                sy.dma_start(ck[:], ckT[l]).then_inc(ld_k, 16)
                sy.dma_start(cv[:], cvt[l]).then_inc(ld_k, 16)
                for s in range(2):
                    weight(l, GATE, wgu, 0, s)
                sy.wait_ge(tmw, 1 + (l + 1) * IN_B)
                for n, c in enumerate((NA_K, NA_K + 1, DIFF_K, DIFF_K + 1, SWA_K)):
                    sy.dma_start(okT[l, :, n], qk[:, c, 0:NCTX]).then_inc(st_k, 16)
                sy.dma_start(ovt[l], tm[:, 0, 0:640]).then_inc(st_k, 16)
                with sy.Fori(0, 4) as i:
                    for h in range(4):
                        if h < 2:
                            sy.wait_ge(s_pre, l * 5 * NU + NU + i * NU - NU + h + 3)
                        else:
                            sy.wait_ge(s_pre, l * 5 * NU + NU + i * NU + h - 1)
                        sy.dma_start(bt[:, h % 2, :], bias[l, i, h]).then_inc(ld_b[h % 2], 16)
                    sy.dma_start(bt[:, 2, :], bias[l, i, 4]).then_inc(ld_b[2], 16)

                def smalls(j):
                    for s in range(2):
                        little(l, ADA_S + DFT, adb[l, 2 * j + s], j, s)

                smalls(0)
                with sy.Fori(1, N_GATE // 2) as j:
                    for s in range(2):
                        weight(l, GATE, wgu, j, s)
                    smalls(j)
                for stage, src in ((W_O, wo), (FF_A, wff), (OUT_A, wfa), (FF_B, wff)):
                    with sy.Fori(0, SLOTS[stage] // 2) as j:
                        for s in range(2):
                            weight(l, stage, src, j, s, 2 * FA if stage == FF_B else 0)
                for j in range(KD // 2):
                    for s in range(2):
                        weight(l, OUT_B, wfb, j, s)
                    if j == 0:
                        for s in range(2):
                            sy.wait_ge(lin[s], 1 + l * PER_DR + D0[OUT_B])
                    early((l + 1) % L, j)
                sy.wait_ge(drained[1], 1 + (l + 1) * PER_DR)
                sy.wait_ge(drained[0], 1 + (l + 1) * PER_DR)
                sy.dma_start(vc[:], vec[(l + 1) % L]).then_inc(ld_v, 16)
            sy.dma_start(fg[:], fgv).then_inc(ld_f, 16)
            for k in range(KD):
                sy.wait_ge(fin, k + 1)
                sy.dma_start(yT[:, k, :], x[:, k, :]).then_inc(st_y, 16)
            sy.wait_ge(st_y, 16 * KD)
            sy.wait_ge(st_k, 16 * 6 * L)
            sy.wait_ge(ld_v, 16 * (L + 1))
            sy.wait_ge(ld_r, 16 * L)
            for i in range(ADA_E // 2):
                sy.wait_ge(ld_a[i], 16 * (L + 1))

        @block.gpsimd
        def _(pool):
            pool.wait_ge(ld_c, 16)

            def split_weights(l, stage, j, s):
                n = l * PER_SLOT + SLOT0[stage] // 2 + j
                w = UNITS[stage] * P
                pool.wait_ge(ld_w[s], 16 * (n + 1))
                if stage == GATE and not isinstance(j, int):
                    pool.wait_ge(lin[1], 1 + l * PER_DR + D0[GATE] + 2 * j + s - 1)
                else:
                    pool.wait_ge(lin[s], 1 + l * PER_DR + D0[stage] + j)
                pool.tensor_tensor(wr[:, s, 0, 0:w], wst[:, s, 0:w], con[:, C_ONE:C_ONE + 1].to_broadcast([P, w]), ALU.mult).then_inc(w_hi[s], 1)
                pool.wait_ge(w_hi[s], n + 1)
                pool.tensor_tensor(wr[:, s, 1, 0:w], wst[:, s, 0:w], wr[:, s, 0, 0:w].bitcast(F32),
                                   ALU.subtract).then_inc(w_lo[s], 1)

            with pool.Fori(0, L) as l:
                with pool.Fori(0, SLOTS[W_IN] // 2) as j:
                    for s in range(2):
                        split_weights(l, W_IN, j, s)
                for s in range(2):
                    split_weights(l, GATE, 0, s)
                with pool.Fori(0, 2) as i:
                    pool.wait_ge(roped, (l + 1) * 7)
                    for s in range(2):
                        pool.wait_ge(s_ready, l * 5 * NU + (2 * i + s) * NU + (1 - s))
                        pool.tensor_copy(qs[:, s, :, :], qk[:, 0:6, bass.ds(NCTX + (2 * i + s) * P, P)])\
                            .then_inc(staged, 1)
                pool.wait_ge(pv_done, 1 + (l + 1) * 5 * NF)
                pool.wait_ge(st_k, 16 * 6 * (l + 1))
                pool.wait_ge(nrs, l + 1)
                for k in range(KD):
                    pool.tensor_tensor(xn[:, k, :], x[:, k, :], rstd[:], ALU.mult).then_inc(norm_x, 1)
                with pool.Fori(1, SLOTS[GATE] // 2) as j:
                    for s in range(2):
                        split_weights(l, GATE, j, s)
                for stage in (W_O, FF_A, OUT_A, FF_B, OUT_B):
                    with pool.Fori(0, SLOTS[stage] // 2) as j:
                        for s in range(2):
                            split_weights(l, stage, j, s)

        @block.tensor
        def _(pe):
            def product(out, w, act, k, first, last):
                for i, (wi, ai) in enumerate(((0, 0), (0, 1), (1, 0))):
                    for h in range(2):
                        mm = pe.matmul(out[:, h, 0:TH], w[wi], act[:, ai, k, h * TH:(h + 1) * TH],
                                       start=first and i == 0, stop=last and i == 2)
                return mm

            def chunk(l, stage, j, s, act, kk, unit0=0, c=None, pair=None, ready=None, halfway=None):
                pair = s if pair is None else pair
                pe.wait_ge(drained[pair], 1 + l * PER_DR + D0[stage] + (j if c is None else c))
                for n, k in enumerate(kk):
                    if halfway and n == len(kk) // 2:
                        halfway()
                    if ready is not None:
                        pe.wait_ge(split, l * PER_SPL + SP0[ready] + n + 1)
                    w = [wr[:, s, i, (unit0 + n) * P:(unit0 + n + 1) * P] for i in range(2)]
                    mm = product(lp[pair], w, act, k, n == 0, n == len(kk) - 1)
                mm.then_inc(lin[pair], 1)

            def weights(l, stage, j, s):
                pe.wait_ge(w_lo[s], 1 + l * PER_SLOT + SLOT0[stage] // 2 + j + 1)

            def ada_rows_of(l, g, k, j, s):
                pe.wait_ge(s_lo[s], l * ADA_B // 2 + j + 1)
                if k == 0:
                    pe.wait_ge(grow_out, 1 + l * (ADA_B // KD) + g)
                for h in range(2):
                    for i, part in enumerate((small_hi, small_lo)):
                        mm = pe.matmul(ss[0][0:4, h, :], cds[:, k, :], part[:, s, h * 512:(h + 1) * 512],
                                       start=(k == 0 and i == 0), stop=(k == KD - 1 and i == 1))
                mm.then_inc(small_used[s], 1)

            def norm_sum(n):
                pe.wait_ge(ld_c, 16)
                pe.wait_ge(sqs, n)
                for t in range(TILES):
                    mm = pe.matmul(ss[0][:, 0, t:t + 1], sqacc[:, t * P:(t + 1) * P], ones[:, 0:1], start=True, stop=True)
                mm.then_inc(nsum, 1)

            def norm_spread(n):
                for t in range(TILES):
                    pe.wait_ge(diag, n * TILES + t + 1)
                    mm = pe.matmul(sflat[0][:, t * P:(t + 1) * P], ones, rstd[:, t * P:(t + 1) * P], start=True, stop=True)
                mm.then_inc(nbc, 1)

            def attend(seq, u0, f0, comb0):
                turn, combs = plan(seq)
                for u in range(len(seq) + 5):
                    if u < len(seq):
                        t, (kind, h, c) = seq[u]
                        if u >= 2:
                            pt_, (k_, _, _) = seq[u - 2]
                            if (k_ == "na" and pt_ is not None) or k_ == "swa":
                                pe.wait_ge(s_pre, u0 + u - 1)
                            else:
                                pe.wait_ge(s_exp, u0 + u - 1)
                        if kind == "na":
                            qc, kc, p0, n = NA_Q + h // 2, NA_K + h // 2, (h % 2) * 64, 64
                            cc = h // 2
                        elif kind == "swa":
                            qc, kc, p0, n = SWA_Q + h % 2, SWA_K, (h // 2) * 64, 64
                            cc = 2
                        else:
                            qc, kc, p0, n = DIFF_Q + h // 2, DIFF_K + h // 2, (h % 2) * 64 + c * 32, 32
                            cc = 3 + h // 2
                        out = sflat[u % 2]
                        if t is None:
                            mm = pe.matmul(out[:, NLAT:KEYS], qk[p0:p0 + n, qc, 0:NCTX], qk[p0:p0 + n, kc, 0:NCTX],
                                           start=True, stop=True)
                        else:
                            q = qs[p0:p0 + n, t, qc, :]
                            pe.matmul(out[:, 0:NLAT], q, qk[p0:p0 + n, kc, NCTX:T], start=True, stop=True)
                            mm = pe.matmul(out[:, NLAT:KEYS], q, ck[p0:p0 + n, cc, :], start=True, stop=True)
                        mm.then_inc(s_ready, 1)
                    for v, f in turn.get(u - 1, ()):
                        t, (kind, h, c) = seq[v]
                        pe.wait_ge(pt_out, 1 + f0 + f + 1)
                        pe.wait_ge(o_out, 1 + f0 + f - 1) if f >= 2 else pe.wait_ge(o_out, 1 + f0)
                        v0 = {"na": V_NA + h * 64, "swa": V_SWA + (h // 2) * 64, "df": V_DIFF + h * 64}[kind]
                        v0 -= v0 % P
                        js = (4,) if t is None else range(5)
                        for j in js:
                            val = tm[:, 0, v0:v0 + P] if t is None else \
                                cv[:, v0:v0 + P] if j == 4 else tm[:, 1 + j, v0:v0 + P]
                            mm = pe.matmul(lp[1][:, f % 2, 0:P], pts[:, f % 2, j * P:(j + 1) * P], val,
                                           start=(j == js[0]), stop=(j == 4))
                        mm.then_inc(pv_done, 1)
                    for v, f in turn.get(u, ()):
                        t, (kind, h, c) = seq[v]
                        if kind == "df":
                            pe.wait_ge(s_comb, comb0 + combs[v])
                        else:
                            pe.wait_ge(s_exp, u0 + v + 1)
                        pe.wait_ge(pt_out, 1 + f0 + f)
                        src = prob[:, v % 4, :]
                        for j in (4,) if t is None else range(5):
                            mm = pe.transpose(pt[:, j * P:(j + 1) * P], src[:, j * P:(j + 1) * P], ident)
                        mm.then_inc(t_done, 1)

            pe.wait_ge(cond_ready, 1)
            pe.wait_ge(cond_split, 1)
            with pe.Fori(0, L) as l:
                for s in range(2):
                    pe.wait_ge(drained[s], 1 + l * PER_DR)
                for m in range(ADA_A):
                    if m < ADA_E:
                        if m % 2 == 0:
                            pe.wait_ge(ld_a[m // 2], 16 * (l + 1))
                        w = adae[:, m, :]
                    else:
                        pe.wait_ge(ld_s[m % 2], 16 * (l * PER_SM + (m - ADA_E) // 2 + 1))
                        w = small[:, m % 2, :]
                    for k in range(KD):
                        mm = pe.matmul(lp[m // 8][0:2, m // 4 % 2, m % 4 * P:(m % 4 + 1) * P], cd[:, k, :],
                                       w[:, k * P:(k + 1) * P], start=(k == 0), stop=(k == KD - 1))
                    if m == ADA_E - 1:
                        mm.then_inc(ada_rows, 1)
                    elif m >= ADA_E:
                        mm.then_inc(small_used[m % 2], 1)
                    if m == ADA_E + 2:
                        norm_sum(l * 2 * KD + KD)
                    if m == ADA_E + 5:
                        norm_spread(2 * l)
                pe.wait_ge(mrow_out, 2 * (l + 1))
                for m in range(ADA_A):
                    mm = pe.matmul(ss[1][:, 0, 2 * m:2 * m + 2], mrow[0:2, m * P:(m + 1) * P], con[0:2, C_ID:C_ID + 2],
                                   start=True, stop=True)
                mm.then_inc(ada_turned, 1)
                with pe.Fori(0, IN_A // 2) as j:
                    for s in range(2):
                        weights(l, W_IN, j, s)
                        chunk(l, W_IN, j, s, H, range(KD), ready=None if s else S_H1)

                with pe.Fori(0, IN_B // 2) as j:
                    for s in range(2):
                        weights(l, W_IN, j + IN_A // 2, s)
                        chunk(l, W_IN, j + IN_A // 2, s, H, range(KD))
                    for s in range(2):
                        pe.wait_ge(drained[s], 1 + l * PER_DR + IN_A // 2 + j + 1)
                        pe.wait_ge(tmw, 1 + l * IN_B + 2 * j)
                        for t in range(TILES):
                            mm = pe.transpose(sflat[s][:, t * P:(t + 1) * P], qk[:, IN_A + s, t * P:(t + 1) * P], ident)
                        mm.then_inc(turned, 1)
                pe.wait_ge(tmw, 1 + (l + 1) * IN_B)
                turns = (SWA_Q, SWA_Q + 1, SWA_K, DIFF_Q, DIFF_Q + 1, DIFF_K, DIFF_K + 1)
                for kc in range(4):
                    for n in range(2 * kc, min(2 * kc + 2, len(turns))):
                        r = C_RS if n < 3 else C_RD
                        if n >= 2:
                            pe.wait_ge(roped, l * 7 + n - 1)
                        pe.matmul(ss[n % 2][:, n % 2, :], con[:, r:r + P], qk[:, turns[n], NCTX:T], start=True, stop=True)\
                            .then_inc(rot, 1)
                    s = kc % 2
                    pe.wait_ge(ld_s[s], 16 * (l * PER_SM + ADA_S // 2 + kc // 2 + 1))
                    for c in range(2):
                        for i in range(2):
                            mm = pe.matmul(lp[c][:, i, :], tm[:, 1 + kc, FU + c * P:FU + (c + 1) * P],
                                           small[:, s, i * NLAT:(i + 1) * NLAT], start=(kc == 0), stop=(kc == 3))
                    mm.then_inc(small_used[s], 1)
                for c in range(2):
                    for i in range(2):
                        mm = pe.matmul(ss[1][:, 0, (2 * c + i) * P:(2 * c + i + 1) * P], tm[:, 0, FU + c * P:FU + (c + 1) * P],
                                       con[:, C_C1 + i * P:C_C1 + (i + 1) * P], start=True, stop=True)
                mm.then_inc(f1, 1)
                pe.wait_ge(f2, l * 3 + 3)
                for c in range(2):
                    for i in range(2):
                        mm = pe.matmul(lp[0][:, c, :], con[:, C_CB + i * P:C_CB + (i + 1) * P], ft[:, c, i, :],
                                       start=(i == 0), stop=(i == 1))
                for c in range(2):
                    for i in range(2):
                        mm = pe.matmul(lp[1][:, 0, c * P:(c + 1) * P], con[:, C_CB + i * P:C_CB + (i + 1) * P], ftp[:, c, i, :],
                                       start=(i == 0), stop=(i == 1))
                mm.then_inc(f3, 1)
                pe.wait_ge(f4, l + 1)
                pe.wait_ge(roped, (l + 1) * 7)
                attend([(None, u) for u in UNITS_T], l * 5 * NU, l * 5 * NF, l * 5 * NC)
                with pe.Fori(0, 2) as i:
                    pe.wait_ge(ld_k, 32 * (l + 1))
                    pe.wait_ge(staged, l * 4 + 2 * i + 2)
                    attend([(s, u) for s in range(2) for u in UNITS_T], l * 5 * NU + NU + i * 2 * NU,
                           l * 5 * NF + NF + i * 2 * NF, l * 5 * NC + NC + i * 2 * NC)
                for n in range(6):
                    if n == 0:
                        pe.wait_ge(o_out, 1 + (l + 1) * 5 * NF)
                    if n == 4:
                        pe.wait_ge(sub_d, l + 1)
                    if n >= 2:
                        pe.wait_ge(split, l * PER_SPL + SP0[S_BR] + n - 1)
                    for t in range(TILES):
                        mm = pe.transpose(sflat[n % 2][:, t * P:(t + 1) * P], otm[:, t, n * P:(n + 1) * P], ident)
                    mm.then_inc(bt_done, 1)
                with pe.Fori(0, KD // 2) as g:
                    for k in range(2 * NBR):
                        j, b, s = 4 * g + k // 2, k % NBR, k % 2
                        weights(l, GATE, j, s)
                        chunk(l, GATE, j, s, H, range(KD), c=8 * g + k, pair=0, ready=None if b else S_H1B,
                              halfway=lambda: ada_rows_of(l, g, k, j, s))
                        if k == KD - 1:
                            pe.wait_ge(grow_out, 1 + l * (ADA_B // KD) + g + 1)
                        chunk(l, GATE, j, s, BR, (2 * b, 2 * b + 1), unit0=KD, c=8 * g + k, pair=1)
                    for c in range(KD):
                        mm = pe.matmul(ss[1][:, 0, bass.ds(32 * g + 4 * c, 4)], grow[0:4, c * P:(c + 1) * P],
                                       con[0:4, C_ID:C_ID + 4], start=True, stop=True)
                    mm.then_inc(group_turned, 1)
                with pe.Fori(0, KD // 2) as j:
                    for s in range(2):
                        weights(l, W_O, j, s)
                        chunk(l, W_O, j, s, H, range(KD), ready=None if s else S_MG)
                norm_sum(l * 2 * KD + 2 * KD)
                norm_spread(2 * l + 1)
                for ff, out, inner in ((FF_A, OUT_A, S_GA), (FF_B, OUT_B, S_GB)):
                    with pe.Fori(0, SLOTS[ff] // 2) as j:
                        for s in range(2):
                            weights(l, ff, j, s)
                            chunk(l, ff, j, s, H, range(KD), ready=None if s else S_H2)
                    with pe.Fori(0, KD // 2) as j:
                        for s in range(2):
                            weights(l, out, j, s)
                            chunk(l, out, j, s, G, range(UNITS[out]), ready=None if s else inner)
            norm_sum(L * 2 * KD + KD)
            norm_spread(2 * L)

        @block.scalar
        def _(act):
            own = Own(act, a_own)

            def root(n):
                act.wait_ge(nsum, n)
                act.activation(rt, ss[0][:, 0, 0:TILES], ACT.Sqrt, bias=epst, scale=1.0 / DM).then_inc(nrt, 1)

            def h_hi_part(l, use, k):
                if k % 2 == 0:
                    act.wait_ge(norm_x, (l * 3 + use) * KD + k + 1)
                    act.activation(xn[:, k, 0:NCTX], xn[:, k, 0:NCTX], ACT.Identity, bias=mod[:, k, 0:1],
                                   scale=am[:, 0, k, 0:1])
                    own.step(act.activation(xn[:, k, NCTX:T], xn[:, k, NCTX:T], ACT.Identity,
                                            bias=mod[:, k, 1:2], scale=am[:, 0, k, 1:2]))
                else:
                    act.wait_ge(v_f, odd_h(l, use, k))
                act.activation(H[:, 0, k, :], xn[:, k, :], ACT.Copy).then_inc(h_hi, 1)

            def exps(l, seq, u0, f0, comb0):
                turn, combs = plan(seq)
                done = {v: f for vf in turn.values() for v, f in vf}
                for u in range(len(seq) + 5):
                    for v, f in turn.get(u, ()):
                        lo = NLAT if seq[v][0] is None else 0
                        act.wait_ge(t_done, f0 + f + 1)
                        act.wait_ge(pv_done, 1 + f0 + max(f - 1, 0))
                        act.activation(pts[:, f % 2, lo:KEYS], pt[:, lo:KEYS], ACT.Copy).then_inc(pt_out, 1)
                    if u < len(seq):
                        t, (kind, h, c) = seq[u]
                        lo = NLAT if t is None else 0
                        act.wait_ge(s_pre, u0 + u + 1)
                        if u >= 4:
                            if u - 4 in done:
                                act.wait_ge(t_done, f0 + done[u - 4] + 1)
                            else:
                                act.wait_ge(s_comb, comb0 + combs[u - 3])
                        if kind == "swa":
                            act.activation(prob[:, u % 4, lo:KEYS + 1], sp[:, u % 2, lo:KEYS + 1], ACT.Exp,
                                           bias=nm[:, u % 4:u % 4 + 1], accum_out=rs[:, u % 4:u % 4 + 1]).then_inc(s_exp, 1)
                        elif kind == "na" and t is not None:
                            act.activation(prob[:, u % 4, 0:KEYS], sp[:, u % 2, 0:KEYS], ACT.Exp,
                                           bias=nm[:, u % 4:u % 4 + 1], accum_out=rs[:, u % 4:u % 4 + 1]).then_inc(s_exp, 1)
                        else:
                            act.activation(prob[:, u % 4, lo:KEYS], sflat[u % 2][:, lo:KEYS], ACT.Exp,
                                           bias=nm[:, u % 4:u % 4 + 1], scale=1.0 if kind == "na" else SC_DIFF,
                                           accum_out=rs[:, u % 4:u % 4 + 1]).then_inc(s_exp, 1)

            act.wait_ge(ld_cd, 16)
            own.step(act.activation(tmp[:, 2, 0:2 * KD], cd[:, :, :].rearrange("p k c -> p (k c)"), ACT.Silu))
            act.activation(cd[:, :, :].rearrange("p k c -> p (k c)"), tmp[:, 2, 0:2 * KD], ACT.Copy).then_inc(cond_ready, 1)
            act.wait_ge(cond_ready, 1)
            act.activation(cds[:, :, 0:2], cd[:], ACT.Copy).then_inc(cond_hi, 1)
            act.wait_ge(ld_x, 16)
            for k in range(KD):
                if k >= 2:
                    act.wait_ge(sqs, k - 1)
                act.activation(tmp[:, 2 + k % 2, :], x[:, k, :], ACT.Square).then_inc(sq, 1)
            PER_A = KD
            with act.Fori(0, L) as l:
                own.enter(l, PER_A)
                act.wait_ge(ld_v, 16 * (l + 1))
                act.wait_ge(v_f, l * PER_VF + 1)
                act.activation(lam2, lam2, ACT.Exp).then_inc(a_f, 1)
                act.wait_ge(ada_rows, l + 1)
                act.activation(mrow[0:2, 0:ADA_A * P // 2], lp[0][0:2, :, :].rearrange("p a b -> p (a b)"), ACT.Copy)\
                    .then_inc(mrow_out, 1)
                act.wait_ge(sqs, l * 2 * KD + KD)
                root(l * 2 + 1)
                act.wait_ge(small_used[1], 1 + l * PER_SM + ADA_S // 2)
                act.activation(mrow[0:2, ADA_A * P // 2:ADA_A * P], lp[1][0:2, :, :].rearrange("p a b -> p (a b)"), ACT.Copy)\
                    .then_inc(mrow_out, 1)
                act.wait_ge(nbc, l * 2 + 1)
                act.activation(rstd[:], sflat[0][:, 0:T], ACT.Copy).then_inc(nrs, 1)
                act.wait_ge(mods, l * 2 + 1)
                for k in range(KD):
                    h_hi_part(l, 0, k)
                for j0, j1, scale in ((0, DIFF_Q // 2, SC_HEAD), (DIFF_Q // 2, IN_A // 2, 1.0)):
                    with act.Fori(j0, j1) as j:
                        for s in range(2):
                            act.wait_ge(lin[s], 1 + l * PER_DR + j + 1)
                            act.activation(halves(qk[:, 2 * j + s, :]), lp[s][:, :, 0:TH], ACT.Copy, scale=scale)\
                                .then_inc(drained[s], 1)
                with act.Fori(0, IN_B // 2) as j:
                    for s in range(2):
                        act.wait_ge(lin[s], 1 + l * PER_DR + IN_A // 2 + j + 1)
                        act.wait_ge(turned, 1 + l * IN_B + 2 * j)
                        act.activation(halves(qk[:, IN_A + s, :]), lp[s][:, :, 0:TH], ACT.Copy).then_inc(drained[s], 1)
                act.wait_ge(f1, l + 1)
                for c in range(2):
                    act.activation(ft[:, c, :, :], lp[c][:, :, :], ACT.Copy).then_inc(f2, 1)
                act.activation(ftp.rearrange("p c s t -> p (c s t)"), ss[1][:, 0, :], ACT.Copy).then_inc(f2, 1)
                act.wait_ge(f3, l + 1)
                act.activation(yf[:, :, NCTX:T], lp[0][:, :, :], ACT.Copy, scale=(NLAT * HD) ** -0.5)
                act.activation(yf[:, :, 0:NCTX], lp[1][:, 0, 0:2 * P].rearrange("p (c t) -> p c t", c=2), ACT.Copy,
                               scale=(NCTX * HD) ** -0.5).then_inc(f4, 1)
                act.wait_ge(f4, l + 1)
                exps(l, [(None, u) for u in UNITS_T], l * 5 * NU, l * 5 * NF, l * 5 * NC)
                with act.Fori(0, 2) as i:
                    exps(l, [(s, u) for s in range(2) for u in UNITS_T], l * 5 * NU + NU + i * 2 * NU,
                         l * 5 * NF + NF + i * 2 * NF, l * 5 * NC + NC + i * 2 * NC)
                act.wait_ge(st_k, 16 * 6 * (l + 1))
                for n in range(6):
                    act.wait_ge(bt_done, l * 6 + n + 1)
                    c = n if n < 4 else n + 2
                    if n == 0:
                        act.wait_ge(pv_done, 1 + (l + 1) * 5 * NF)
                    act.activation(BR[:, 0, c, :], sflat[n % 2][:, 0:T], ACT.Copy,
                                   scale=vc[:, V_SUBG:V_SUBG + 1] if n >= 4 else 1.0).then_inc(a_hi, 1)
                    if n == 1:
                        act.wait_ge(sub_a, l + 1)
                        act.activation(srt, ssq, ACT.Sqrt, bias=epst, scale=1.0 / HD).then_inc(sub_s, 1)
                    if n >= 3:
                        h_hi_part(l, 1, n - 3)
                for c in range(2):
                    act.activation(BR[:, 0, 4 + c, :], yf[:, c, :], ACT.Copy).then_inc(a_hi, 1)
                for k in range(3, KD):
                    h_hi_part(l, 1, k)
                with act.Fori(0, KD // 2) as g:
                    for k in range(2 * NBR):
                        act.wait_ge(ld_s[k % 2], 16 * (l * PER_SM + (ADA_S + DFT) // 2 + 4 * g + k // 2 + 1))
                        act.activation(small_hi[:, k % 2, :], small[:, k % 2, :], ACT.Copy).then_inc(s_hi[k % 2], 1)
                        if k == KD - 1:
                            act.wait_ge(small_used[1], 1 + l * PER_SM + (ADA_S + DFT) // 2 + 4 * g + 4)
                            act.activation(grow[0:4, :], ss[0][0:4, :, :].rearrange("p a b -> p (a b)"), ACT.Copy)\
                                .then_inc(grow_out, 1)
                        act.wait_ge(lin[0], 1 + l * PER_DR + D0[GATE] + 8 * g + k + 1)
                        act.wait_ge(drained[1], 1 + l * PER_DR + D0[GATE] + 8 * g + k - 1)
                        act.activation(halves(tmp[:, 2 + k % 2, :]), lp[0][:, :, 0:TH], ACT.Sigmoid,
                                       bias=vc[:, bass.ds(V_BG + 8 * g + k, 1)]).then_inc(drained[0], 1)
                act.wait_ge(lin[1], 1 + l * PER_DR + D0[W_O])
                for k in range(KD):
                    if k == 0:
                        act.wait_ge(v_f, l * PER_VF + 1 + 2 * KD)
                    act.activation(H[:, 0, k, :], mg[:, k, :], ACT.Copy).then_inc(a_hi, 1)
                with act.Fori(0, KD // 2) as j:
                    for s in range(2):
                        act.wait_ge(drained[s], 1 + l * PER_DR + D0[W_O] + j + 1)
                        act.wait_ge(sqs, l * 2 * KD + KD + 2 * j + s - 1)
                        act.activation(tmp[:, 2 + s, :], x[:, 2 * j + s, :], ACT.Square).then_inc(sq, 1)
                act.wait_ge(sqs, l * 2 * KD + 2 * KD)
                root(l * 2 + 2)
                act.wait_ge(mods, l * 2 + 2)
                for k in range(KD):
                    act.wait_ge(norm_x, (l * 3 + 2) * KD + k + 1)
                    act.activation(H[:, 0, k, 0:NCTX], xn[:, k, 0:NCTX], ACT.Identity, bias=mod[:, 24 + k, 0:1])
                    act.activation(H[:, 0, k, NCTX:T], xn[:, k, NCTX:T], ACT.Identity, bias=mod[:, 24 + k, 1:2])\
                        .then_inc(h_hi, 1)
                for ff, out, n, f0, sg in ((FF_A, OUT_A, FA, 0, S_GA), (FF_B, OUT_B, FB, FA, S_GB)):
                    with act.Fori(0, n // 2) as j:
                        for s in range(2):
                            act.wait_ge(lin[0], 1 + l * PER_DR + D0[ff] + 2 * j + s + 1)
                            act.activation(halves(tmp[:, 2 + s, :]), lp[0][:, :, 0:TH], ACT.Silu).then_inc(drained[0], 1)
                            act.wait_ge(drained[1], 1 + l * PER_DR + D0[ff] + 2 * j + s + 1)
                            act.activation(G[:, 0, 2 * j + s, :], tmp[:, s, :], ACT.Copy).then_inc(a_hi, 1)
                    if out == OUT_B:
                        with act.Fori(0, KD // 2) as j:
                            for s in range(2):
                                act.wait_ge(drained[s], 1 + l * PER_DR + D0[OUT_B] + j + 1)
                                act.wait_ge(sqs, l * 2 * KD + 2 * KD + 2 * j + s - 1)
                                act.activation(tmp[:, 2 + s, :], x[:, 2 * j + s, :], ACT.Square).then_inc(sq, 1)
                own.leave(L, PER_A)
            root(2 * L + 1)

        @block.vector
        def _(ve):
            own = Own(ve, v_own)

            def rstd_of(n):
                ve.wait_ge(nrt, n)
                own.step(ve.reciprocal(rt, rt))
                for t in range(TILES):
                    ve.tensor_scalar(rstd[:, t * P:(t + 1) * P], ident, rt[:, t:t + 1], None, ALU.mult).then_inc(diag, 1)
                ve.wait_ge(nbc, n)

            def sum_square(n, k2):
                ve.wait_ge(sq, n)
                ve.tensor_tensor(sqacc[:], sqacc[:], tmp[:, 2 + k2, :], ALU.add).then_inc(sqs, 1)
                ve.wait_ge(sqs, n)

            def normalised(k, over_rms):
                ve.tensor_tensor(xn[:, k, :], x[:, k, :], over_rms, ALU.mult).then_inc(norm_x, 1)

            def odd(l, use, k):
                ve.wait_ge(norm_x, (l * 3 + use) * KD + k + 1)
                for a, b, c in ((0, NCTX, 0), (NCTX, T, 1)):
                    m = ve.tensor_scalar(xn[:, k, a:b], xn[:, k, a:b], am[:, 0, k, c:c + 1],
                                         mod[:, k, c:c + 1], ALU.mult, ALU.add)
                m.then_inc(v_f, 1)

            def h_lo_part(l, use, k):
                ve.wait_ge(h_hi, (l * 3 + use) * KD + k + 1)
                ve.tensor_tensor(H[:, 1, k, :], xn[:, k, :], H[:, 0, k, :].bitcast(F32), ALU.subtract).then_inc(split, 1)

            def gains(which, scale, gain, n):
                for c in range(2):
                    m = ve.scalar_tensor_tensor(out=am[:, which, :, c], in0=mod[:, scale:scale + KD, c], scalar=1.0,
                                                in1=vc[:, gain:gain + KD], op0=ALU.add, op1=ALU.mult)
                m.then_inc(mods, 1)
                ve.wait_ge(mods, n)

            def residual(l, stage, j, s, gate):
                ve.wait_ge(lin[s], 1 + l * PER_DR + D0[stage] + j + 1)
                k = 2 * j + s
                for a, b, c in ((0, NCTX, 0), (NCTX, TH, 1), (TH, T, 1)):
                    h = a // TH
                    m = ve.scalar_tensor_tensor(out=x[:, k, a:b], in0=lp[s][:, h, a - h * TH:b - h * TH],
                                                scalar=mod[:, gate + 2 * j + s, c:c + 1], in1=x[:, k, a:b],
                                                op0=ALU.mult, op1=ALU.add)
                m.then_inc(drained[s], 1)

            def soft(l, seq, u0, f0, tile, i):
                turn, combs = plan(seq)
                for u in range(len(seq) + 5):
                    if u < len(seq):
                        t, (kind, h, c) = seq[u]
                        lo = NLAT if t is None else 0
                        ve.wait_ge(s_ready, u0 + u + 1)
                        mx = nm[:, u % 4:u % 4 + 1]
                        S = sflat[u % 2]
                        if kind == "swa" or (kind == "na" and t is not None):
                            if u >= 2:
                                ve.wait_ge(s_exp, u0 + u - 1)
                            hi = KEYS + (kind == "swa")
                            if kind == "na":
                                ve.wait_ge(ld_b[h % 2], 16 * (l * 8 + 4 * i + 2 * t + h // 2 + 1))
                            elif t is not None and h == 0:
                                ve.wait_ge(ld_b[2], 16 * (l * 4 + 2 * i + t + 1))
                            if kind == "swa":
                                ve.tensor_copy(sp[:, u % 2, KEYS:KEYS + 1], vc[:, V_SINK + h:V_SINK + h + 1])
                            else:
                                ve.memset(sp[:, u % 2, KEYS:KEYS + 1], LOWEST)
                            if t is None:
                                own.step(ve.tensor_copy(sp[:, u % 2, lo:KEYS], S[:, lo:KEYS]))
                                ve.tensor_reduce(mx, sp[:, u % 2, lo:hi], AX.X, ALU.max, negate=True).then_inc(s_pre, 1)
                            else:
                                b = bt[:, h % 2 if kind == "na" else 2, :]
                                own.step(ve.tensor_tensor_reduce(
                                    out=sp[:, u % 2, 0:KEYS], in0=S[:, 0:KEYS], in1=b, scale=1.0,
                                    scalar=vc[:, V_SINK + h:V_SINK + h + 1] if kind == "swa" else LOWEST,
                                    op0=ALU.add, op1=ALU.max, accum_out=mx))
                                ve.tensor_scalar(mx, mx, -1.0, None, ALU.mult).then_inc(s_pre, 1)
                        else:
                            own.step(ve.tensor_reduce(mx, S[:, lo:KEYS], AX.X, ALU.max))
                            ve.tensor_scalar(mx, mx, -(1.0 if kind == "na" else SC_DIFF), None, ALU.mult)\
                                .then_inc(s_pre, 1)
                    if 0 <= u - 1 < len(seq):
                        t, (kind, h, c) = seq[u - 1]
                        q, q8 = (u - 1) % 4, (u - 1) % 8
                        lo = NLAT if t is None else 0
                        if kind != "df":
                            ve.wait_ge(s_exp, u0 + u)
                            own.mark(ve.reciprocal(rv[:, q8:q8 + 1], rs[:, q:q + 1]))
                        elif c == 1:
                            ve.wait_ge(s_exp, u0 + u)
                            own.step(ve.reciprocal(rv[:, q8 - 1:q8 + 1], rs[:, q - 1:q + 1]))
                            own.step(ve.scalar_tensor_tensor(out=c1[:, 0:1], in0=rs[:, q - 1:q], scalar=neglam,
                                                             in1=rv[:, q8:q8 + 1], op0=ALU.mult, op1=ALU.mult))
                            ve.scalar_tensor_tensor(out=prob[:, q, lo:KEYS], in0=prob[:, q, lo:KEYS], scalar=c1[:, 0:1],
                                                    in1=prob[:, q - 1, lo:KEYS], op0=ALU.mult, op1=ALU.add)\
                                .then_inc(s_comb, 1)
                    for v, f in turn.get(u - 1, ()):
                        t, (kind, h, c) = seq[v]
                        q = v % 8 - (1 if kind == "df" else 0)
                        col = {"na": 0, "swa": 256, "df": 512}[kind] + h * 64
                        o = (h // 2 if kind == "swa" else h) % 2 * HD
                        ve.wait_ge(pv_done, 1 + f0 + f + 1)
                        own.wait()
                        where = 0 if t is None else tile + t
                        ve.tensor_scalar(otm[:, where, col:col + 64], lp[1][:, f % 2, o:o + HD], rv[:, q:q + 1], None, ALU.mult)\
                            .then_inc(o_out, 1)

            ve.memset(epst, EPS)
            own.step(ve.memset(sqacc[:], 0.0))
            ve.wait_ge(cond_hi, 1)
            ve.tensor_tensor(cds[:, :, 2:4], cd[:], cds[:, :, 0:2].bitcast(F32), ALU.subtract).then_inc(cond_split, 1)
            for k in range(KD):
                sum_square(k + 1, k % 2)
            PER_V = LOCAL["PER_V"]
            with ve.Fori(0, L) as l:
                own.enter(l, PER_V)
                ve.wait_ge(ld_v, 16 * (l + 1))
                ah = l * PER_HI
                merged0 = l * PER_VF + 1 + KD
                for i in range(2):
                    lv = vc[:, V_LAM + 64 * i:V_LAM + 64 * i + 64]
                    m = ve.tensor_tensor_reduce(out=tmp[:, i, 0:32], in0=lv[:, 0:32], in1=lv[:, 32:64], scale=1.0, scalar=0.0,
                                                op0=ALU.mult, op1=ALU.add, accum_out=lam2[:, i:i + 1])
                m.then_inc(v_f, 1)
                ve.wait_ge(a_f, l + 1)
                own.step(ve.tensor_tensor(neglam, lam2[:, 1:2], lam2[:, 0:1], ALU.subtract))
                own.step(ve.tensor_tensor(neglam, neglam, vc[:, V_LI:V_LI + 1], ALU.subtract))
                rstd_of(2 * l + 1)
                ve.wait_ge(nrs, l + 1)
                for k in range(KD):
                    normalised(k, rstd[:])
                ve.wait_ge(ada_turned, l + 1)
                for c in range(2):
                    m = ve.tensor_tensor(mod[:, 0:ADA_A, c], ss[1][:, 0, c:2 * ADA_A:2], vc[:, V_ADAB:V_ADAB + ADA_A], ALU.add)
                own.step(m)
                gains(0, 8, V_N1, 2 * l + 1)
                for k in range(KD + 2):
                    if k < KD and k % 2:
                        odd(l, 0, k)
                    if k == KD:
                        own.mark(ve.memset(sqacc[:], 0.0))
                    if k == KD + 1:
                        own.wait()
                    if k >= 2:
                        h_lo_part(l, 0, k - 2)
                with ve.Fori(0, IN_B // 2) as j:
                    for s in range(2):
                        ve.wait_ge(turned, 1 + l * IN_B + 2 * j + s + 1)
                        ve.tensor_copy(tm[:, :, bass.ds((2 * j + s) * P, P)],
                                       sflat[s][:, 0:T].rearrange("p (t c) -> p t c", t=TILES)).then_inc(tmw, 1)
                ve.wait_ge(ld_r, 16 * (l + 1))
                for n, c in enumerate((SWA_Q, SWA_Q + 1, SWA_K, DIFF_Q, DIFF_Q + 1, DIFF_K, DIFF_K + 1)):
                    r = 0 if n < 3 else 2
                    ve.wait_ge(rot, l * 7 + n + 1)
                    ve.wait_ge(tmw, 1 + (l + 1) * IN_B)
                    ve.tensor_tensor(tmp[:, 0, 0:NLAT], ss[n % 2][:, n % 2, :], rp[:, r + 1, :], ALU.mult)
                    own.step(ve.tensor_tensor(tmp[:, 1, 0:NLAT], qk[:, c, NCTX:T], rp[:, r, :], ALU.mult))
                    ve.tensor_tensor(qk[:, c, NCTX:T], tmp[:, 0, 0:NLAT], tmp[:, 1, 0:NLAT], ALU.add).then_inc(roped, 1)
                    ve.wait_ge(roped, l * 7 + n + 1)
                soft(l, [(None, u) for u in UNITS_T], l * 5 * NU, l * 5 * NF, 0, None)
                with ve.Fori(0, 2) as i:
                    own.enter(i, LOCAL["PER_ATT"])
                    soft(l, [(s, u) for s in range(2) for u in UNITS_T], l * 5 * NU + NU + i * 2 * NU,
                         l * 5 * NF + NF + i * 2 * NF, 1 + 2 * i, i)
                    own.leave(2, LOCAL["PER_ATT"])
                def branch_lo(n):
                    ve.wait_ge(a_hi, ah + HI0[S_BR] + n + 1)
                    c = n if n < 4 else n + 2
                    if n < 4:
                        m = ve.tensor_tensor(BR[:, 1, c, :], sflat[n % 2][:, 0:T], BR[:, 0, c, :].bitcast(F32), ALU.subtract)
                    else:
                        m = ve.scalar_tensor_tensor(out=BR[:, 1, c, :], in0=sflat[n % 2][:, 0:T],
                                                    scalar=vc[:, V_SUBG:V_SUBG + 1], in1=BR[:, 0, c, :].bitcast(F32),
                                                    op0=ALU.mult, op1=ALU.subtract)
                    m.then_inc(split, 1)

                ve.wait_ge(o_out, 1 + (l + 1) * 5 * NF)
                df = otm[:, :, 512:768].rearrange("p t (h d) -> p t h d", h=4)
                df2 = tmp[:, 0:2, :].rearrange("p a b -> p (a b)")
                own.step(ve.tensor_tensor(df2.rearrange("p (t h d) -> p t h d", t=TILES, h=4), df, df, ALU.mult))
                ve.tensor_reduce(ssq, df2.rearrange("p (n d) -> p n d", d=HD), AX.X, ALU.add).then_inc(sub_a, 1)
                for n in range(4):
                    branch_lo(n)
                ve.wait_ge(sub_s, l + 1)
                own.step(ve.reciprocal(ssq, srt))
                own.step(ve.tensor_scalar(srt, ssq, vc[:, V_LI + 1:V_LI + 2], None, ALU.mult))
                ve.tensor_tensor(df, df, srt.rearrange("p (t h o) -> p t h o", t=TILES, o=1).to_broadcast([P, TILES, 4, HD]),
                                 ALU.mult).then_inc(sub_d, 1)
                for n in range(4, 6):
                    odd(l, 1, 4 * n - 15)
                    odd(l, 1, 4 * n - 13)
                    branch_lo(n)
                for c in range(2):
                    ve.wait_ge(a_hi, ah + HI0[S_BR] + 7 + c)
                    ve.tensor_tensor(BR[:, 1, 4 + c, :], yf[:, c, :], BR[:, 0, 4 + c, :].bitcast(F32), ALU.subtract)\
                        .then_inc(split, 1)
                ve.wait_ge(split, l * PER_SPL + SP0[S_H1B])
                for k in range(KD):
                    h_lo_part(l, 1, k)
                with ve.Fori(0, KD // 2) as g:
                    own.enter(g, 4)
                    for k in range(2 * NBR):
                        b = k % NBR
                        ve.wait_ge(s_hi[k % 2], l * ADA_B // 2 + 4 * g + k // 2 + 1)
                        ve.tensor_tensor(small_lo[:, k % 2, :], small[:, k % 2, :], small_hi[:, k % 2, :].bitcast(F32),
                                         ALU.subtract).then_inc(s_lo[k % 2], 1)
                        ve.wait_ge(lin[1], 1 + l * PER_DR + D0[GATE] + 8 * g + k + 1)
                        ve.wait_ge(drained[0], 1 + l * PER_DR + D0[GATE] + 8 * g + k + 1)
                        gate = halves(tmp[:, 2 + b % 2, :])
                        if b == 0:
                            ve.wait_ge(v_f, merged0 + 2 * g + k // NBR)
                            ve.tensor_tensor(halves(tmp[:, 0, :]), lp[1][:, :, 0:TH], gate, ALU.mult).then_inc(drained[1], 1)
                        else:
                            ve.tensor_tensor(halves(tmp[:, 1, :]), lp[1][:, :, 0:TH], gate, ALU.mult).then_inc(drained[1], 1)
                            ve.wait_ge(drained[1], 1 + l * PER_DR + D0[GATE] + 8 * g + k + 1)
                            if b < NBR - 1:
                                own.step(ve.tensor_tensor(tmp[:, 0, :], tmp[:, 0, :], tmp[:, 1, :], ALU.add))
                            else:
                                ve.tensor_tensor(mg[:, 2 * g + k // NBR, :], tmp[:, 0, :], tmp[:, 1, :], ALU.add)\
                                    .then_inc(v_f, 1)
                    own.leave(KD // 2, 4)
                ve.wait_ge(v_f, merged0 + KD)
                ve.wait_ge(group_turned, (l + 1) * (ADA_B // KD))
                for c in range(2):
                    m = ve.tensor_tensor(mod[:, ADA_A:48, c], ss[1][:, 0, c:4 * ADA_B:4], vc[:, V_ADAB + ADA_A:V_ADAB + 48], ALU.add)
                own.step(m)
                for c in range(2):
                    m = ve.tensor_tensor(mod[:, ADA_A:48, c], mod[:, ADA_A:48, c], ss[1][:, 0, 2 + c:4 * ADA_B:4], ALU.add)
                own.step(m)
                gains(1, 32, V_N2, 2 * l + 2)
                for k in range(KD):
                    ve.wait_ge(a_hi, ah + HI0[S_MG] + k + 1)
                    ve.tensor_tensor(H[:, 1, k, :], mg[:, k, :], H[:, 0, k, :].bitcast(F32), ALU.subtract).then_inc(split, 1)
                with ve.Fori(0, KD // 2) as j:
                    for s in range(2):
                        residual(l, W_O, j, s, 16)
                        sum_square(l * 2 * KD + KD + 2 * j + s + 1, s)
                rstd_of(2 * l + 2)
                for k in range(KD + 2):
                    if k < KD:
                        for a, b, c in ((0, NCTX, 0), (NCTX, T, 1)):
                            m = ve.scalar_tensor_tensor(out=xn[:, k, a:b], in0=x[:, k, a:b], scalar=am[:, 1, k, c:c + 1],
                                                        in1=sflat[0][:, a:b], op0=ALU.mult, op1=ALU.mult)
                        m.then_inc(norm_x, 1)
                    if k == KD:
                        own.mark(ve.memset(sqacc[:], 0.0))
                    if k == KD + 1:
                        own.wait()
                    if k >= 2:
                        ve.wait_ge(h_hi, (l * 3 + 2) * KD + k - 1)
                        for a, b, c in ((0, NCTX, 0), (NCTX, T, 1)):
                            m = ve.scalar_tensor_tensor(out=H[:, 1, k - 2, a:b], in0=xn[:, k - 2, a:b],
                                                        scalar=mod[:, 24 + k - 2, c:c + 1],
                                                        in1=H[:, 0, k - 2, a:b].bitcast(F32), op0=ALU.add, op1=ALU.subtract)
                        m.then_inc(split, 1)
                for ff, out, n, f0, sg in ((FF_A, OUT_A, FA, 0, S_GA), (FF_B, OUT_B, FB, FA, S_GB)):
                    with ve.Fori(0, n // 2) as j:
                        for s in range(2):
                            ve.wait_ge(lin[1], 1 + l * PER_DR + D0[ff] + 2 * j + s + 1)
                            ve.wait_ge(drained[0], 1 + l * PER_DR + D0[ff] + 2 * j + s + 1)
                            ve.tensor_tensor(halves(tmp[:, s, :]), lp[1][:, :, 0:TH], halves(tmp[:, 2 + s, :]), ALU.mult)\
                                .then_inc(drained[1], 1)
                            ve.wait_ge(drained[1], 1 + l * PER_DR + D0[ff] + 2 * j + s + 1)
                            ve.wait_ge(a_hi, ah + HI0[sg] + 2 * j + s + 1)
                            ve.tensor_tensor(G[:, 1, 2 * j + s, :], tmp[:, s, :], G[:, 0, 2 * j + s, :].bitcast(F32),
                                             ALU.subtract).then_inc(split, 1)
                    with ve.Fori(0, KD // 2) as j:
                        for s in range(2):
                            residual(l, out, j, s, 40)
                            if out == OUT_B:
                                sum_square(l * 2 * KD + 2 * KD + 2 * j + s + 1, s)
                own.leave(L, PER_V)
            ve.wait_ge(ld_f, 16)
            rstd_of(2 * L + 1)
            for k in range(KD):
                ve.scalar_tensor_tensor(out=x[:, k, :], in0=x[:, k, :], scalar=fg[:, k:k + 1], in1=sflat[0][:, 0:T],
                                        op0=ALU.mult, op1=ALU.mult).then_inc(fin, 1)


def constants():
    f8 = np.float64
    con = np.zeros((P, NCC), f8)
    con[:, C_ID:C_ID + P] = np.eye(P)
    con[:, C_ONE:C_ONE + P] = 1
    rope = np.zeros((P, 4, NLAT), np.float32)
    rows, cols = np.arange(NLAT) // GRID_W, np.arange(NLAT) % GRID_W
    for n, (w, c0) in enumerate(((64, C_RS), (32, C_RD))):
        half, quarter = w // 2, w // 4
        inv = np.float32(10000.0) ** (-np.arange(quarter, dtype=np.float32) * np.float32(2.0) / np.float32(half))
        for p in range(P):
            d = p % w
            e = d % half
            ang = (rows if d < half else cols).astype(np.float32) * inv[e % quarter]
            rope[p, 2 * n], rope[p, 2 * n + 1] = np.cos(ang), np.sin(ang)
            if e < quarter:
                con[p + quarter, c0 + p] = -1
            else:
                con[p - quarter, c0 + p] = 1
    a64 = 2 * np.pi * (np.outer(np.arange(64), np.arange(64)) % 64) / 64
    for g in range(2):
        con[64 * g:64 * g + 64, C_CB + 64 * g:C_CB + 64 * g + 64] = np.cos(a64)
        con[64 * g:64 * g + 64, C_SB + 64 * g:C_SB + 64 * g + 64] = -np.sin(a64)
    a = 2 * np.pi * (np.outer(np.arange(P), np.arange(P)) % P) / P
    con[:, C_C1:C_C1 + P], con[:, C_S1:C_S1 + P] = np.cos(a), np.sin(a)
    a = 2 * np.pi * (np.outer(np.arange(NLAT), np.arange(NLAT)) % NLAT) / NLAT
    dft = np.stack([np.cos(a), np.sin(a)], 1).reshape(4, P, 2 * NLAT)
    return con.astype(np.float32), rope, dft.astype(np.float32)


def biases(rpb):
    tok = np.arange(NLAT)
    r, c = tok // GRID_W, tok % GRID_W
    cs = np.clip(c - 8, 0, GRID_W - 16)
    dr = r[None, :] - r[:, None] + 7
    dc = c[None, :] - c[:, None] + 15
    valid = (c[None, :] >= cs[:, None]) & (c[None, :] < cs[:, None] + 16)
    out = np.zeros((L, 5, NLAT, KEYS), np.float32)
    out[:, :4, :, :NLAT] = np.where(valid, rpb[:, :, dr, np.clip(dc, 0, 30)], np.float32(-1e30))
    out[:, 4, :, :NLAT] = np.where(np.abs(tok[None, :] - tok[:, None]) <= 128, 0, -1e30).astype(np.float32)
    return np.ascontiguousarray(out.reshape(L, 5, 4, P, KEYS).transpose(0, 2, 1, 3, 4))


def tiles(w):
    *lead, k, m = w.shape
    w = w.reshape(*lead, k // P, P, m // P, P)
    n = len(lead)
    w = w.transpose(*range(n), n + 2, n + 1, n, n + 3)
    return np.ascontiguousarray(w.reshape(*lead, m // P, P, k))


def kernel(**inputs):
    import concourse.bacc as _bacc
    from concourse.bass_utils import run_bass_kernel_spmd as _run

    I = {k: np.asarray(v) for k, v in inputs.items()}
    f4 = np.float32

    def col(v):
        return np.swapaxes(v.reshape(*v.shape[:-1], -1, P), -1, -2)

    x = np.concatenate([I["x_prompt"][0], I["x_sample"][0]], 0)
    A = {"xT": np.ascontiguousarray(x.T.reshape(KD, P, T).transpose(1, 0, 2))}
    A["ada"] = tiles(I["ada_w"])
    adb = I["ada_w"][:, :, ADA_A * P:].reshape(L, KD, P, ADA_B // KD, DM).transpose(0, 3, 1, 2, 4)
    A["adb"] = np.ascontiguousarray(adb).reshape(L, ADA_B, P, DM)
    w = I["w_in"]
    swq = w[:, :, 768:1024].reshape(L, DM, 4, HD)[:, :, [0, 2, 1, 3]].reshape(L, DM, 256)
    order = [w[:, :, 0:256], swq, w[:, :, 1536:1792], w[:, :, 256:512], w[:, :, 1792:2048],
             w[:, :, 512:768], w[:, :, 1152:1280], w[:, :, 2048:2304], w[:, :, 1280:1536], w[:, :, 1024:1152]]
    A["win"] = tiles(np.concatenate(order, 2))
    gate = tiles(I["w_gate"]).reshape(L, NBR, KD, P, DM).transpose(0, 2, 1, 3, 4)
    up = tiles(I["w_branch"]).transpose(0, 2, 1, 3, 4)
    A["wgu"] = np.ascontiguousarray(np.concatenate([gate, up], 4)).reshape(L, N_GATE, P, (KD + 2) * P)
    A["wo"] = tiles(I["w_o"])
    ff = tiles(I["w_ffn_in"])
    nf = DFF // P
    A["wff"] = np.ascontiguousarray(np.stack([ff[:, :nf], ff[:, nf:]], 2)).reshape(L, 2 * nf, P, DM)
    A["wfa"] = tiles(I["w_ffn_out"][:, :FA * P])
    A["wfb"] = tiles(I["w_ffn_out"][:, FA * P:])
    rep = lambda v: np.broadcast_to(v.reshape(L, 1, -1), (L, P, v.reshape(L, -1).shape[1]))
    init = np.array([0.8 - 0.6 * math.exp(-0.3 * l) for l in range(L)])
    li = rep(np.stack([init, 1.0 - init], 1).astype(f4))
    bg = I["b_gate"].reshape(L, NBR, KD, P).transpose(0, 3, 2, 1).reshape(L, P, N_GATE)
    A["vec"] = np.ascontiguousarray(np.concatenate(
        [col(I["norm1_g"]), col(I["norm2_g"]), col(I["ada_b"]), bg, rep(I["swa_sink"]), col(np.tile(I["diff_subln_g"], 2)),
         rep(I["diff_lambda"]), li], 2))
    A["cond"] = np.ascontiguousarray(np.stack([col(I["c_ctx"]), col(I["c"][0])], 2))
    A["fgv"] = np.ascontiguousarray(col(I["final_norm_g"]))
    A["cst"], A["rope"], A["dft"] = constants()
    A["bias"] = biases(I["na_rpb"])
    kT = lambda v: v[0, :, 0].transpose(0, 2, 3, 1).reshape(L, -1, P, PAST)
    A["ckT"] = np.ascontiguousarray(np.concatenate(
        [kT(I["cache_na_kv"]), kT(I["cache_swa_kv"]), kT(I["cache_diff_kv"])], 1).transpose(0, 2, 1, 3))
    vt = lambda v: v[0, :, 1].reshape(L, PAST, -1)
    A["cvt"] = np.ascontiguousarray(np.concatenate(
        [vt(I["cache_na_kv"]), vt(I["cache_swa_kv"]), vt(I["cache_diff_kv"])], 2))

    nc = _bacc.Bacc("TRN2", target_bir_lowering=False, num_devices=1)
    args = [nc.dram_tensor(n, a.shape, mybir.dt.from_np(a.dtype), kind="ExternalInput").ap() for n, a in A.items()]
    for n, shape in (("yT", (P, KD, T)), ("okT", (L, P, 5, NCTX)), ("ovt", (L, NCTX, 640))):
        args.append(nc.dram_tensor(n, shape, F32, kind="ExternalOutput").ap())
    build(nc, *args)
    out = _run(nc, [A], core_ids=[0]).results[0]
    y = out["yT"].transpose(1, 0, 2).reshape(DM, T).T
    ok, ov = out["okT"].transpose(0, 2, 1, 3), out["ovt"]
    back = lambda k, h: k.reshape(L, h, HD, NCTX).transpose(0, 3, 1, 2)
    pair = lambda k, v, h: np.ascontiguousarray(np.stack([back(k, h), v.reshape(L, NCTX, h, HD)], 1)[None])
    return (np.ascontiguousarray(y[:NCTX])[None], np.ascontiguousarray(y[NCTX:])[None],
            pair(ok[:, 0:2], ov[:, :, 0:256], 4), pair(ok[:, 4:5], ov[:, :, 256:384], 2),
            pair(ok[:, 2:4], ov[:, :, 384:640], 4))
```
